# Optimizing a Trainium2 kernel written in Bass

```python
import math
import jax, jax.numpy as jnp
from jax import lax
import numpy as np

D_MODEL = 1024
BATCH = 1
SEQ = 1024
DEPTH = 1
DEC_BATCH = 8
DEC_SEQ = 8
PAST_LEN = 4096
PAGE_SIZE = 128

NSA_HEADS = 8
NSA_KV_HEADS = 2
NSA_HD = 64
CMP_BLOCK = 32
CMP_STRIDE = 16
SEL_BLOCK = 64
SEL_TOPN = 8
WINDOW = 512
Q_BLOCK = 128
FORCED_BONUS = 1e4
GDN_HEADS = 4
GDN_HD = 128
GDN_CONV = 4
GDN_CHUNK = 64
MEM_TOKENS = 256
XA_HEADS = 4
XA_HD = D_MODEL // XA_HEADS
D_FF = 2816
FFN_CONV = 3

ROPE_THETA = 10000.0
EPS = 1e-6
NEG = -1e30

NSA_Q_W = NSA_HEADS * NSA_HD
NSA_KV_W = 3 * 2 * NSA_KV_HEADS * NSA_HD
NSA_GATE_W = 3 * NSA_HEADS
GDN_W = GDN_HEADS * GDN_HD
MIX_W = NSA_Q_W + GDN_W
XA_W = XA_HEADS * XA_HD
IN_SPLITS = (NSA_Q_W, NSA_KV_W, NSA_GATE_W, 3 * GDN_W, GDN_W, GDN_HEADS, GDN_HEADS)
IN_COLS = NSA_Q_W + NSA_KV_W + NSA_GATE_W + 4 * GDN_W + 2 * GDN_HEADS

kernel_name = 'hymba_nsa_gdn_convffn_step'

def _rms(x, w):
    xf = x.astype(jnp.float32)
    y = xf * lax.rsqrt(jnp.mean(xf * xf, axis=-1, keepdims=True) + EPS)
    return (y * w.astype(jnp.float32)).astype(x.dtype)

def _l2n(x):
    xf = x.astype(jnp.float32)
    return xf * lax.rsqrt(jnp.sum(xf * xf, axis=-1, keepdims=True) + EPS)

def _rope(x, pos):
    half = x.shape[-1] // 2
    inv = jnp.power(ROPE_THETA, -jnp.arange(half, dtype=jnp.float32) / half)
    ang = pos.astype(jnp.float32)[:, None] * inv[None, :]
    cos = jnp.cos(ang)[None, :, None, :]
    sin = jnp.sin(ang)[None, :, None, :]
    xf = x.astype(jnp.float32)
    x1, x2 = xf[..., :half], xf[..., half:]
    return jnp.concatenate([x1 * cos - x2 * sin, x1 * sin + x2 * cos], axis=-1).astype(x.dtype)

def _causal_dwconv(x, buf, w):
    K = w.shape[0]
    T = x.shape[1]
    xp = jnp.concatenate([buf.astype(x.dtype), x], axis=1)
    y = xp[:, 0:T] * w[0]
    for i in range(1, K):
        y = y + xp[:, i:i + T] * w[i]
    return y, xp[:, xp.shape[1] - (K - 1):]

def _masked_probs(s, valid):
    s = jnp.where(valid, s, NEG)
    p = jnp.where(valid, jnp.exp(s - jnp.max(s, axis=-1, keepdims=True)), 0.0)
    return p / jnp.maximum(jnp.sum(p, axis=-1, keepdims=True), 1e-30)

def _compress(x, pe, w):
    B, L = x.shape[:2]
    n_chunk = L // CMP_STRIDE
    r = CMP_BLOCK // CMP_STRIDE
    n_cmp = n_chunk - r + 1
    ch = x.reshape(B, n_chunk, CMP_STRIDE, NSA_KV_HEADS, NSA_HD)
    blocks = jnp.concatenate([ch[:, i:i + n_cmp] for i in range(r)], axis=2)
    blocks = blocks + pe[None, None, :, None, :]
    return jnp.einsum('bcjkd,jde->bcke', blocks, w)

def _cmp_to_sel(n_cmp, n_sel):
    cs = jnp.arange(n_cmp)[:, None] * CMP_STRIDE
    ss = jnp.arange(n_sel)[None, :] * SEL_BLOCK
    return ((cs < ss + SEL_BLOCK) & (cs + CMP_BLOCK > ss)).astype(jnp.float32)

def _sel_blocks(x):
    B, L = x.shape[:2]
    return x.reshape(B, L // SEL_BLOCK, SEL_BLOCK, NSA_KV_HEADS, NSA_HD).transpose(0, 3, 1, 2, 4)

def _nsa_core(qc, qr, gates, q_pos, k_cmp, v_cmp, c2s, ks_b, vs_b, kw, vw, kw_pos):
    f32 = jnp.float32
    B, Tq = qc.shape[:2]
    K = NSA_KV_HEADS
    G = NSA_HEADS // K
    scale = NSA_HD ** -0.5
    qcg = qc.reshape(B, Tq, K, G, NSA_HD).astype(f32)
    qrg = qr.reshape(B, Tq, K, G, NSA_HD).astype(f32)
    n_cmp = k_cmp.shape[1]
    cmp_end = jnp.arange(n_cmp) * CMP_STRIDE + (CMP_BLOCK - 1)
    s = jnp.einsum('btkgd,bckd->bkgtc', qcg, k_cmp.astype(f32)) * scale
    p_cmp = _masked_probs(s, cmp_end[None, :] <= q_pos[:, None])
    o_cmp = jnp.einsum('bkgtc,bckd->btkgd', p_cmp, v_cmp.astype(f32))
    n_sel = ks_b.shape[2]
    imp = jnp.einsum('bkgtc,cs->bkts', p_cmp, c2s)
    blk = jnp.arange(n_sel)[None, :]
    q_blk = (q_pos // SEL_BLOCK)[:, None]
    visible = blk <= q_blk
    forced = (blk == 0) | (blk == q_blk) | (blk == q_blk - 1)
    score = jnp.where(visible, imp + jnp.where(forced, FORCED_BONUS, 0.0), NEG)
    n_top = min(SEL_TOPN, n_sel)
    top_val, top_idx = lax.top_k(score, n_top)
    bi = jnp.arange(B)[:, None, None, None]
    ki = jnp.arange(K)[None, :, None, None]
    k_sel = ks_b[bi, ki, top_idx].astype(f32)
    v_sel = vs_b[bi, ki, top_idx].astype(f32)
    key_pos = top_idx[..., None] * SEL_BLOCK + jnp.arange(SEL_BLOCK)
    sel_valid = (top_val > 0.5 * NEG)[..., None] & (key_pos <= q_pos[None, None, :, None, None])
    m = n_top * SEL_BLOCK
    s = jnp.einsum('btkgd,bktnjd->bkgtnj', qrg, k_sel).reshape(B, K, G, Tq, m) * scale
    p_sel = _masked_probs(s, sel_valid.reshape(B, K, 1, Tq, m))
    o_sel = jnp.einsum('bkgtm,bktmd->btkgd', p_sel, v_sel.reshape(B, K, Tq, m, NSA_HD))
    s = jnp.einsum('btkgd,blkd->bkgtl', qrg, kw.astype(f32)) * scale
    rel = q_pos[:, None] - kw_pos[None, :]
    p_win = _masked_probs(s, (rel >= 0) & (rel < WINDOW) & (kw_pos[None, :] >= 0))
    o_win = jnp.einsum('bkgtl,blkd->btkgd', p_win, vw.astype(f32))
    g = gates.reshape(B, Tq, K, G, 3).astype(f32)
    o = o_cmp * g[..., 0:1] + o_sel * g[..., 1:2] + o_win * g[..., 2:3]
    return o.reshape(B, Tq, NSA_Q_W).astype(qc.dtype)

def _nsa_prompt(qc, qr, gates, rows, wrows, cmp_pe, cmp_w):
    B, T = qc.shape[:2]
    k_cmp = _compress(rows[:, :, 0], cmp_pe[0], cmp_w[0])
    v_cmp = _compress(rows[:, :, 1], cmp_pe[1], cmp_w[1])
    ks_b = _sel_blocks(rows[:, :, 2])
    vs_b = _sel_blocks(rows[:, :, 3])
    c2s = _cmp_to_sel(k_cmp.shape[1], ks_b.shape[2])
    wpad = jnp.pad(wrows, ((0, 0), (WINDOW, 0), (0, 0), (0, 0), (0, 0)))
    n_blk = T // Q_BLOCK

    def one_block(args):
        b, qc_b, qr_b, g_b = args
        start = b * Q_BLOCK
        q_pos = start + jnp.arange(Q_BLOCK)
        band = lax.dynamic_slice_in_dim(wpad, start, WINDOW + Q_BLOCK, axis=1)
        kw_pos = start - WINDOW + jnp.arange(WINDOW + Q_BLOCK)
        return _nsa_core(qc_b, qr_b, g_b, q_pos, k_cmp, v_cmp, c2s, ks_b, vs_b,
                         band[:, :, 0], band[:, :, 1], kw_pos)

    def split(a):
        return a.reshape(B, n_blk, Q_BLOCK, *a.shape[2:]).swapaxes(0, 1)

    out = lax.map(one_block, (jnp.arange(n_blk), split(qc), split(qr), split(gates)))
    return out.swapaxes(0, 1).reshape(B, T, NSA_Q_W)

def _nsa_sample(qc, qr, gates, rows, wrows, past_rows, win_buf, cmp_pe, cmp_w):
    B, T = qc.shape[:2]
    past = past_rows.shape[1]
    full = jnp.concatenate([past_rows.astype(rows.dtype), rows], axis=1)
    L = full.shape[1]
    Lp = -(-L // SEL_BLOCK) * SEL_BLOCK
    full = jnp.pad(full, ((0, 0), (0, Lp - L), (0, 0), (0, 0), (0, 0)))
    k_cmp = _compress(full[:, :, 0], cmp_pe[0], cmp_w[0])
    v_cmp = _compress(full[:, :, 1], cmp_pe[1], cmp_w[1])
    ks_b = _sel_blocks(full[:, :, 2])
    vs_b = _sel_blocks(full[:, :, 3])
    c2s = _cmp_to_sel(k_cmp.shape[1], ks_b.shape[2])
    wb = win_buf.shape[1]
    wall = jnp.concatenate([win_buf.astype(wrows.dtype), wrows], axis=1)
    kw_pos = past - wb + jnp.arange(wb + T)
    q_pos = past + jnp.arange(T)
    o = _nsa_core(qc, qr, gates, q_pos, k_cmp, v_cmp, c2s, ks_b, vs_b,
                  wall[:, :, 0], wall[:, :, 1], kw_pos)
    keep = min(WINDOW, wb + T)
    return o, wall[:, wb + T - keep:]

def _gated_delta(q, k, v, beta, g, s0):
    f32 = jnp.float32
    B, T, H, dk = q.shape
    dv = v.shape[-1]
    C = GDN_CHUNK
    n = -(-T // C)
    pad = n * C - T

    def chunk(a):
        a = jnp.pad(a.astype(f32), [(0, 0), (0, pad)] + [(0, 0)] * (a.ndim - 2))
        return a.reshape(B, n, C, *a.shape[2:]).swapaxes(2, 3)

    qc, kc, vc, bc = chunk(q), chunk(k), chunk(v), chunk(beta)
    gc = jnp.cumsum(chunk(g), axis=-1)
    causal = jnp.tril(jnp.ones((C, C), bool))
    strict = jnp.tril(jnp.ones((C, C), bool), -1)
    diff = gc[..., :, None] - gc[..., None, :]
    decay = jnp.where(causal, jnp.exp(jnp.where(causal, diff, 0.0)), 0.0)
    kb = kc * bc[..., None]
    a_mat = jnp.where(strict, jnp.einsum('bnhid,bnhjd->bnhij', kb, kc) * decay, 0.0)
    rhs = jnp.concatenate([vc * bc[..., None], kb * jnp.exp(gc)[..., None]], axis=-1)
    sol = lax.linalg.triangular_solve(jnp.eye(C, dtype=f32) + a_mat, rhs, left_side=True,
                                      lower=True, unit_diagonal=True)
    u, w = sol[..., :dv], sol[..., dv:]
    qk = jnp.einsum('bnhid,bnhjd->bnhij', qc, kc) * decay
    q_dec = qc * jnp.exp(gc)[..., None]
    g_last = gc[..., -1]
    k_dec = kc * jnp.exp(g_last[..., None] - gc)[..., None]

    def step(S, xs):
        u_c, w_c, qd_c, qk_c, kd_c, gl_c = xs
        v_new = u_c - jnp.einsum('bhck,bhkv->bhcv', w_c, S)
        o_c = jnp.einsum('bhck,bhkv->bhcv', qd_c, S) + jnp.einsum('bhij,bhjv->bhiv', qk_c, v_new)
        S = S * jnp.exp(gl_c)[..., None, None] + jnp.einsum('bhck,bhcv->bhkv', kd_c, v_new)
        return S, o_c

    xs = tuple(a.swapaxes(0, 1) for a in (u, w, q_dec, qk, k_dec, g_last))
    S, o = lax.scan(step, s0.astype(f32), xs)
    o = o.transpose(1, 0, 3, 2, 4).reshape(B, n * C, H, dv)[:, :T]
    return o, S

def _gdn(qkv_pre, z_pre, b_pre, a_pre, conv_buf, s0, conv_w, a_log, dt_bias, norm_w):
    f32 = jnp.float32
    B, T = qkv_pre.shape[:2]
    qkv, buf_new = _causal_dwconv(qkv_pre, conv_buf, conv_w)
    qkv = jax.nn.silu(qkv)
    q, k, v = jnp.split(qkv, 3, axis=-1)
    shp = (B, T, GDN_HEADS, GDN_HD)
    q = _l2n(q.reshape(shp)) * (GDN_HD ** -0.5)
    k = _l2n(k.reshape(shp))
    v = v.reshape(shp).astype(f32)
    beta = jax.nn.sigmoid(b_pre.astype(f32))
    g = -jnp.exp(a_log.astype(f32)) * jax.nn.softplus(a_pre.astype(f32) + dt_bias.astype(f32))
    o, s_new = _gated_delta(q, k, v, beta, g, s0)
    o = _rms(o, norm_w) * jax.nn.silu(z_pre.reshape(shp).astype(f32))
    return o.reshape(B, T, GDN_W).astype(qkv_pre.dtype), buf_new, s_new.astype(s0.dtype)

def _mem_kv(mem, mem_norm_w, w_xk, w_xv, xk_norm_w):
    B, M = mem.shape[:2]
    mn = _rms(mem, mem_norm_w)
    k = _rms((mn @ w_xk).reshape(B, M, XA_HEADS, XA_HD), xk_norm_w)
    v = (mn @ w_xv).reshape(B, M, XA_HEADS, XA_HD)
    return jnp.stack([k, v], axis=2)

def _cross_attn(x, mem_kv, norm_w, w_xq, xq_norm_w, w_xo):
    f32 = jnp.float32
    B, T = x.shape[:2]
    q = _rms((_rms(x, norm_w) @ w_xq).reshape(B, T, XA_HEADS, XA_HD), xq_norm_w)
    s = jnp.einsum('bthd,bmhd->bhtm', q.astype(f32), mem_kv[:, :, 0].astype(f32)) * (XA_HD ** -0.5)
    p = jax.nn.softmax(s, axis=-1)
    o = jnp.einsum('bhtm,bmhd->bthd', p, mem_kv[:, :, 1].astype(f32))
    return o.reshape(B, T, XA_W).astype(x.dtype) @ w_xo

def _conv_ffn(x, buf, norm_w, w_up, conv_w, conv_b, w_down):
    up = _rms(x, norm_w) @ w_up
    h, buf_new = _causal_dwconv(up, buf, conv_w)
    a, u = jnp.split(h + conv_b, 2, axis=-1)
    return (jax.nn.silu(a) * u) @ w_down, buf_new

def _layer(x, pos, nsa_attend, gdn_buf, gdn_s0, mem_kv, ffn_buf,
           attn_norm_w, w_in, nsa_q_norm_w, nsa_k_norm_w, gdn_conv_w, gdn_a_log,
           gdn_dt_bias, gdn_norm_w, w_out, xattn_norm_w, w_xq, xq_norm_w, w_xo,
           ffn_norm_w, w_up, ffn_conv_w, ffn_conv_b, w_down):
    B, T = x.shape[:2]
    xn = _rms(x, attn_norm_w)
    cuts, acc = [], 0
    for width in IN_SPLITS[:-1]:
        acc += width
        cuts.append(acc)
    q_pre, kv_pre, gate_pre, qkv_pre, z_pre, b_pre, a_pre = jnp.split(xn @ w_in, cuts, axis=-1)
    q = _rms(q_pre.reshape(B, T, NSA_HEADS, NSA_HD), nsa_q_norm_w)
    qr = _rope(q, pos)
    kv = kv_pre.reshape(B, T, 3, 2, NSA_KV_HEADS, NSA_HD)
    k = _rms(kv[:, :, :, 0], nsa_k_norm_w[:, None, :])
    v = kv[:, :, :, 1]
    rows = jnp.stack([k[:, :, 0], v[:, :, 0], _rope(k[:, :, 1], pos), v[:, :, 1]], axis=2)
    wrows = jnp.stack([_rope(k[:, :, 2], pos), v[:, :, 2]], axis=2)
    gates = jax.nn.sigmoid(gate_pre.reshape(B, T, NSA_HEADS, 3))
    o_nsa, win_state = nsa_attend(q, qr, gates, rows, wrows)
    o_gdn, gdn_buf_new, gdn_s = _gdn(qkv_pre, z_pre, b_pre, a_pre, gdn_buf, gdn_s0,
                                     gdn_conv_w, gdn_a_log, gdn_dt_bias, gdn_norm_w)
    h = x + jnp.concatenate([o_nsa, o_gdn.astype(o_nsa.dtype)], axis=-1) @ w_out
    h = h + _cross_attn(h, mem_kv, xattn_norm_w, w_xq, xq_norm_w, w_xo)
    f, ffn_buf_new = _conv_ffn(h, ffn_buf, ffn_norm_w, w_up, ffn_conv_w, ffn_conv_b, w_down)
    return h + f, rows, win_state, gdn_s, gdn_buf_new, ffn_buf_new

def setup_inputs(seed: int = 0) -> dict:
    key = jax.random.key(seed)
    ks = iter(jax.random.split(key, 48))

    def nrm(shape, scale):
        return jax.random.normal(next(ks), shape, jnp.float32) * scale

    def gain(shape):
        return 1.0 + 0.02 * jax.random.normal(next(ks), shape, jnp.float32)

    n_pages = PAST_LEN // PAGE_SIZE
    n_used = DEC_BATCH * n_pages
    n_pool = n_used + n_used // 4
    win_len = min(WINDOW, PAST_LEN)
    page_table = jax.random.permutation(next(ks), n_pool)[:n_used].reshape(DEC_BATCH, n_pages).astype(jnp.int32)
    a_log = jnp.log(jax.random.uniform(next(ks), (DEPTH, GDN_HEADS), jnp.float32, 1.0, 16.0))
    dt = jnp.exp(jax.random.uniform(next(ks), (DEPTH, GDN_HEADS), jnp.float32,
                                    math.log(1e-3), math.log(1e-1)))
    dt_bias = dt + jnp.log(-jnp.expm1(-dt))
    return {
        'x_prompt': nrm((BATCH, SEQ, D_MODEL), 1.0),
        'x_sample': nrm((DEC_BATCH, DEC_SEQ, D_MODEL), 1.0),
        'mem_prompt': nrm((BATCH, MEM_TOKENS, D_MODEL), 1.0),
        'cache_nsa_kv': nrm((DEPTH, n_pool, PAGE_SIZE, 4, NSA_KV_HEADS, NSA_HD), 1.0),
        'cache_nsa_win': nrm((DEPTH, DEC_BATCH, win_len, 2, NSA_KV_HEADS, NSA_HD), 1.0),
        'state_gdn': nrm((DEPTH, DEC_BATCH, GDN_HEADS, GDN_HD, GDN_HD), 1.0),
        'cache_gdn_conv': nrm((DEPTH, DEC_BATCH, GDN_CONV - 1, 3 * GDN_W), 1.0),
        'cache_ffn_conv': nrm((DEPTH, DEC_BATCH, FFN_CONV - 1, 2 * D_FF), 1.0),
        'cache_mem_kv': nrm((DEPTH, DEC_BATCH, MEM_TOKENS, 2, XA_HEADS, XA_HD), 1.0),
        'page_table': page_table,
        'attn_norm_w': gain((DEPTH, D_MODEL)),
        'w_in': nrm((DEPTH, D_MODEL, IN_COLS), D_MODEL ** -0.5),
        'nsa_q_norm_w': gain((DEPTH, NSA_HD)),
        'nsa_k_norm_w': gain((DEPTH, 3, NSA_HD)),
        'cmp_pe': nrm((DEPTH, 2, CMP_BLOCK, NSA_HD), 0.1),
        'cmp_w': nrm((DEPTH, 2, CMP_BLOCK, NSA_HD, NSA_HD), (CMP_BLOCK * NSA_HD) ** -0.5),
        'gdn_conv_w': nrm((DEPTH, GDN_CONV, 3 * GDN_W), GDN_CONV ** -0.5),
        'gdn_a_log': a_log,
        'gdn_dt_bias': dt_bias,
        'gdn_norm_w': gain((DEPTH, GDN_HD)),
        'w_out': nrm((DEPTH, MIX_W, D_MODEL), MIX_W ** -0.5),
        'mem_norm_w': gain((DEPTH, D_MODEL)),
        'w_xk': nrm((DEPTH, D_MODEL, XA_W), D_MODEL ** -0.5),
        'w_xv': nrm((DEPTH, D_MODEL, XA_W), D_MODEL ** -0.5),
        'xk_norm_w': gain((DEPTH, XA_HD)),
        'xattn_norm_w': gain((DEPTH, D_MODEL)),
        'w_xq': nrm((DEPTH, D_MODEL, XA_W), D_MODEL ** -0.5),
        'xq_norm_w': gain((DEPTH, XA_HD)),
        'w_xo': nrm((DEPTH, XA_W, D_MODEL), XA_W ** -0.5),
        'ffn_norm_w': gain((DEPTH, D_MODEL)),
        'w_up': nrm((DEPTH, D_MODEL, 2 * D_FF), D_MODEL ** -0.5),
        'ffn_conv_w': nrm((DEPTH, FFN_CONV, 2 * D_FF), FFN_CONV ** -0.5),
        'ffn_conv_b': nrm((DEPTH, 2 * D_FF), 0.01),
        'w_down': nrm((DEPTH, D_FF, D_MODEL), D_FF ** -0.5),
    }

def reference(x_prompt, x_sample, mem_prompt, cache_nsa_kv, cache_nsa_win, state_gdn,
              cache_gdn_conv, cache_ffn_conv, cache_mem_kv, page_table,
              attn_norm_w, w_in, nsa_q_norm_w, nsa_k_norm_w, cmp_pe, cmp_w, gdn_conv_w,
              gdn_a_log, gdn_dt_bias, gdn_norm_w, w_out, mem_norm_w, w_xk, w_xv, xk_norm_w,
              xattn_norm_w, w_xq, xq_norm_w, w_xo, ffn_norm_w, w_up, ffn_conv_w, ffn_conv_b, w_down):
    B, T = x_prompt.shape[:2]
    Bs, Ts = x_sample.shape[:2]
    past_len = page_table.shape[1] * cache_nsa_kv.shape[2]
    pos_p = jnp.arange(T)
    pos_s = past_len + jnp.arange(Ts)
    hp, hs = x_prompt, x_sample
    kv_p, win_p, st_p, gc_p, fc_p, mkv_p = [], [], [], [], [], []
    kv_s, win_s, st_s, gc_s, fc_s = [], [], [], [], []
    for l in range(DEPTH):
        def run(x, pos, attend, gbuf, gs0, mkv, fbuf):
            return _layer(x, pos, attend, gbuf, gs0, mkv, fbuf,
                          attn_norm_w[l], w_in[l], nsa_q_norm_w[l], nsa_k_norm_w[l], gdn_conv_w[l],
                          gdn_a_log[l], gdn_dt_bias[l], gdn_norm_w[l], w_out[l], xattn_norm_w[l],
                          w_xq[l], xq_norm_w[l], w_xo[l], ffn_norm_w[l], w_up[l], ffn_conv_w[l],
                          ffn_conv_b[l], w_down[l])

        def attend_prompt(q, qr, g, rows, wrows):
            n = rows.shape[1]
            keep = min(WINDOW, n)
            return _nsa_prompt(q, qr, g, rows, wrows, cmp_pe[l], cmp_w[l]), wrows[:, n - keep:]

        past_rows = cache_nsa_kv[l][page_table].reshape(Bs, past_len, 4, NSA_KV_HEADS, NSA_HD)

        def attend_sample(q, qr, g, rows, wrows):
            return _nsa_sample(q, qr, g, rows, wrows, past_rows, cache_nsa_win[l], cmp_pe[l], cmp_w[l])

        mem_kv = _mem_kv(mem_prompt, mem_norm_w[l], w_xk[l], w_xv[l], xk_norm_w[l])
        hp, a1, a2, a3, a4, a5 = run(hp, pos_p, attend_prompt,
                                     jnp.zeros((B, GDN_CONV - 1, 3 * GDN_W), hp.dtype),
                                     jnp.zeros((B, GDN_HEADS, GDN_HD, GDN_HD), hp.dtype),
                                     mem_kv,
                                     jnp.zeros((B, FFN_CONV - 1, 2 * D_FF), hp.dtype))
        kv_p.append(a1); win_p.append(a2); st_p.append(a3); gc_p.append(a4); fc_p.append(a5)
        mkv_p.append(mem_kv)
        hs, b1, b2, b3, b4, b5 = run(hs, pos_s, attend_sample, cache_gdn_conv[l], state_gdn[l],
                                     cache_mem_kv[l], cache_ffn_conv[l])
        kv_s.append(b1); win_s.append(b2); st_s.append(b3); gc_s.append(b4); fc_s.append(b5)
    nsa_kv_p = jnp.stack(kv_p)
    nsa_win_p = jnp.stack(win_p)
    gdn_state_p = jnp.stack(st_p)
    gdn_conv_p = jnp.stack(gc_p)
    ffn_conv_p = jnp.stack(fc_p)
    mem_kv_p = jnp.stack(mkv_p)
    nsa_kv_s = jnp.stack(kv_s)
    nsa_win_s = jnp.stack(win_s)
    gdn_state_s = jnp.stack(st_s)
    gdn_conv_s = jnp.stack(gc_s)
    ffn_conv_s = jnp.stack(fc_s)
    return (hp, hs, nsa_kv_p, nsa_win_p, gdn_state_p, gdn_conv_p, ffn_conv_p, mem_kv_p,
            nsa_kv_s, nsa_win_s, gdn_state_s, gdn_conv_s, ffn_conv_s)


_drawn_inputs = setup_inputs


def setup_inputs(seed=0):
    import zlib

    import numpy as np

    out = dict(_drawn_inputs(seed))
    spreads = {}
    factors = {'nsa_q_norm_w': 8.0,
     'nsa_k_norm_w': 3.872,
     'gdn_norm_w': 6.487,
     'mem_norm_w': 2.752,
     'xk_norm_w': 3.77,
     'xattn_norm_w': 8.0,
     'xq_norm_w': 8.0,
     'ffn_norm_w': 2.942,
     'ffn_conv_b': 8.0}
    for name, (base, spread) in spreads.items():
        noise = np.random.default_rng([zlib.crc32(name.encode()), seed]).standard_normal(out[name].shape)
        drawn = base * np.exp(spread * noise) if base else spread * noise
        out[name] = __import__('jax').numpy.asarray(drawn.astype(out[name].dtype))
    for name, factor in factors.items():
        out[name] = (out[name] * factor).astype(out[name].dtype)
    return out
```

```python
from contextlib import ExitStack

import concourse.bass as bass
from concourse import mybir

F32 = mybir.dt.float32
I32 = mybir.dt.int32
ALU = mybir.AluOpType
ACT = mybir.ActivationFunctionType
AX = mybir.AxisListType.X
ds = bass.ds

P = 128
D = 1024
KD = D // P
SEQ = 1024
NB, NT = 8, 8
SAMP = NB * NT
TOK = SEQ + SAMP
NTILE = 9
TOKP = NTILE * P
PAST = 4096
PAGE = 128
NPAGE = PAST // PAGE
POOL = 320
HD = 64
QW = 512
KVW = 768
NATW = QW + KVW + 24
GW = 512
ZW = GW + 8
GCH = 3 * GW // P
EPS = 1e-6
NEG = -1e30
MEM = 256
XH, XD = 4, 256
FF = 2816
FT = FF // P
WIN = 512


class Stage:

    def __init__(self, nc, name):
        self.nc, self.name, self.ctx, self.sems = nc, name, ExitStack(), []

    def sb(self, name, shape, dt=F32):
        return self.ctx.enter_context(self.nc.sbuf_tensor(f"{self.name}_{name}", shape, dt))

    def ps(self, name, shape=(P, 512), dt=F32):
        return self.ctx.enter_context(self.nc.psum_tensor(f"{self.name}_{name}", list(shape), dt))

    def sem(self, name):
        s = self.nc.alloc_semaphore(f"{self.name}_{name}")
        self.sems.append(s)
        return s

    def __enter__(self):
        return self

    def __exit__(self, *a):
        if a[0] is None:
            self.nc.clear_and_free_semaphores(self.sems)
            self.nc.all_engine_barrier()
        self.ctx.close()


def pool_rsqrt(pool, out, sums, n, half):
    pool.tensor_scalar(out, sums, 1.0 / n, EPS, ALU.mult, ALU.add)
    pool.drain()
    return pool.tensor_tensor(out, out, half, ALU.pow)


def wait_turn(sp, sem, value, turns):
    sp.wait_ge(sem, value)
    sp.sem_inc(turns, 1)


def stage_project(nc, io, scr, xnT, ident, half):
    with Stage(nc, "proj") as st:
        w_nat = st.sb("w_nat", [P, KD, NATW])
        w_zba = st.sb("w_zba", [P, KD, ZW])
        norm_w = st.sb("norm_w", [P, D])
        q_w = st.sb("q_w", [P, HD])
        k_w = st.sb("k_w", [P, 3, HD])
        a_log = st.sb("a_log", [P, 4])
        dt_b = st.sb("dt_b", [P, 4])
        x_in = st.sb("x_in", [P, D])
        rope = st.sb("rope", [P, 2, HD])
        xn = st.sb("xn", [P, D])
        sq = st.sb("sq", [P, QW + KVW])
        x_sq = st.sb("x_sq", [P, D])
        ss = st.sb("ss", [P, 1])
        rstd = st.sb("rstd", [P, 1])
        xT = st.sb("xT", [P, KD, P])
        nat = st.sb("nat", [P, NATW])
        z = st.sb("z", [P, GW])
        ba = st.sb("ba", [P, 8])
        misc = st.sb("misc", [P, 32])
        hs = st.sb("hs", [P, 20])
        rs = st.sb("rs", [P, 20])
        normed = st.sb("normed", [P, 14, HD])
        rot = st.sb("rot", [P, 14, HD])
        rt = st.sb("rt", [P, 14, HD])
        y = st.sb("y", [P, 4])
        ya = st.sb("ya", [P, 4])
        ps_t = [st.ps(f"t{k}") for k in range(2)]
        ps_p = [st.ps(f"p{k}") for k in range(5)]

        w_here = st.sem("w_here")
        x_here = st.sem("x_here")
        rope_here = st.sem("rope_here")
        squares = st.sem("squares")
        rstd_ready = st.sem("rstd_ready")
        hs_ready = st.sem("hs_ready")
        rs_ready = st.sem("rs_ready")
        turns = st.sem("turns")
        pool_turns = st.sem("pool_turns")
        xn_ready = st.sem("xn_ready")
        turned = st.sem("turned")
        xT_ready = st.sem("xT_ready")
        xT_kept = st.sem("xT_kept")
        projected = st.sem("projected")
        evacuated = st.sem("evacuated")
        alog_ready = st.sem("alog_ready")
        nega_ready = st.sem("nega_ready")
        ya_ready = st.sem("ya_ready")
        ln_ready = st.sem("ln_ready")
        rows_ready = st.sem("rows_ready")
        stored = st.sem("stored")
        NSTORE = 10
        NW = 10

        with nc.Block() as block:

            @block.sync
            def _(sp):
                w_v = io["w_in"].rearrange("(k p) n -> p k n", p=P)
                rows, wrows = io["rows"], io["wrows"]

                def load(t):
                    sp.dma_start(x_in[:, :], io["x_all"][ds(t * P, P), :]).then_inc(x_here, 16)

                def load_rope(t):
                    sp.dma_start(rope[:, :, :], io["rope"][ds(t * P, P), :, :]).then_inc(rope_here, 16)

                def store(t):
                    row = ds(t * P, P)
                    wait_turn(sp, rows_ready, t + 1, turns)
                    wait_turn(sp, evacuated, 5 * (t + 1), turns)
                    for out, src in [(scr["qc"][row, :], normed[:, 0:8, :]), (scr["qr"][row, :], rot[:, 0:8, :]),
                                     (rows[row, 0:128], normed[:, 8:10, :]), (rows[row, 256:384], rot[:, 10:12, :]),
                                     (wrows[row, 0:128], rot[:, 12:14, :])]:
                        sp.dma_start(out, src.rearrange("p a b -> p (a b)")).then_inc(stored, 16)
                    for out, src in [(rows[row, 128:256], nat[:, 640:768]), (rows[row, 384:512], nat[:, 896:1024]),
                                     (wrows[row, 128:256], nat[:, 1152:1280]), (scr["z"][row, :], z[:, :]),
                                     (scr["misc"][row, :], misc[:, :])]:
                        sp.dma_start(out, src).then_inc(stored, 16)

                load(0)
                load_rope(0)
                for dst, name in [(norm_w, "attn_norm_w"), (q_w, "nsa_q_norm_w"), (a_log, "gdn_a_log"),
                                  (dt_b, "gdn_dt_bias")]:
                    sp.dma_start(dst[:, :], io[name].partition_broadcast(P)).then_inc(w_here, 16)
                sp.dma_start(k_w[:, :, :], io["nsa_k_norm_w"].partition_broadcast(P)).then_inc(w_here, 16)
                for k in range(0, KD, 2):
                    sp.dma_start(w_nat[:, k:k + 2, :], w_v[:, k:k + 2, 0:NATW]).then_inc(w_here, 16)
                sp.dma_start(w_zba[:, :, :], w_v[:, :, NATW + 3 * GW:]).then_inc(w_here, 16)
                with sp.Fori(1, NTILE) as i:
                    wait_turn(sp, xn_ready, i, turns)
                    load(i)
                    store(i - 1)
                    load_rope(i)
                store(NTILE - 1)
                sp.wait_ge(stored, 16 * NSTORE * (NTILE + 1))

            @block.gpsimd
            def _(pool):
                def rstd_of(t):
                    wait_turn(pool, squares, t + 1, pool_turns)
                    pool_rsqrt(pool, rstd[:, :], ss[:, :], D, half[:, 0:1]).then_inc(rstd_ready, 1)

                def tile(i, last=False):
                    pool.wait_ge(xT_ready, i + 1)
                    pool.tensor_copy(xnT[:, :, ds(i * P, P)], xT[:, :, :]).then_inc(xT_kept, 1)
                    if not last:
                        rstd_of(i + 1)
                    wait_turn(pool, hs_ready, i + 1, pool_turns)
                    pool_rsqrt(pool, rs[:, :], hs[:, :], HD, half[:, 0:20]).then_inc(rs_ready, 1)

                rstd_of(0)
                with pool.Fori(0, NTILE - 1) as i:
                    tile(i)
                tile(NTILE - 1, last=True)

            @block.scalar
            def _(act):
                act.wait_ge(w_here, 16 * NW)
                act.activation(a_log[:, :], a_log[:, :], ACT.Exp).then_inc(alog_ready, 1)

                def square(t):
                    act.wait_ge(x_here, 16 * t + 16)
                    act.activation(x_sq[:, :], x_in[:, :], ACT.Square, accum_out=ss[:, :]).then_inc(squares, 1)

                def tile(i, last=False):
                    act.wait_ge(xT_kept, i + 1)
                    act.wait_ge(turned, i + 1)
                    act.activation(xT[:, 0:4, :].rearrange("p a b -> p (a b)"), ps_t[0][:, :], ACT.Copy)
                    act.activation(xT[:, 4:8, :].rearrange("p a b -> p (a b)"), ps_t[1][:, :], ACT.Copy).then_inc(xT_ready, 1)
                    if not last:
                        square(i + 1)
                    act.wait_ge(stored, 16 * NSTORE * (i + 1))
                    act.wait_ge(projected, 5 * i + 1)
                    act.activation(nat[:, 0:512], ps_p[0][:, :], ACT.Copy).then_inc(evacuated, 1)
                    act.wait_ge(projected, 5 * i + 2)
                    act.activation(nat[:, 512:1024], ps_p[1][:, :], ACT.Copy).then_inc(evacuated, 1)
                    act.wait_ge(projected, 5 * i + 3)
                    act.activation(misc[:, 0:24], ps_p[2][:, 256:280], ACT.Sigmoid)
                    act.activation(nat[:, 1024:1280], ps_p[2][:, 0:256], ACT.Copy).then_inc(evacuated, 1)
                    act.wait_ge(projected, 5 * i + 4)
                    act.activation(z[:, 0:260], ps_p[3][:, 0:260], ACT.Silu).then_inc(evacuated, 1)
                    act.wait_ge(projected, 5 * i + 5)
                    act.activation(z[:, 260:512], ps_p[4][:, 0:252], ACT.Silu)
                    act.activation(misc[:, 24:28], ps_p[4][:, 252:256], ACT.Sigmoid)
                    act.activation(ba[:, :], ps_p[4][:, 252:260], ACT.Copy).then_inc(evacuated, 1)
                    act.wait_ge(ya_ready, i + 1)
                    act.activation(ya[:, :], ya[:, :], ACT.Exp)
                    act.drain()
                    act.activation(ya[:, :], ya[:, :], ACT.Ln, bias=1.0).then_inc(ln_ready, 1)

                square(0)
                with act.Fori(0, NTILE - 1) as i:
                    tile(i)
                tile(NTILE - 1, last=True)

            @block.vector
            def _(dve):
                dve.sem_inc(xT_kept, 1)
                dve.sem_inc(stored, 16 * NSTORE)
                dve.wait_ge(alog_ready, 1)
                dve.tensor_scalar(a_log[:, :], a_log[:, :], -1.0, None, ALU.mult)
                dve.memset(misc[:, :], 0.0)
                dve.drain()

                def norm_x(t):
                    dve.wait_ge(rstd_ready, t + 1)
                    dve.scalar_tensor_tensor(xn[:, :], x_in[:, :], rstd[:, 0:1], norm_w[:, :],
                                             ALU.mult, ALU.mult).then_inc(xn_ready, 1)

                def heads(i):
                    dve.wait_ge(evacuated, 5 * (i + 1))
                    dve.wait_ge(rope_here, 16 * (i + 1))
                    dve.tensor_tensor(sq[:, :], nat[:, 0:1280], nat[:, 0:1280], ALU.mult)
                    dve.tensor_tensor(y[:, :], ba[:, 4:8], dt_b[:, :], ALU.add)
                    dve.drain()
                    dve.tensor_scalar(ya[:, :], y[:, :], -1.0, None, ALU.mult)
                    dve.drain()
                    dve.tensor_tensor(ya[:, :], ya[:, :], y[:, :], ALU.min).then_inc(ya_ready, 1)
                    dve.tensor_reduce(hs[:, :], sq[:, :].rearrange("p (a b) -> p a b", b=HD), AX, ALU.add).then_inc(hs_ready, 1)
                    dve.wait_ge(rs_ready, i + 1)
                    dve.tensor_tensor(normed[:, 0:8, :], nat[:, 0:512].rearrange("p (a b) -> p a b", b=HD),
                                      rs[:, 0:8].unsqueeze(2).to_broadcast([P, 8, HD]), ALU.mult)
                    kin = nat[:, 512:1280].rearrange("p (r c a b) -> p r c a b", r=3, c=2, b=HD)[:, :, 0]
                    kout = normed[:, 8:14, :].rearrange("p (r a) b -> p r a b", r=3)
                    krs = rs[:, 8:20].rearrange("p (r c a) -> p r c a", r=3, c=2)[:, :, 0]
                    dve.tensor_tensor(kout, kin, krs.unsqueeze(3).to_broadcast([P, 3, 2, HD]), ALU.mult)
                    dve.drain()
                    dve.tensor_tensor(normed[:, 0:8, :], normed[:, 0:8, :],
                                      q_w[:, :].unsqueeze(1).to_broadcast([P, 8, HD]), ALU.mult)
                    dve.tensor_tensor(kout, kout, k_w[:, :, :].unsqueeze(2).to_broadcast([P, 3, 2, HD]), ALU.mult)
                    dve.drain()
                    h = HD // 2
                    dve.tensor_tensor(rot[:, :, :], normed[:, :, :],
                                      rope[:, 0, :].unsqueeze(1).to_broadcast([P, 14, HD]), ALU.mult)
                    dve.tensor_tensor(rt[:, :, 0:h], normed[:, :, h:HD],
                                      rope[:, 1, 0:h].unsqueeze(1).to_broadcast([P, 14, h]), ALU.mult)
                    dve.tensor_tensor(rt[:, :, h:HD], normed[:, :, 0:h],
                                      rope[:, 1, h:HD].unsqueeze(1).to_broadcast([P, 14, h]), ALU.mult)
                    dve.drain()
                    dve.tensor_tensor(rot[:, :, :], rot[:, :, :], rt[:, :, :], ALU.add)
                    dve.wait_ge(ln_ready, i + 1)
                    dve.scalar_tensor_tensor(y[:, :], y[:, :], 0.0, ya[:, :], ALU.max, ALU.add)
                    dve.drain()
                    dve.tensor_tensor(misc[:, 28:32], y[:, :], a_log[:, :], ALU.mult).then_inc(rows_ready, 1)

                norm_x(0)
                with dve.Fori(0, NTILE - 1) as i:
                    dve.wait_ge(turned, i + 1)
                    norm_x(i + 1)
                    heads(i)
                heads(NTILE - 1)

            @block.tensor
            def _(pe):
                pe.wait_ge(w_here, 16 * NW)
                with pe.Fori(0, NTILE) as i:
                    pe.wait_ge(xn_ready, i + 1)
                    for k in range(KD):
                        t = pe.transpose(ps_t[k // 4][:, (k % 4) * P:(k % 4 + 1) * P], xn[:, k * P:(k + 1) * P], ident[:, :])
                    t.then_inc(turned, 1)
                    pe.wait_ge(xT_ready, i + 1)
                    for g, (w, a, b) in enumerate([(w_nat, 0, 512), (w_nat, 512, 1024), (w_nat, 1024, NATW),
                                                   (w_zba, 0, 260), (w_zba, 260, ZW)]):
                        for k in range(KD):
                            m = pe.matmul(ps_p[g][:, 0:b - a], xT[:, k, :], w[:, k, a:b], start=(k == 0), stop=(k == KD - 1))
                        m.then_inc(projected, 1)


def stage_channels(nc, io, scr, xnT, gT):
    with Stage(nc, "chan") as st:
        w = st.sb("w", [P, 2, KD, P])
        conv_w = st.sb("conv_w", [P, GCH, 4])
        conv_buf = st.sb("conv_buf", [P, GCH, NB, 3])
        tap = st.sb("tap", [P, 4])
        xp = st.sb("xp", [P, SEQ + 3])
        xs = st.sb("xs", [P, NB, NT + 3])
        sq = st.sb("sq", [P, TOK])
        nrm = st.sb("nrm", [P, TOK])
        kept = st.sb("kept", [P, GCH, 27])
        ones = st.sb("ones", [P, P])
        eps = st.sb("eps", [P, 1])
        acc = [st.ps(f"acc{s}", [P, 3, 512]) for s in range(2)]

        small_here = st.sem("small_here")
        w_here = [st.sem(f"w_here{s}") for s in range(2)]
        ones_ready = st.sem("ones_ready")
        projected = st.sem("projected")
        x_ready = st.sem("x_ready")
        conv_done = st.sem("conv_done")
        sq_ready = st.sem("sq_ready")
        sums_done = st.sem("sums_done")
        root_ready = st.sem("root_ready")
        channel_done = st.sem("channel_done")
        turns = st.sem("turns")
        kept_out = st.sem("kept_out")
        SPLIT = [(0, 512), (512, 1024), (1024, TOK)]

        with nc.Block() as block:

            @block.sync
            def _(sp):
                w_v = io["w_in"][:, NATW:NATW + 3 * GW].rearrange("(k p) (c n) -> c p k n", p=P, n=P)

                def load(c, s):
                    sp.dma_start(w[:, s, :, :], w_v[ds(c, 1), :, :, :].rearrange("c p k n -> p (c k) n")).then_inc(w_here[s], 16)

                load(0, 0)
                load(1, 1)
                sp.dma_start(conv_w[:, :, :], io["gconv_wT"].rearrange("(c p) k -> p c k", p=P)).then_inc(small_here, 16)
                sp.dma_start(conv_buf[:, :, :, :].rearrange("p c b k -> p c (b k)"),
                             io["gconv_bufT"].rearrange("(c p) k -> p c k", p=P)).then_inc(small_here, 16)
                with sp.Fori(0, GCH // 2 - 1) as i:
                    for s in range(2):
                        wait_turn(sp, projected, 2 * i + s + 1, turns)
                        load(2 * i + s + 2, s)
                sp.wait_ge(channel_done, GCH + 1)
                sp.dma_start(io["gconvT"].rearrange("(c p) k -> p c k", p=P), kept[:, :, :]).then_inc(kept_out, 16)
                sp.wait_ge(kept_out, 16)

            @block.tensor
            def _(pe):
                pe.wait_ge(ones_ready, 1)

                def project(c, i, s):
                    pe.wait_ge(w_here[s], 16 * (i + 1))
                    for g, (a, b) in enumerate(SPLIT):
                        for k in range(KD):
                            m = pe.matmul(acc[s][:, g, 0:b - a], w[:, s, k, :], xnT[:, k, a:b],
                                          start=(k == 0), stop=(k == KD - 1))
                    m.then_inc(projected, 1)

                def sums(c, s):
                    pe.wait_ge(sq_ready, c + 1)
                    for g, (a, b) in enumerate(SPLIT):
                        m = pe.matmul(acc[s][:, g, 0:b - a], ones[:, :], sq[:, a:b], start=True, stop=True)
                    m.then_inc(sums_done, 1)

                project(0, 0, 0)
                with pe.Fori(0, 4) as i:
                    pe.wait_ge(channel_done, 2 * i + 1)
                    project(2 * i + 1, i, 1)
                    sums(2 * i, 0)
                    pe.wait_ge(root_ready, 2 * i + 1)
                    project(2 * i + 2, i + 1, 0)
                    sums(2 * i + 1, 1)
                pe.wait_ge(root_ready, 8)
                project(9, 4, 1)
                pe.wait_ge(x_ready, 9)
                project(10, 5, 0)
                pe.wait_ge(x_ready, 10)
                project(11, 5, 1)

            @block.scalar
            def _(act):
                def channel(c, s, normed):
                    act.wait_ge(conv_done, c + 1)
                    act.wait_ge(projected, c + 1)
                    act.activation(xp[:, 3:515], acc[s][:, 0, :], ACT.Copy)
                    act.activation(xp[:, 515:1027], acc[s][:, 1, :], ACT.Copy)
                    act.activation(xs[:, :, 3:], acc[s][:, 2, 0:SAMP].rearrange("p (b t) -> p b t", t=NT),
                                   ACT.Copy).then_inc(x_ready, 1)
                    act.wait_ge(conv_done, c + 2)
                    g = gT[:, ds(c, 1), 0:TOK].rearrange("p a n -> p (a n)")
                    if not normed:
                        act.activation(g, g, ACT.Silu).then_inc(channel_done, 1)
                        return
                    act.activation(g, g, ACT.Silu)
                    act.drain()
                    act.activation(sq[:, :], g, ACT.Square).then_inc(sq_ready, 1)
                    act.wait_ge(sums_done, c + 1)
                    act.activation(nrm[:, 0:1024], acc[s][:, 0:2, :].rearrange("p a b -> p (a b)"), ACT.Sqrt, bias=eps[:, 0:1])
                    act.activation(nrm[:, 1024:TOK], acc[s][:, 2, 0:SAMP], ACT.Sqrt, bias=eps[:, 0:1]).then_inc(root_ready, 1)

                act.wait_ge(ones_ready, 1)
                with act.Fori(0, 4) as i:
                    for s in range(2):
                        channel(2 * i + s, s, True)
                with act.Fori(4, 6) as i:
                    for s in range(2):
                        channel(2 * i + s, s, False)

            @block.vector
            def _(dve):
                dve.memset(ones[:, :], 1.0)
                dve.memset(eps[:, :], EPS)
                dve.memset(xp[:, 0:3], 0.0)
                dve.memset(gT[:, :, TOK:TOKP], 0.0)
                dve.drain()
                dve.sem_inc(ones_ready, 1)
                dve.sem_inc(conv_done, 1)
                dve.sem_inc(channel_done, 1)
                dve.wait_ge(small_here, 32)

                def channel(c, scale):
                    dve.tensor_copy(tap[:, :], conv_w[:, ds(c, 1), :].rearrange("p a k -> p (a k)"))
                    dve.tensor_copy(xs[:, :, 0:3], conv_buf[:, ds(c, 1), :, :].rearrange("p a b k -> p (a b) k"))
                    dve.drain()
                    dve.wait_ge(x_ready, c + 1)
                    g = gT[:, ds(c, 1), 0:SEQ].rearrange("p a n -> p (a n)")
                    gs = gT[:, ds(c, 1), SEQ:TOK].rearrange("p a (b t) -> p (a b) t", t=NT)
                    dve.tensor_scalar(g, xp[:, 0:SEQ], tap[:, 0:1], None, ALU.mult)
                    dve.tensor_scalar(gs, xs[:, :, 0:NT], tap[:, 0:1], None, ALU.mult)
                    for k in range(1, 4):
                        dve.drain()
                        dve.scalar_tensor_tensor(g, xp[:, k:SEQ + k], tap[:, k:k + 1], g, ALU.mult, ALU.add)
                        dve.scalar_tensor_tensor(gs, xs[:, :, k:NT + k], tap[:, k:k + 1], gs, ALU.mult, ALU.add)
                    kc = kept[:, ds(c, 1), :].rearrange("p a k -> p (a k)")
                    dve.tensor_copy(kc[:, 0:3], xp[:, SEQ:SEQ + 3])
                    dve.tensor_copy(kc[:, 3:27].rearrange("p (b k) -> p b k", k=3), xs[:, :, NT:NT + 3])
                    dve.drain()
                    dve.sem_inc(conv_done, 1)
                    if scale is None:
                        return
                    dve.wait_ge(root_ready, c + 1)
                    dve.reciprocal(nrm[:, :], nrm[:, :])
                    dve.drain()
                    ga = gT[:, ds(c, 1), 0:TOK].rearrange("p a n -> p (a n)")
                    dve.scalar_tensor_tensor(ga, ga, scale, nrm[:, :], ALU.mult, ALU.mult).then_inc(channel_done, 1)

                for lo, hi, scale in ((0, 2, P ** -0.5), (2, 4, 1.0), (4, 6, None)):
                    with dve.Fori(lo, hi) as i:
                        for s in range(2):
                            channel(2 * i + s, scale)


def stage_delta(nc, io, scr, gT, ident, half, sample):
    kind = "s" if sample else "p"
    H, C = 4, (NT if sample else 64)
    L = 3 if sample else 6
    with Stage(nc, "delta_" + kind) as st:
        masks = st.sb("masks", [P, 8, P])
        ones = st.sb("ones", [P, P])
        norm_w = st.sb("norm_w", [P, P])
        gates = st.sb("gates", [P, NTILE, 32])
        cur = st.sb("cur", [P, 12, P])
        bg = st.sb("bg", [P, 8])
        ug = st.sb("ug", [P, H, P])
        bd = st.sb("bd", [P, H, P])
        gsm = st.sb("gsm", [P, 8])
        dec = st.sb("dec", [P, H, P])
        er = st.sb("er", [P, H, P])
        ex = st.sb("ex", [P, 8])
        qkT = st.sb("qkT", [P, H, P])
        bm = st.sb("bm", [P, H, P])
        wr = st.sb("wr", [P, H, P])
        kd = st.sb("kd", [P, H, P])
        vb = st.sb("vb", [P, H, P])
        tm = st.sb("tm", [P, H, P])
        X = st.sb("X", [P, H, P])
        Z = st.sb("Z", [P, H, P])
        Y = st.sb("Y", [P, H, P])
        u = st.sb("u", [P, H, P])
        wq = st.sb("wq", [P, H, 2, P])
        vn = st.sb("vn", [P, H, P])
        nS = NB if sample else 1
        S = st.sb("S", [P, H, nS, P])
        zt = st.sb("zt", [P, H, P])
        o = st.sb("o", [P, H, P])
        osq = st.sb("osq", [P, H, P])
        oss = st.sb("oss", [P, H])
        ors = st.sb("ors", [P, H])
        if sample:
            bsel = st.sb("bsel", [SAMP, NB])
            vx = st.sb("vx", [SAMP, NB, P])
            back = st.sb("back", [P, H, 2, SAMP])
            o_in = st.sb("o_in", [SAMP, H, P])
        bank = [st.ps(f"b{k}") for k in range(8)]

        here = st.sem("here")
        z_here = st.sem("z_here")
        ones_ready = st.sem("ones_ready")
        cur_ready = st.sem("cur_ready")
        src_ready = st.sem("src_ready")
        pairs_done = st.sem("pairs_done")
        gsm_ready = st.sem("gsm_ready")
        er_ready = st.sem("er_ready")
        arg_ready = st.sem("arg_ready")
        dec_ready = st.sem("dec_ready")
        mats_ready = st.sem("mats_ready")
        tm_ready = st.sem("tm_ready")
        y_done = st.sem("y_done")
        y_ready = st.sem("y_ready")
        step_done = st.sem("step_done")
        xz_ready = st.sem("xz_ready")
        uw_done = st.sem("uw_done")
        u_ready = st.sem("u_ready")
        w_ready = st.sem("w_ready")
        qd_ready = st.sem("qd_ready")
        ws_done = st.sem("ws_done")
        vn_ready = st.sem("vn_ready")
        chunk_done = st.sem("chunk_done")
        S_ready = st.sem("S_ready")
        osq_ready = st.sem("osq_ready")
        oss_ready = st.sem("oss_ready")
        ors_ready = st.sem("ors_ready")
        o_ready = st.sem("o_ready")
        o_out = st.sem("o_out")
        turns = st.sem("turns")
        pool_turns = st.sem("pool_turns")
        back_ready = st.sem("back_ready")
        NC = 1 if sample else 2
        n_here = 8 if sample else 3

        def tiles(eng, body):
            if sample:
                body(0)
            else:
                with eng.Fori(0, 8) as j:
                    body(j)

        def col(ap, h=H, n=P):
            return ap.unsqueeze(2).to_broadcast([P, h, n])

        def head(ap):
            return ap.unsqueeze(1).to_broadcast([P, H, P])

        def flat(t):
            return t[:, :, :].rearrange("p a b -> p (a b)")

        with nc.Block() as block:

            @block.sync
            def _(sp):
                sp.dma_start(masks[:, :, :], io["gm_" + kind]).then_inc(here, 16)
                sp.dma_start(norm_w[:, :], io["gdn_norm_w"].partition_broadcast(P)).then_inc(here, 16)
                sp.dma_start(gates[:, :, :], scr["misc"].rearrange("(t p) n -> p t n", p=P)).then_inc(here, 16)
                if sample:
                    sp.dma_start(bsel[:, :], io["bsel"]).then_inc(here, 16)
                    for h in range(H):
                        sp.dma_start(S[:, h, :, :], io["state_gdn"][:, h].rearrange("b k d -> k b d")).then_inc(here, 16)

                def tile(j):
                    row = ds(j * P, P) if not sample else slice(SEQ, SEQ + P)
                    wait_turn(sp, o_ready, j + 1, turns)
                    sp.dma_start(flat(zt), scr["z"][row, :]).then_inc(z_here, 16)
                    wait_turn(sp, o_ready, j + 2, turns)
                    sp.dma_start(scr["mix"][row, 512:1024], flat(o)).then_inc(o_out, 16)
                    wait_turn(sp, o_out, 16 * (j + 1), turns)

                tiles(sp, tile)
                if sample:
                    for h in range(H):
                        sp.dma_start(io["gstate_s"][:, h].rearrange("b k d -> k b d"), S[:, h, :, :]).then_inc(o_out, 16)
                else:
                    sp.wait_ge(S_ready, 17)
                    sp.dma_start(io["gstate_p"].rearrange("h k d -> k h d"), S[:, :, 0, :]).then_inc(o_out, 16)
                sp.wait_ge(o_out, 16 * (5 if sample else 9))

            @block.scalar
            def _(act):
                def tile(j):
                    tok = ds(j * P, P) if not sample else slice(SEQ, SEQ + P)
                    act.wait_ge(o_ready, j + 1)
                    act.activation(cur[:, :, :], gT[:, :, tok], ACT.Copy).then_inc(cur_ready, 1)
                    act.wait_ge(gsm_ready, j + 1)
                    act.activation(flat(er), bank[0][:, :], ACT.Exp)
                    act.activation(ex[:, :], gsm[:, :], ACT.Exp).then_inc(er_ready, 1)
                    act.wait_ge(arg_ready, j + 1)
                    act.activation(flat(dec), flat(dec), ACT.Exp).then_inc(dec_ready, 1)
                    act.wait_ge(uw_done, j + 1)
                    act.activation(wq[:, :, 0, :], bank[6][:, :].rearrange("p (h n) -> p h n", h=H), ACT.Copy).then_inc(w_ready, 1)
                    if sample:
                        act.wait_ge(ws_done, 1)
                        act.activation(back[:, :, :, :].rearrange("p a b c -> p (a b c)"), bank[0][:, :], ACT.Copy).then_inc(back_ready, 1)
                    act.wait_ge(chunk_done, NC * (j + 1))
                    if not sample:
                        act.activation(flat(osq), bank[1][:, :], ACT.Square).then_inc(osq_ready, 1)

                tiles(act, tile)

            @block.gpsimd
            def _(pool):
                pool.wait_ge(here, 16 * n_here)

                def tile(j):
                    for l in range(L):
                        wait_turn(pool, mats_ready, j + 1, pool_turns)
                        if l == 1:
                            wait_turn(pool, xz_ready, L * j + 1, pool_turns)
                        elif l:
                            wait_turn(pool, y_done, L * j + l, pool_turns)
                        pool.tensor_tensor(tm[:, :, :], bm[:, :, :], head(masks[:, 2 + l, :]), ALU.mult).then_inc(tm_ready, 1)
                        if l == 0:
                            pool.tensor_tensor(wq[:, :, 1, :], cur[:, 0:4, :], er[:, :, :], ALU.mult).then_inc(qd_ready, 1)
                    wait_turn(pool, oss_ready, j + 1, pool_turns)
                    pool_rsqrt(pool, ors[:, :], oss[:, :], P, half[:, 0:H]).then_inc(ors_ready, 1)

                tiles(pool, tile)

            @block.tensor
            def _(pe):
                pe.wait_ge(here, 16 * n_here)
                pe.wait_ge(ones_ready, 1)

                def per_head(out, lhs, rhs):
                    for h in range(H):
                        m = pe.matmul(out[:, h * P:(h + 1) * P], lhs(h), rhs(h), start=True, stop=True)
                    return m

                def tile(j):
                    pe.wait_ge(src_ready, j + 1)
                    pe.matmul(bank[0][:, :], ones[:, :], flat(ug), start=True, stop=True)
                    pe.matmul(bank[1][:, :], ones[:, :], flat(bd), start=True, stop=True)
                    pe.matmul(bank[2][:, 0:4], masks[:, 0, :], bg[:, 4:8], start=True, stop=True)
                    pe.matmul(bank[2][:, 4:8], masks[:, 1, :], bg[:, 4:8], start=True, stop=True)
                    pe.wait_ge(cur_ready, j + 1)
                    for h in range(H):
                        pe.transpose(bank[3][:, h * P:(h + 1) * P], cur[:, 4 + h, :], ident[:, :])
                    for h in range(H):
                        pe.transpose(bank[4][:, h * P:(h + 1) * P], cur[:, 8 + h, :], ident[:, :])
                    per_head(bank[5], lambda h: cur[:, 4 + h, :], lambda h: cur[:, 4 + h, :])
                    per_head(bank[6], lambda h: cur[:, 4 + h, :], lambda h: cur[:, h, :]).then_inc(pairs_done, 1)
                    for l in range(L):
                        pe.wait_ge(tm_ready, L * j + l + 1)
                        if l:
                            pe.wait_ge(xz_ready, L * j + l)
                        per_head(bank[7], lambda h: tm[:, h, :],
                                 lambda h: X[:, h, :] if l else ident[:, :]).then_inc(y_done, 1)
                        if l:
                            pe.wait_ge(y_ready, L * j + l + 1)
                            per_head(bank[3], lambda h: Z[:, h, :], lambda h: Y[:, h, :])
                            per_head(bank[4], lambda h: Y[:, h, :], lambda h: Z[:, h, :]).then_inc(step_done, 1)
                    pe.wait_ge(xz_ready, L * j + L)
                    per_head(bank[5], lambda h: Z[:, h, :], lambda h: vb[:, h, :])
                    per_head(bank[6], lambda h: wr[:, h, :], lambda h: Z[:, h, :]).then_inc(uw_done, 1)
                    pe.wait_ge(w_ready, j + 1)
                    pe.wait_ge(qd_ready, j + 1)
                    if sample:
                        scan_sample()
                        return
                    for c in range(2):
                        r = slice(64 * c, 64 * c + 64)
                        pe.wait_ge(S_ready, 2 * j + c + 1)
                        for h in range(H):
                            m = pe.matmul(bank[0][r, h * P:(h + 1) * P], wq[:, h, 0, r], S[:, h, 0, :], start=True, stop=True)
                        m.then_inc(ws_done, 1)
                        pe.wait_ge(vn_ready, 2 * j + c + 1)
                        for h in range(H):
                            n = slice(h * P, (h + 1) * P)
                            pe.matmul(bank[7][:, n], kd[r, h, :], vn[r, h, :], start=True, stop=True)
                            pe.matmul(bank[1][r, n], wq[:, h, 1, r], S[:, h, 0, :], start=True, stop=False)
                            m = pe.matmul(bank[1][r, n], qkT[r, h, r], vn[r, h, :], start=False, stop=True)
                        m.then_inc(chunk_done, 1)

                def scan_sample():
                    for h in range(H):
                        for b in range(NB):
                            t = slice(b * NT, (b + 1) * NT)
                            out = bank[0][:, h * P:(h + 1) * P].rearrange("p (w t) -> p w t", w=2)[:, :, t]
                            m = pe.matmul(out, S[:, h, b, :], wq[:, h, :, t], start=True, stop=True)
                    m.then_inc(ws_done, 1)
                    pe.wait_ge(back_ready, 1)
                    for h in range(H):
                        pe.transpose(bank[2][0:SAMP, h * P:(h + 1) * P], back[:, h, 0, :], ident[:, :])
                    for h in range(H):
                        m = pe.transpose(bank[3][0:SAMP, h * P:(h + 1) * P], back[:, h, 1, :], ident[:, :])
                    m.then_inc(back_ready, 1)
                    pe.wait_ge(vn_ready, 1)
                    for h in range(H):
                        m = pe.matmul(bank[1][0:SAMP, h * P:(h + 1) * P], qkT[0:SAMP, h, 0:SAMP], vn[0:SAMP, h, :], start=True, stop=True)
                    m.then_inc(chunk_done, 1)
                    for h in range(H):
                        pe.wait_ge(vn_ready, 2 + h)
                        pe.matmul(bank[4][:, :], kd[0:SAMP, h, :], vx[:, 0:4, :].rearrange("p a b -> p (a b)"), start=True, stop=True)
                        m = pe.matmul(bank[5][:, :], kd[0:SAMP, h, :], vx[:, 4:8, :].rearrange("p a b -> p (a b)"), start=True, stop=True)
                        m.then_inc(chunk_done, 1)

                tiles(pe, tile)

            @block.vector
            def _(dve):
                dve.memset(ones[:, :], 1.0)
                if not sample:
                    dve.memset(S[:, :, :, :], 0.0)
                dve.drain()
                dve.sem_inc(ones_ready, 1)
                dve.sem_inc(S_ready, 1)
                dve.sem_inc(o_ready, 1)
                dve.wait_ge(here, 16 * n_here)

                def tile(j):
                    t = ds(j, 1) if not sample else slice(8, 9)
                    dve.tensor_copy(bg[:, :], gates[:, t, 24:32].rearrange("p a n -> p (a n)"))
                    dve.drain()
                    dve.tensor_tensor(ug[:, :, :], head(masks[:, 0, :]), col(bg[:, 4:8]), ALU.mult)
                    dve.tensor_tensor(bd[:, :, :], head(ident[:, :]), col(bg[:, 0:4]), ALU.mult)
                    dve.drain()
                    dve.sem_inc(src_ready, 1)
                    dve.wait_ge(pairs_done, j + 1)
                    dve.tensor_copy(gsm[:, 0:4], bank[2][:, 0:4])
                    dve.drain()
                    dve.tensor_tensor(gsm[:, 4:8], bank[2][:, 4:8], gsm[:, 0:4], ALU.subtract)
                    dve.tensor_tensor(dec[:, :, :], bank[0][:, :].rearrange("p (h n) -> p h n", h=H), col(gsm[:, 0:4]), ALU.subtract)
                    dve.drain()
                    dve.tensor_scalar(dec[:, :, :], dec[:, :, :], 0.0, None, ALU.min).then_inc(arg_ready, 1)
                    dve.sem_inc(gsm_ready, 1)
                    dve.wait_ge(er_ready, j + 1)
                    dve.wait_ge(dec_ready, j + 1)
                    dve.tensor_tensor(ex[:, 0:4], ex[:, 0:4], bg[:, 0:4], ALU.mult)
                    dve.tensor_tensor(dec[:, :, :], dec[:, :, :], head(masks[:, 0, :]), ALU.mult)
                    dve.drain()
                    dve.tensor_tensor(bm[:, :, :], bank[5][:, :].rearrange("p (h n) -> p h n", h=H), dec[:, :, :], ALU.mult)
                    dve.tensor_tensor(qkT[:, :, :], bank[6][:, :].rearrange("p (h n) -> p h n", h=H), dec[:, :, :], ALU.mult)
                    dve.drain()
                    dve.tensor_tensor(flat(bm), flat(bm), bank[1][:, :], ALU.mult).then_inc(mats_ready, 1)
                    dve.tensor_tensor(wr[:, :, :], bank[3][:, :].rearrange("p (h n) -> p h n", h=H), col(ex[:, 0:4]), ALU.mult)
                    dve.tensor_tensor(kd[:, :, :], bank[3][:, :].rearrange("p (h n) -> p h n", h=H), col(ex[:, 4:8]), ALU.mult)
                    dve.tensor_tensor(vb[:, :, :], bank[4][:, :].rearrange("p (h n) -> p h n", h=H), col(bg[:, 0:4]), ALU.mult)
                    for l in range(L):
                        dve.wait_ge(y_done, L * j + l + 1)
                        if l == 0:
                            dve.tensor_tensor(X[:, :, :], head(ident[:, :]), bank[7][:, :].rearrange("p (h n) -> p h n", h=H), ALU.subtract)
                            dve.tensor_tensor(Z[:, :, :], head(ident[:, :]), tm[:, :, :], ALU.subtract)
                            dve.drain()
                            dve.sem_inc(y_ready, 1)
                            dve.sem_inc(xz_ready, 1)
                            continue
                        dve.tensor_copy(flat(Y), bank[7][:, :]).then_inc(y_ready, 1)
                        dve.wait_ge(step_done, (L - 1) * j + l)
                        dve.tensor_tensor(flat(X), flat(X), bank[3][:, :], ALU.subtract)
                        dve.tensor_tensor(flat(Z), flat(Z), bank[4][:, :], ALU.subtract)
                        dve.drain()
                        dve.sem_inc(xz_ready, 1)
                    dve.wait_ge(uw_done, j + 1)
                    dve.tensor_copy(flat(u), bank[5][:, :])
                    dve.drain()
                    if sample:
                        scan_sample()
                    else:
                        for c in range(2):
                            r = slice(64 * c, 64 * c + 64)
                            dve.wait_ge(ws_done, 2 * j + c + 1)
                            dve.tensor_tensor(vn[r, :, :], u[r, :, :], bank[0][r, :].rearrange("p (h n) -> p h n", h=H),
                                              ALU.subtract).then_inc(vn_ready, 1)
                            dve.wait_ge(chunk_done, 2 * j + c + 1)
                            last = er[:, :, 64 * c + 63]
                            dve.tensor_tensor(S[:, :, 0, :], S[:, :, 0, :], col(last), ALU.mult)
                            dve.drain()
                            dve.tensor_tensor(S[:, :, 0, :], S[:, :, 0, :], bank[7][:, :].rearrange("p (h n) -> p h n", h=H),
                                              ALU.add).then_inc(S_ready, 1)
                        dve.wait_ge(osq_ready, j + 1)
                        src = bank[1][:, :].rearrange("p (h n) -> p h n", h=H)
                        finish(j, src, P)

                def finish(j, src, n):
                    dve.tensor_reduce(oss[0:n, :], osq[0:n, :, :], AX, ALU.add).then_inc(oss_ready, 1)
                    dve.wait_ge(ors_ready, j + 1)
                    dve.wait_ge(z_here, 16 * (j + 1))
                    dve.tensor_tensor(o[0:n, :, :], src, ors[0:n, :].unsqueeze(2).to_broadcast([n, H, P]), ALU.mult)
                    dve.drain()
                    dve.tensor_tensor(o[0:n, :, :], o[0:n, :, :], norm_w[0:n, :].unsqueeze(1).to_broadcast([n, H, P]), ALU.mult)
                    dve.drain()
                    dve.tensor_tensor(o[0:n, :, :], o[0:n, :, :], zt[0:n, :, :], ALU.mult)
                    dve.drain()
                    dve.sem_inc(o_ready, 1)

                def scan_sample():
                    n = SAMP
                    dve.wait_ge(back_ready, 2)
                    v3 = lambda b: b[0:n, :].rearrange("p (h n) -> p h n", h=H)
                    dve.tensor_tensor(vn[0:n, :, :], u[0:n, :, :], v3(bank[2]), ALU.subtract).then_inc(vn_ready, 1)
                    dve.tensor_copy(o_in[:, :, :], v3(bank[3]))
                    dve.drain()
                    dve.wait_ge(chunk_done, 1)
                    dve.tensor_tensor(o_in[:, :, :], o_in[:, :, :], v3(bank[1]), ALU.add)
                    dve.drain()
                    dve.memset(oss[:, :], 1.0)
                    dve.memset(o[:, :, :], 0.0)
                    dve.tensor_tensor(osq[0:n, :, :], o_in[:, :, :], o_in[:, :, :], ALU.mult)
                    for h in range(H):
                        dve.tensor_tensor(vx[:, :, :], vn[0:n, h, :].unsqueeze(1).to_broadcast([n, NB, P]),
                                          bsel[:, :].unsqueeze(2).to_broadcast([n, NB, P]), ALU.mult).then_inc(vn_ready, 1)
                        keep = er[:, h, 0:SAMP].rearrange("p (b t) -> p b t", t=NT)[:, :, NT - 1]
                        dve.wait_ge(chunk_done, 2 + h)
                        dve.tensor_tensor(S[:, h, :, :], S[:, h, :, :], keep.unsqueeze(2).to_broadcast([P, NB, P]), ALU.mult)
                        dve.drain()
                        dve.tensor_tensor(S[:, h, 0:4, :], S[:, h, 0:4, :], bank[4][:, :].rearrange("p (h n) -> p h n", h=4), ALU.add)
                        dve.tensor_tensor(S[:, h, 4:8, :], S[:, h, 4:8, :], bank[5][:, :].rearrange("p (h n) -> p h n", h=4), ALU.add)
                        dve.drain()
                    finish(0, o_in[:, :, :], n)

                tiles(dve, tile)


def stage_delta_prompt(nc, io, scr, gT, ident, half):
    H, L, C = 4, 6, 64
    ROUNDS = SEQ // P // 2
    with Stage(nc, "delta_p") as st:
        masks = st.sb("masks", [P, 8, P])
        ones = st.sb("ones", [P, P])
        norm_w = st.sb("norm_w", [P, P])
        gates = st.sb("gates", [P, NTILE, 32])
        S = st.sb("S", [P, 2, H, P])

        def slots(name, shape):
            return [st.sb(f"{name}{s}", shape) for s in range(2)]

        cur = slots("cur", [P, 12, P])
        bg = slots("bg", [P, 8])
        ug_y = slots("ug_y", [P, H, P])
        bd_vn = slots("bd_vn", [P, H, P])
        dec_sq = slots("dec_sq", [P, H, P])
        gsm = slots("gsm", [P, 8])
        er = slots("er", [P, H, P])
        ex = slots("ex", [P, 8])
        qkT = slots("qkT", [P, H, P])
        bm = slots("bm", [P, H, P])
        wr = slots("wr", [P, H, P])
        kd = slots("kd", [P, H, P])
        vb = slots("vb", [P, H, P])
        tm = slots("tm", [P, H, P])
        X = slots("X", [P, H, P])
        Z = slots("Z", [P, H, P])
        u = slots("u", [P, H, P])
        wq = slots("wq", [P, H, 2, P])
        zt = slots("zt", [P, H, P])
        o = slots("o", [P, H, P])
        oss = slots("oss", [P, H])
        ors = slots("ors", [P, H])
        bank = [st.ps(f"b{k}") for k in range(8)]
        Y_BANK, X_BANK, Z_BANK = (7, 0), (3, 1), (4, 2)
        U_BANK, W_BANK, O_BANK = (5, 3), (6, 7), (1, 7)

        here = st.sem("here")
        ones_ready = st.sem("ones_ready")

        def by_slot(name):
            return [st.sem(f"{name}{s}") for s in range(2)]

        z_here = by_slot("z_here")
        cur_ready = by_slot("cur_ready")
        src_ready = by_slot("src_ready")
        pairs_done = by_slot("pairs_done")
        gsm_ready = by_slot("gsm_ready")
        er_ready = by_slot("er_ready")
        arg_ready = by_slot("arg_ready")
        dec_ready = by_slot("dec_ready")
        mats_ready = by_slot("mats_ready")
        banks_read = by_slot("banks_read")
        tm_ready = by_slot("tm_ready")
        y_done = by_slot("y_done")
        y_ready = by_slot("y_ready")
        step_done = by_slot("step_done")
        xz_ready = by_slot("xz_ready")
        uw_done = by_slot("uw_done")
        w_ready = by_slot("w_ready")
        qd_ready = by_slot("qd_ready")
        out_done = by_slot("out_done")
        sq_ready = by_slot("sq_ready")
        oss_ready = by_slot("oss_ready")
        ors_ready = by_slot("ors_ready")
        o_ready = by_slot("o_ready")
        ws_done = st.sem("ws_done")
        vn_ready = st.sem("vn_ready")
        kv_done = st.sem("kv_done")
        S_ready = st.sem("S_ready")
        o_out = st.sem("o_out")
        turns = st.sem("turns")
        pool_turns = st.sem("pool_turns")

        def col(ap, h=H, n=P):
            return ap.unsqueeze(2).to_broadcast([P, h, n])

        def head(ap):
            return ap.unsqueeze(1).to_broadcast([P, H, P])

        def flat(t):
            return t[:, :, :].rearrange("p a b -> p (a b)")

        def heads_of(b, r=slice(0, P)):
            return bank[b][r, :].rearrange("p (h n) -> p h n", h=H)

        def run(eng, two_tiles):
            with eng.Fori(0, ROUNDS - 1) as i:
                two_tiles(i, False)
            two_tiles(ROUNDS - 1, True)

        with nc.Block() as block:

            @block.sync
            def _(sp):
                sp.dma_start(masks[:, :, :], io["gm_p"]).then_inc(here, 16)
                sp.dma_start(norm_w[:, :], io["gdn_norm_w"].partition_broadcast(P)).then_inc(here, 16)
                sp.dma_start(gates[:, :, :], scr["misc"].rearrange("(t p) n -> p t n", p=P)).then_inc(here, 16)
                with sp.Fori(0, ROUNDS) as i:
                    for s in range(2):
                        row = ds((2 * i + s) * P, P)
                        wait_turn(sp, o_ready[s], i + 1, turns)
                        sp.dma_start(flat(zt[s]), scr["z"][row, :]).then_inc(z_here[s], 16)
                    for s in range(2):
                        row = ds((2 * i + s) * P, P)
                        wait_turn(sp, o_ready[s], i + 2, turns)
                        sp.dma_start(scr["mix"][row, 512:1024], flat(o[s])).then_inc(o_out, 16)
                    wait_turn(sp, o_out, 32 * (i + 1), turns)
                sp.wait_ge(S_ready, 4 * ROUNDS + 1)
                sp.dma_start(io["gstate_p"].rearrange("h k d -> k h d"), S[:, 0, :, :]).then_inc(o_out, 16)
                sp.wait_ge(o_out, 32 * ROUNDS + 16)

            @block.scalar
            def _(act):
                def take(j, s):
                    act.activation(cur[s][:, :, :], gT[:, :, ds(j * P, P)], ACT.Copy).then_inc(cur_ready[s], 1)

                def two_tiles(i, last):
                    for s in range(2):
                        act.wait_ge(gsm_ready[s], i + 1)
                        act.activation(flat(er[s]), bank[0][:, :], ACT.Exp)
                        act.activation(ex[s][:, :], gsm[s][:, :], ACT.Exp).then_inc(er_ready[s], 1)
                        act.wait_ge(arg_ready[s], i + 1)
                        act.activation(flat(dec_sq[s]), flat(dec_sq[s]), ACT.Exp).then_inc(dec_ready[s], 1)
                    for l in range(1, L):
                        for s in range(2):
                            act.wait_ge(y_done[s], L * i + l + 1)
                            act.activation(flat(ug_y[s]), bank[Y_BANK[s]][:, :], ACT.Copy).then_inc(y_ready[s], 1)
                    for s in range(2):
                        act.wait_ge(uw_done[s], i + 1)
                        act.activation(wq[s][:, :, 0, :], heads_of(W_BANK[s]), ACT.Copy).then_inc(w_ready[s], 1)
                    if not last:
                        for s in range(2):
                            act.wait_ge(qd_ready[s], i + 1)
                            take(2 * i + 2 + s, s)
                    for s in range(2):
                        act.wait_ge(out_done[s], 2 * (i + 1))
                        act.activation(flat(dec_sq[s]), bank[O_BANK[s]][:, :], ACT.Square).then_inc(sq_ready[s], 1)

                for s in range(2):
                    take(s, s)
                run(act, two_tiles)

            @block.gpsimd
            def _(pool):
                pool.wait_ge(here, 48)
                with pool.Fori(0, ROUNDS) as i:
                    for l in range(L):
                        for s in range(2):
                            if l == 0:
                                wait_turn(pool, mats_ready[s], i + 1, pool_turns)
                            elif l == 1:
                                wait_turn(pool, xz_ready[s], L * i + 1, pool_turns)
                            else:
                                wait_turn(pool, y_done[s], L * i + l, pool_turns)
                            pool.tensor_tensor(tm[s][:, :, :], bm[s][:, :, :], head(masks[:, 2 + l, :]), ALU.mult).then_inc(tm_ready[s], 1)
                            if l == 0:
                                pool.tensor_tensor(wq[s][:, :, 1, :], cur[s][:, 0:4, :], er[s][:, :, :], ALU.mult).then_inc(qd_ready[s], 1)
                    for s in range(2):
                        wait_turn(pool, oss_ready[s], i + 1, pool_turns)
                        pool_rsqrt(pool, ors[s][:, :], oss[s][:, :], P, half[:, 0:H]).then_inc(ors_ready[s], 1)

            @block.tensor
            def _(pe):
                pe.wait_ge(here, 48)
                pe.wait_ge(ones_ready, 1)

                def per_head(out, lhs, rhs):
                    for h in range(H):
                        m = pe.matmul(bank[out][:, h * P:(h + 1) * P], lhs(h), rhs(h), start=True, stop=True)
                    return m

                def prepare(i, s):
                    c = cur[s]
                    pe.wait_ge(src_ready[s], i + 1)
                    if s:
                        pe.wait_ge(banks_read[0], i + 1)
                    pe.matmul(bank[0][:, :], ones[:, :], flat(ug_y[s]), start=True, stop=True)
                    pe.matmul(bank[2][:, 0:4], masks[:, 0, :], bg[s][:, 4:8], start=True, stop=True)
                    pe.matmul(bank[2][:, 4:8], masks[:, 1, :], bg[s][:, 4:8], start=True, stop=True)
                    pe.wait_ge(cur_ready[s], i + 1)
                    for h in range(H):
                        pe.transpose(bank[3][:, h * P:(h + 1) * P], c[:, 4 + h, :], ident[:, :])
                    for h in range(H):
                        pe.transpose(bank[4][:, h * P:(h + 1) * P], c[:, 8 + h, :], ident[:, :])
                    per_head(5, lambda h: c[:, 4 + h, :], lambda h: c[:, 4 + h, :])
                    per_head(6, lambda h: c[:, 4 + h, :], lambda h: c[:, h, :])
                    if s == 0:
                        pe.wait_ge(o_ready[0], i + 1)
                    pe.matmul(bank[1][:, :], ones[:, :], flat(bd_vn[s]), start=True, stop=True).then_inc(pairs_done[s], 1)

                def scan(i, s):
                    pe.wait_ge(w_ready[s], i + 1)
                    pe.wait_ge(qd_ready[s], i + 1)
                    for c in range(2):
                        r = slice(C * c, C * c + C)
                        n = 4 * i + 2 * s + c
                        each = [slice(h * P, (h + 1) * P) for h in range(H)]
                        pe.wait_ge(S_ready, n + 1)
                        for h in range(H):
                            m = pe.matmul(bank[0][r, each[h]], wq[s][:, h, 0, r], S[:, c, h, :], start=True, stop=True)
                        m.then_inc(ws_done, 1)
                        for h in range(H):
                            pe.matmul(bank[O_BANK[s]][r, each[h]], wq[s][:, h, 1, r], S[:, c, h, :], start=(h == 0), stop=False,
                                      skip_group_check=True)
                        pe.wait_ge(vn_ready, n + 1)
                        for h in range(H):
                            m = pe.matmul(bank[4][:, each[h]], kd[s][r, h, :], bd_vn[s][r, h, :], start=True, stop=True)
                        m.then_inc(kv_done, 1)
                        for h in range(H):
                            m = pe.matmul(bank[O_BANK[s]][r, each[h]], qkT[s][r, h, r], bd_vn[s][r, h, :], start=False, stop=True,
                                          skip_group_check=True)
                        m.then_inc(out_done[s], 1)

                with pe.Fori(0, ROUNDS) as i:
                    prepare(i, 0)
                    prepare(i, 1)
                    for l in range(L):
                        for s in range(2):
                            if l == 0 and s == 0:
                                pe.wait_ge(o_ready[1], i + 1)
                            if l:
                                pe.wait_ge(xz_ready[s], L * i + l)
                            pe.wait_ge(tm_ready[s], L * i + l + 1)
                            per_head(Y_BANK[s], lambda h: tm[s][:, h, :],
                                     lambda h: X[s][:, h, :] if l else ident[:, :]).then_inc(y_done[s], 1)
                        if l == 1:
                            pe.wait_ge(banks_read[1], i + 1)
                        for s in range(2):
                            if l:
                                pe.wait_ge(y_ready[s], (L - 1) * i + l)
                                if l < L - 1:
                                    per_head(X_BANK[s], lambda h: Z[s][:, h, :], lambda h: ug_y[s][:, h, :])
                                per_head(Z_BANK[s], lambda h: ug_y[s][:, h, :], lambda h: Z[s][:, h, :]).then_inc(step_done[s], 1)
                    for s in range(2):
                        pe.wait_ge(xz_ready[s], L * i + L)
                        per_head(W_BANK[s], lambda h: wr[s][:, h, :], lambda h: Z[s][:, h, :])
                        per_head(U_BANK[s], lambda h: Z[s][:, h, :], lambda h: vb[s][:, h, :]).then_inc(uw_done[s], 1)
                    for s in range(2):
                        scan(i, s)

            @block.vector
            def _(dve):
                dve.memset(ones[:, :], 1.0)
                dve.memset(S[:, :, :, :], 0.0)
                dve.drain()
                dve.sem_inc(ones_ready, 1)
                dve.sem_inc(S_ready, 1)
                for s in range(2):
                    dve.sem_inc(o_ready[s], 1)
                dve.wait_ge(here, 48)

                def begin(i, s):
                    j = 2 * i + s
                    dve.tensor_copy(bg[s][:, :], gates[:, ds(j, 1), 24:32].rearrange("p a n -> p (a n)"))
                    dve.drain()
                    dve.tensor_tensor(ug_y[s][:, :, :], head(masks[:, 0, :]), col(bg[s][:, 4:8]), ALU.mult)
                    dve.tensor_tensor(bd_vn[s][:, :, :], head(ident[:, :]), col(bg[s][:, 0:4]), ALU.mult)
                    dve.drain()
                    dve.sem_inc(src_ready[s], 1)

                def matrices(i, s):
                    dec, g, e = dec_sq[s], gsm[s], ex[s]
                    dve.wait_ge(pairs_done[s], i + 1)
                    dve.tensor_copy(g[:, 0:4], bank[2][:, 0:4])
                    dve.drain()
                    dve.tensor_tensor(g[:, 4:8], bank[2][:, 4:8], g[:, 0:4], ALU.subtract)
                    dve.tensor_tensor(dec[:, :, :], heads_of(0), col(g[:, 0:4]), ALU.subtract)
                    dve.drain()
                    dve.sem_inc(gsm_ready[s], 1)
                    dve.tensor_scalar(dec[:, :, :], dec[:, :, :], 0.0, None, ALU.min).then_inc(arg_ready[s], 1)
                    dve.wait_ge(er_ready[s], i + 1)
                    dve.tensor_tensor(e[:, 0:4], e[:, 0:4], bg[s][:, 0:4], ALU.mult)
                    dve.tensor_tensor(vb[s][:, :, :], heads_of(4), col(bg[s][:, 0:4]), ALU.mult)
                    dve.wait_ge(dec_ready[s], i + 1)
                    dve.tensor_tensor(dec[:, :, :], dec[:, :, :], head(masks[:, 0, :]), ALU.mult)
                    dve.drain()
                    dve.tensor_tensor(bm[s][:, :, :], heads_of(5), dec[:, :, :], ALU.mult)
                    dve.tensor_tensor(qkT[s][:, :, :], heads_of(6), dec[:, :, :], ALU.mult)
                    dve.drain()
                    dve.tensor_tensor(flat(bm[s]), flat(bm[s]), bank[1][:, :], ALU.mult).then_inc(mats_ready[s], 1)
                    dve.tensor_tensor(wr[s][:, :, :], heads_of(3), col(e[:, 0:4]), ALU.mult)
                    dve.tensor_tensor(kd[s][:, :, :], heads_of(3), col(e[:, 4:8]), ALU.mult)
                    dve.drain()
                    dve.sem_inc(banks_read[s], 1)

                def scan(i, s):
                    for c in range(2):
                        r = slice(C * c, C * c + C)
                        n = 4 * i + 2 * s + c
                        dve.wait_ge(ws_done, n + 1)
                        dve.tensor_tensor(bd_vn[s][r, :, :], u[s][r, :, :], heads_of(0, r), ALU.subtract).then_inc(vn_ready, 1)
                        dve.tensor_tensor(S[:, 1 - c, :, :], S[:, c, :, :], col(er[s][:, :, C * c + C - 1]), ALU.mult)
                        dve.drain()
                        dve.wait_ge(kv_done, n + 1)
                        dve.tensor_tensor(S[:, 1 - c, :, :], S[:, 1 - c, :, :], heads_of(4), ALU.add).then_inc(S_ready, 1)

                def finish(i, s):
                    dve.wait_ge(ors_ready[s], i + 1)
                    dve.wait_ge(z_here[s], 16 * (i + 1))
                    dve.tensor_tensor(o[s][:, :, :], heads_of(O_BANK[s]), col(ors[s][:, :]), ALU.mult)
                    dve.drain()
                    dve.tensor_tensor(o[s][:, :, :], o[s][:, :, :], head(norm_w[:, :]), ALU.mult)
                    dve.drain()
                    dve.tensor_tensor(o[s][:, :, :], o[s][:, :, :], zt[s][:, :, :], ALU.mult).then_inc(o_ready[s], 1)

                def two_tiles(i, last):
                    matrices(i, 0)
                    matrices(i, 1)
                    for s in range(2):
                        dve.wait_ge(y_done[s], L * i + 1)
                        dve.tensor_tensor(X[s][:, :, :], head(ident[:, :]), heads_of(Y_BANK[s]), ALU.subtract)
                        dve.tensor_tensor(Z[s][:, :, :], head(ident[:, :]), tm[s][:, :, :], ALU.subtract)
                        dve.drain()
                        dve.sem_inc(xz_ready[s], 1)
                    for l in range(1, L):
                        for s in range(2):
                            dve.wait_ge(step_done[s], (L - 1) * i + l)
                            if l < L - 1:
                                dve.tensor_tensor(flat(X[s]), flat(X[s]), bank[X_BANK[s]][:, :], ALU.subtract)
                            dve.tensor_tensor(flat(Z[s]), flat(Z[s]), bank[Z_BANK[s]][:, :], ALU.subtract)
                            dve.drain()
                            dve.sem_inc(xz_ready[s], 1)
                    for s in range(2):
                        dve.wait_ge(uw_done[s], i + 1)
                        dve.tensor_copy(flat(u[s]), bank[U_BANK[s]][:, :])
                    dve.drain()
                    scan(i, 0)
                    scan(i, 1)
                    for s in range(2):
                        dve.wait_ge(sq_ready[s], i + 1)
                        dve.tensor_reduce(oss[s][:, :], dec_sq[s][:, :, :], AX, ALU.add).then_inc(oss_ready[s], 1)
                    if not last:
                        begin(i + 1, 0)
                        begin(i + 1, 1)
                    finish(i, 0)
                    finish(i, 1)

                begin(0, 0)
                begin(0, 1)
                run(dve, two_tiles)


def stage_channels_and_delta(nc, io, scr, xnT, ident, half):
    with nc.sbuf_tensor("gT", [P, GCH, TOKP], F32) as gT:
        stage_channels(nc, io, scr, xnT, gT)
        stage_delta_prompt(nc, io, scr, gT, ident, half)
        stage_delta(nc, io, scr, gT, ident, half, True)


def stage_compress_weights(nc, io, wblk, peT, kbias, vbias):
    with Stage(nc, "cw") as st:
        acc_k = st.ps("acc_k")
        acc_v = st.ps("acc_v")
        cleared = st.sem("cleared")
        here = st.sem("here")
        summed = st.sem("summed")
        with nc.Block() as block:

            @block.vector
            def _(dve):
                dve.memset(wblk[:, :, :, :], 0.0).then_inc(cleared, 1)
                dve.wait_ge(summed, 1)
                dve.tensor_copy(kbias[:, :], acc_k[:, 0:1])
                dve.tensor_copy(vbias[:, :], acc_v[:, 0:P])

            @block.sync
            def _(sp):
                sp.wait_ge(cleared, 1)
                for half in range(2):
                    r = slice(HD * half, HD * (half + 1))
                    for c in range(2):
                        sp.dma_start(wblk[r, c, :, r], io["cmp_w"][c].rearrange("j d e -> d j e")).then_inc(here, 16)
                    sp.dma_start(peT[r, :, :], io["cmp_peT"]).then_inc(here, 16)

            @block.tensor
            def _(pe):
                pe.wait_ge(here, 96)
                for j in range(32):
                    pe.matmul(acc_k[:, 0:1], wblk[:, 0, j, :], peT[:, 0, j:j + 1], start=(j == 0), stop=(j == 31))
                for j in range(32):
                    m = pe.matmul(acc_v[:, 0:P], peT[:, 1, j:j + 1].to_broadcast([P, P]), wblk[:, 1, j, :],
                                  start=(j == 0), stop=(j == 31))
                m.then_inc(summed, 1)


def stage_prompt_keys(nc, io, scr, ident, wblk, kbias, vbias, ks, kw, kc, vs, vw, vc):
    with Stage(nc, "pk") as st:
        rows = st.sb("rows", [P, 2, 512])
        wk = st.sb("wk", [P, 2, P])
        cT = st.sb("cT", [P, 2, SEQ])
        turned = [st.ps(f"turned{s}") for s in range(2)]
        acc = [st.ps(f"acc{s}") for s in range(2)]
        here = [st.sem(f"here{s}") for s in range(2)]
        v_here = st.sem("v_here")
        cleared = st.sem("cleared")
        turn_done = st.sem("turn_done")
        taken = st.sem("taken")
        summed = st.sem("summed")
        turns = st.sem("turns")
        with nc.Block() as block:

            @block.sync
            def _(sp):
                def load(t, s):
                    row = ds(t * P, P)
                    sp.dma_start(rows[:, s, :], io["rows"][row, :]).then_inc(here[s], 16)
                    sp.dma_start(wk[:, s, :], io["wrows"][row, 0:P]).then_inc(here[s], 16)

                load(0, 0)
                load(1, 1)
                sp.dma_start(vs[:, :, :], io["rows"][0:SEQ, 384:512].rearrange("(t p) n -> p t n", p=P)).then_inc(v_here, 16)
                sp.dma_start(vw[:, 4:, :], io["wrows"][0:SEQ, 128:256].rearrange("(t p) n -> p t n", p=P)).then_inc(v_here, 16)
                with sp.Fori(0, 3) as i:
                    for s in range(2):
                        wait_turn(sp, turn_done, 2 * i + s + 1, turns)
                        load(2 * i + s + 2, s)
                sp.wait_ge(v_here, 32)

            @block.tensor
            def _(pe):
                with pe.Fori(0, 4) as i:
                    for s in range(2):
                        pe.wait_ge(here[s], 32 * (i + 1))
                        pe.wait_ge(taken, 2 * i + s + 1)
                        pe.transpose(turned[s][:, 0:P], rows[:, s, 0:P], ident[:, :])
                        pe.transpose(turned[s][:, P:2 * P], rows[:, s, P:2 * P], ident[:, :])
                        pe.transpose(turned[s][:, 2 * P:3 * P], rows[:, s, 2 * P:3 * P], ident[:, :])
                        pe.transpose(turned[s][:, 3 * P:4 * P], wk[:, s, :], ident[:, :]).then_inc(turn_done, 1)
                pe.wait_ge(taken, 10)
                for j in range(32):
                    pe.matmul(acc[0][:, 0:63], wblk[:, 0, j, :], cT[:, 0, j:j + 16 * 62 + 1:16], start=(j == 0), stop=(j == 31))
                for j in range(32):
                    m = pe.matmul(acc[1][0:63, 0:P], cT[:, 1, j:j + 16 * 62 + 1:16], wblk[:, 1, j, :], start=(j == 0), stop=(j == 31))
                m.then_inc(summed, 1)

            @block.scalar
            def _(act):
                act.sem_inc(taken, 2)
                with act.Fori(0, 4) as i:
                    for s in range(2):
                        t = 2 * i + s
                        act.wait_ge(turn_done, t + 1)
                        act.activation(cT[:, :, ds(t * P, P)], turned[s][:, 0:2 * P].rearrange("p (a n) -> p a n", a=2), ACT.Copy)
                        act.activation(ks[:, ds(t * P, P)], turned[s][:, 2 * P:3 * P], ACT.Copy)
                        act.activation(kw[:, ds(t * P + WIN, P)], turned[s][:, 3 * P:4 * P], ACT.Copy).then_inc(taken, 1)

            @block.vector
            def _(dve):
                dve.memset(kw[:, 0:WIN], 0.0)
                dve.memset(vw[:, 0:4, :], 0.0)
                dve.memset(kc[:, 63:64], 0.0)
                dve.memset(vc[:, :], 0.0)
                dve.drain()
                dve.wait_ge(summed, 1)
                dve.tensor_scalar(kc[:, 0:63], acc[0][:, 0:63], kbias[:, 0:1], None, ALU.add)
                dve.tensor_tensor(vc[0:63, :], acc[1][0:63, 0:P], vbias[0:63, :], ALU.add)


def stage_nsa_prompt_attend(nc, io, scr, ident, ks, kw, kc, vs, vw, vc):
    with Stage(nc, "pa") as st:
        qz = st.sb("qz", [P, 2, 8, P])
        qT = st.sb("qT", [P, 2, 2, 8, P])
        key_no = st.sb("key_no", [P, SEQ])
        q_no = st.sb("q_no", [P, 8])
        qn = st.sb("qn", [P, 1])
        gates = st.sb("gates", [P, 2, 32])
        bonus = st.sb("bonus", [P, 16])
        ok = st.sb("ok", [P, 64])
        okb = st.sb("okb", [P, 64])
        wbias = st.sb("wbias", [P, 2, 640])
        sc = st.sb("sc", [P, 8, 64])
        mx = st.sb("mx", [P, 8])
        sm = st.sb("sm", [P, 8])
        pg = st.sb("pg", [P, 2, 64])
        pp = st.sb("pp", [P, 2, 68])
        imp = st.sb("imp", [P, 2, 16])
        top = st.sb("top", [P, 2, 8])
        rep = st.sb("rep", [P, 2, 16])
        cm = st.sb("cm", [P, SEQ])
        mk = st.sb("mk", [P, 2, 2, SEQ])
        s_sel = st.sb("s_sel", [P, 2, SEQ])
        s_win = st.sb("s_win", [P, 2, 640])
        hm = st.sb("hm", [P, 8, 2])
        sums = st.sb("sums", [P, 8, 2])
        pT = st.sb("pT", [P, 2, 512])
        pcT = st.sb("pcT", [64, 2, 8, P])
        o = st.sb("o", [P, 2, 8, HD])
        psel = st.ps("psel", [P, 1024])
        pwin = st.ps("pwin", [P, 1024])
        pt = [st.ps(f"pt{k}") for k in range(2)]
        pcmp = st.ps("pcmp")
        po = st.ps("po")

        const_here = st.sem("const_here")
        q_here = st.sem("q_here")
        ok_here = st.sem("ok_here")
        late_here = [st.sem(f"late_here{k}") for k in range(2)]
        front_done = st.sem("front_done")
        turned = st.sem("turned")
        turned_read = st.sem("turned_read")
        cs_done = st.sem("cs_done")
        carg_ready = st.sem("carg_ready")
        cexp_done = st.sem("cexp_done")
        p_ready = st.sem("p_ready")
        qk_done = st.sem("qk_done")
        taken = st.sem("taken")
        exp_done = st.sem("exp_done")
        wexp_done = st.sem("wexp_done")
        t_done = [st.sem(f"t_done{k}") for k in range(2)]
        t_ready = [st.sem(f"t_ready{k}") for k in range(2)]
        t_used = [st.sem(f"t_used{k}") for k in range(2)]
        dve_turns = st.sem("dve_turns")
        pe_turns = st.sem("pe_turns")
        o_taken = st.sem("o_taken")
        block_done = st.sem("block_done")
        o_out = st.sem("o_out")
        turns = st.sem("turns")

        ROUNDS = {False: [("s", 0, 4), ("w", 1, 5)],
                  True: [("s", 0, 4), ("s", 4, 8), ("w", 0, 4), ("w", 4, 5)]}

        def turns_before(n, wide):
            return 2 * n - 32 if wide else n

        def span(h, p, wide):
            return (SEQ, 0) if wide or (h == 0 and p == 0) else (SEQ // 2, P)

        def run(eng, pair):
            with eng.Fori(0, 2) as i:
                pair(i, False, False)
            pair(2, True, False)
            pair(3, True, True)

        def heads(i, wide, last):
            for p in range(2):
                b = 2 * i + p
                for h in range(8):
                    nxt = None
                    if h < 7:
                        nxt = (b, p, h + 1, 8 * b + h + 1)
                    elif not (last and p == 1):
                        nxt = (b + 1, 1 - p, 0, 8 * b + 8)
                    yield b, p, h, 8 * b + h, nxt, not (last and p == 1)

        with nc.Block() as block:

            @block.sync
            def _(sp):
                def load_q(b):
                    for n, name in enumerate(("qc", "qr")):
                        src = scr[name][ds(b * P, P), :].rearrange("p (h d) -> p h d", d=HD)
                        sp.dma_start(qz[:, n, 0:4, 0:HD], src[:, 0:4, :]).then_inc(q_here, 16)
                        sp.dma_start(qz[:, n, 4:8, HD:P], src[:, 4:8, :]).then_inc(q_here, 16)

                def load_ok(b):
                    sp.dma_start(bonus[:, :], io["blk_bonus"][ds(b * P, P), :]).then_inc(ok_here, 16)
                    sp.dma_start(ok[:, :], io["cmp_ok"][ds(b * P, P), :]).then_inc(ok_here, 16)

                def load_late(b, p):
                    sp.dma_start(gates[:, p, :], scr["misc"][ds(b * P, P), :]).then_inc(late_here[p], 16)
                    sp.dma_start(wbias[:, p, :], io["win_bias"][ds(b, 1), :, :].rearrange("a p n -> p (a n)")).then_inc(late_here[p], 16)

                def step(b, p, more, late):
                    if more:
                        wait_turn(sp, cs_done, b + 1, turns)
                        load_q(b + 1)
                        wait_turn(sp, front_done, b + 1, turns)
                        load_ok(b + 1)
                    wait_turn(sp, block_done, b + 1, turns)
                    sp.dma_start(scr["mix"][ds(b * P, P), 0:512], o[:, p, :, :].rearrange("p a b -> p (a b)")).then_inc(o_out, 16)
                    if late:
                        load_late(b + 2, p)

                sp.dma_start(key_no[:, :], io["key_no"]).then_inc(const_here, 16)
                sp.dma_start(q_no[:, :], io["q_no"]).then_inc(const_here, 16)
                load_ok(0)
                load_late(0, 0)
                load_late(1, 1)
                sp.wait_ge(const_here, 33)
                load_q(0)
                with sp.Fori(0, 3) as i:
                    for p in range(2):
                        step(2 * i + p, p, True, True)
                step(6, 0, True, False)
                step(7, 1, False, False)
                sp.wait_ge(o_out, 16 * 10)

            @block.tensor
            def _(pe):
                def scores(b, p, h, wide):
                    q = qT[:, p, 1, h, :]
                    keys, skip = span(h, p, wide)
                    for k in range(0, keys, 512):
                        pe.matmul(psel[:, k:k + 512], q, ks[:, k:k + 512], start=True, stop=True)
                    if skip:
                        m = pe.matmul(pwin[:, 0:512], q, kw[:, ds(b * P + P, 512)], start=True, stop=True)
                    else:
                        pe.matmul(pwin[:, 0:512], q, kw[:, ds(b * P, 512)], start=True, stop=True)
                        m = pe.matmul(pwin[:, 512:640], q, kw[:, ds(b * P + 512, P)], start=True, stop=True)
                    m.then_inc(qk_done, 1)

                def front(f, fp, step):
                    if step < 4:
                        if step == 0:
                            pe.wait_ge(q_here, 64 * (f + 1))
                        wait_turn(pe, turned_read, 6 * f + step + 1, pe_turns)
                        for h in range(4):
                            t = pe.transpose(pcmp[:, h * P:(h + 1) * P], qz[:, step // 2, 4 * (step % 2) + h, :], ident[:, :])
                        t.then_inc(turned, 1)
                    elif step == 4:
                        pe.wait_ge(turned_read, 6 * f + 5)
                        for h in range(8):
                            m = pe.matmul(pcmp[:, h * 64:(h + 1) * 64], qT[:, fp, 0, h, :], kc[:, :], start=True, stop=True)
                        m.then_inc(cs_done, 1)
                    elif step >= 6:
                        if step == 6:
                            wait_turn(pe, p_ready, f + 1, pe_turns)
                        else:
                            wait_turn(pe, turned_read, 6 * f + 6, pe_turns)
                        for h in range(4):
                            t = pe.transpose(pcmp[0:64, h * P:(h + 1) * P], sc[:, 4 * (step - 6) + h, :], ident[:, :])
                        t.then_inc(turned, 1)

                def pair(i, wide, last):
                    for b, p, h, n, nxt, fronts in heads(i, wide, last):
                        before = turns_before(n, wide)

                        def turn(r):
                            what, lo, hi = ROUNDS[wide][r]
                            shift = span(h, p, wide)[1] // P if what == "w" else 0
                            src = (s_sel if what == "s" else s_win)[:, h % 2]
                            for k in range(lo, hi):
                                c = k - shift
                                t = pe.transpose(pt[r % 2][:, (k - lo) * P:(k - lo + 1) * P], src[:, c * P:(c + 1) * P], ident[:, :])
                            t.then_inc(t_done[r % 2], 1)

                        def use(r):
                            what, lo, hi = ROUNDS[wide][r]
                            pe.wait_ge(t_ready[r % 2], before + r // 2 + 1)
                            first, end = (0, 8 if wide else 4) if what == "s" else (0 if wide else 1, 5)
                            for k in range(lo, hi):
                                v, c = (vs[:, k, :], 128) if what == "s" else (vw[:, ds(b + k, 1), :].rearrange("p a n -> p (a n)"), 256)
                                m = pe.matmul(po[:, c:c + P], pT[:, r % 2, (k - lo) * P:(k - lo + 1) * P], v,
                                              start=(k == first), stop=(k == end - 1))
                            m.then_inc(t_used[r % 2], 1)

                        pe.wait_ge(exp_done, n + 1)
                        turn(0)
                        if not wide:
                            pe.wait_ge(wexp_done, n + 1)
                        turn(1)
                        if nxt:
                            scores(*nxt[:3], wide)
                        if h == 0:
                            wait_turn(pe, turned_read, 6 * b + 7, pe_turns)
                        pe.wait_ge(o_taken, n + 1)
                        pe.matmul(po[:, 0:P], pcT[:, p, h, :], vc[:, :], start=True, stop=True)
                        use(0)
                        if wide:
                            pe.wait_ge(wexp_done, n + 1)
                            turn(2)
                        use(1)
                        if fronts:
                            front(b + 1, 1 - p, h)
                        if wide:
                            turn(3)
                            use(2)
                            use(3)

                for step in range(8):
                    front(0, 0, step)
                scores(0, 0, 0, True)
                run(pe, pair)

            @block.scalar
            def _(act):
                def exps(b, p, h, n, wide):
                    keys, skip = span(h, p, wide)
                    act.wait_ge(taken, n + 1)
                    act.activation(s_sel[:, h % 2, 0:keys], s_sel[:, h % 2, 0:keys], ACT.Exp, bias=hm[:, h, 0:1],
                                   accum_out=sums[:, h, 0:1]).then_inc(exp_done, 1)
                    act.activation(s_win[:, h % 2, 0:640 - skip], s_win[:, h % 2, 0:640 - skip], ACT.Exp, bias=hm[:, h, 1:2],
                                   accum_out=sums[:, h, 1:2]).then_inc(wexp_done, 1)

                def front(f, fp, step):
                    if step == 5:
                        act.wait_ge(carg_ready, f + 1)
                        act.activation(sc[:, :, :], sc[:, :, :], ACT.Exp).then_inc(cexp_done, 1)
                    elif step < 4:
                        act.wait_ge(turned, 6 * f + step + 1)
                        k = 4 * (step % 2)
                        act.activation(qT[:, fp, step // 2, k:k + 4].rearrange("p a b -> p (a b)"), pcmp[:, :], ACT.Copy,
                                       scale=HD ** -0.5).then_inc(turned_read, 1)
                    elif step >= 6:
                        act.wait_ge(turned, 6 * f + step - 1)
                        k = 4 * (step - 6)
                        act.activation(pcT[:, fp, k:k + 4, :].rearrange("p a b -> p (a b)"), pcmp[0:64, :], ACT.Copy).then_inc(turned_read, 1)

                def pair(i, wide, last):
                    for b, p, h, n, nxt, fronts in heads(i, wide, last):
                        before = turns_before(n, wide)
                        for r in (0, 2) if wide else (0,):
                            act.wait_ge(t_done[0], before + r // 2 + 1)
                            act.wait_ge(t_used[0], before + r // 2 + 1)
                            act.activation(pT[:, 0, :], pt[0][:, :], ACT.Copy).then_inc(t_ready[0], 1)
                            if r == 0 and fronts and h == 5:
                                front(b + 1, 1 - p, h)
                        if nxt:
                            exps(*nxt, wide)
                        if fronts and h != 5:
                            front(b + 1, 1 - p, h)

                act.sem_inc(turned_read, 1)
                for step in range(8):
                    front(0, 0, step)
                exps(0, 0, 0, 0, True)
                run(act, pair)

            @block.vector
            def _(dve):
                h8 = lambda ap: ap.unsqueeze(1).to_broadcast([P, 8, 64])
                c8 = lambda ap: ap.unsqueeze(2).to_broadcast([P, 8, 64])

                def take(b, p, h, n, wide):
                    keys, skip = span(h, p, wide)
                    if h == 0:
                        wait_turn(dve, late_here[p], 16 * (b - p) + 32, dve_turns)
                    wait_turn(dve, qk_done, n + 1, dve_turns)
                    dve.tensor_tensor_reduce(s_sel[:, h % 2, 0:keys], psel[:, 0:keys], mk[:, p, h // 4, 0:keys], 1.0, NEG, ALU.add,
                                             ALU.max, hm[:, h, 0:1])
                    dve.tensor_tensor_reduce(s_win[:, h % 2, 0:640 - skip], pwin[:, 0:640 - skip], wbias[:, p, skip:640], 1.0, NEG,
                                             ALU.add, ALU.max, hm[:, h, 1:2])
                    dve.drain()
                    dve.tensor_scalar(hm[:, h, :], hm[:, h, :], -1.0, None, ALU.mult).then_inc(taken, 1)

                def front(f, fp, step):
                    if step == 3:
                        dve.wait_ge(ok_here, 32 * (f + 1))
                        dve.tensor_scalar(okb[:, :], ok[:, :], 1.0, -NEG, ALU.subtract, ALU.mult)
                        dve.tensor_copy(qn[:, :], q_no[:, ds(f, 1)])
                        dve.drain()
                        dve.tensor_scalar(cm[:, :], key_no[:, :], qn[:, 0:1], NEG, ALU.is_gt, ALU.mult)
                    elif step == 4:
                        dve.wait_ge(cs_done, f + 1)
                        dve.tensor_tensor(sc[:, :, :], pcmp[:, :].rearrange("p (a b) -> p a b", a=8), h8(okb[:, :]), ALU.add)
                        dve.drain()
                        dve.tensor_reduce(mx[:, :], sc[:, :, :], AX, ALU.max)
                        dve.drain()
                        dve.tensor_tensor(sc[:, :, :], sc[:, :, :], c8(mx[:, :]), ALU.subtract).then_inc(carg_ready, 1)
                    elif step == 5:
                        dve.wait_ge(cexp_done, f + 1)
                        dve.tensor_tensor(sc[:, :, :], sc[:, :, :], h8(ok[:, :]), ALU.mult)
                        dve.drain()
                        dve.tensor_reduce(sm[:, :], sc[:, :, :], AX, ALU.add)
                        dve.drain()
                        dve.tensor_scalar(sm[:, :], sm[:, :], 1e-30, None, ALU.max)
                        dve.drain()
                        dve.reciprocal(sm[:, :], sm[:, :])
                        dve.drain()
                        dve.tensor_tensor(sc[:, :, :], sc[:, :, :], c8(sm[:, :]), ALU.mult).then_inc(p_ready, 1)
                        dve.drain()
                        p4 = sc[:, :, :].rearrange("p (k g) n -> p k g n", k=2)
                        dve.tensor_tensor(pg[:, :, :], p4[:, :, 0, :], p4[:, :, 1, :], ALU.add)
                        dve.drain()
                        dve.tensor_tensor(pg[:, :, :], pg[:, :, :], p4[:, :, 2, :], ALU.add)
                        dve.drain()
                        dve.tensor_tensor(pp[:, :, 1:65], pg[:, :, :], p4[:, :, 3, :], ALU.add)
                        dve.drain()
                    elif step == 6:
                        at = lambda k: pp[:, :, k:k + 61:4]
                        dve.tensor_tensor(imp[:, :, :], at(0), at(1), ALU.add)
                        for k in (2, 3, 4):
                            dve.drain()
                            dve.tensor_tensor(imp[:, :, :], imp[:, :, :], at(k), ALU.add)
                        dve.drain()
                        dve.tensor_tensor(imp[:, :, :], imp[:, :, :], bonus[:, :].unsqueeze(1).to_broadcast([P, 2, 16]), ALU.add)
                        dve.drain()
                        for k in range(2):
                            dve.max(top[:, k, :], imp[:, k, :])
                        dve.drain()
                        for k in range(2):
                            dve.match_replace(rep[:, k, :], top[:, k, :], imp[:, k, :], 3 * NEG)
                        dve.drain()
                        dve.tensor_scalar(rep[:, :, :], rep[:, :, :], 3 * NEG, NEG, ALU.not_equal, ALU.mult)
                        dve.drain()
                        for k in range(2):
                            dve.tensor_tensor(mk[:, fp, k, :].rearrange("p (s n) -> p s n", n=64), cm[:, :].rearrange("p (s n) -> p s n", n=64),
                                              rep[:, k, :].unsqueeze(2).to_broadcast([P, 16, 64]), ALU.add)
                        dve.drain()
                        dve.sem_inc(front_done, 1)

                def pair(i, wide, last):
                    for b, p, h, n, nxt, fronts in heads(i, wide, last):
                        before = turns_before(n, wide)
                        for r in (1, 3) if wide else (1,):
                            w = P if r == 3 else 512
                            if r == 3 and nxt:
                                take(*nxt, wide)
                            dve.wait_ge(t_done[1], before + r // 2 + 1)
                            dve.wait_ge(t_used[1], before + r // 2 + 1)
                            dve.tensor_copy(pT[:, 1, 0:w], pt[1][:, 0:w]).then_inc(t_ready[1], 1)
                        if not wide:
                            take(*nxt, wide)
                        dve.wait_ge(t_used[1], before + (3 if wide else 2))
                        if h == 0:
                            wait_turn(dve, o_out, 16 * b + 16, dve_turns)
                        c = HD * (h // 4)
                        dve.tensor_scalar(sums[:, h, :], sums[:, h, :], 1e-30, None, ALU.max)
                        dve.tensor_scalar(o[:, p, h, :], po[:, c:c + HD], gates[:, p, 3 * h:3 * h + 1], None, ALU.mult)
                        dve.drain()
                        dve.reciprocal(sums[:, h, :], sums[:, h, :])
                        dve.drain()
                        dve.tensor_tensor(sums[:, h, :], sums[:, h, :], gates[:, p, 3 * h + 1:3 * h + 3], ALU.mult)
                        dve.drain()
                        dve.scalar_tensor_tensor(o[:, p, h, :], po[:, P + c:P + c + HD], sums[:, h, 0:1], o[:, p, h, :], ALU.mult, ALU.add)
                        dve.drain()
                        dve.scalar_tensor_tensor(o[:, p, h, :], po[:, 2 * P + c:2 * P + c + HD], sums[:, h, 1:2], o[:, p, h, :],
                                                 ALU.mult, ALU.add).then_inc(o_taken, 1)
                        if fronts:
                            front(b + 1, 1 - p, h)
                        if h == 7:
                            dve.drain()
                            dve.sem_inc(block_done, 1)

                dve.memset(qz[:, :, :, :], 0.0)
                dve.memset(pp[:, :, :], 0.0)
                dve.drain()
                dve.sem_inc(const_here, 1)
                dve.sem_inc(o_taken, 1)
                dve.sem_inc(o_out, 32)
                dve.sem_inc(t_used[0], 1)
                dve.sem_inc(t_used[1], 1)
                dve.wait_ge(const_here, 33)
                for step in range(8):
                    front(0, 0, step)
                take(0, 0, 0, 0, True)
                run(dve, pair)


def stage_nsa_prompt(nc, io, scr, ident, wblk, kbias, vbias):
    with ExitStack() as ctx:
        def sb(name, shape):
            return ctx.enter_context(nc.sbuf_tensor(name, shape, F32))

        ks, kw, kc = sb("ks", [P, SEQ]), sb("kw", [P, SEQ + WIN]), sb("kc", [P, 64])
        vs, vw, vc = sb("vs", [P, 8, P]), sb("vw", [P, 12, P]), sb("vc", [64, P])
        stage_prompt_keys(nc, io, scr, ident, wblk, kbias, vbias, ks, kw, kc, vs, vw, vc)
        stage_nsa_prompt_attend(nc, io, scr, ident, ks, kw, kc, vs, vw, vc)


def stage_nsa(nc, io, scr, ident, half):
    with ExitStack() as ctx:
        def sb(name, shape):
            return ctx.enter_context(nc.sbuf_tensor(name, shape, F32))

        wblk, peT = sb("wblk", [P, 2, 32, P]), sb("peT", [P, 2, 32])
        kbias, vbias = sb("kbias", [P, 1]), sb("vbias", [P, P])
        stage_compress_weights(nc, io, wblk, peT, kbias, vbias)
        stage_nsa_prompt(nc, io, scr, ident, wblk, kbias, vbias)
        stage_nsa_sample_attend(nc, io, scr, ident, wblk, kbias, vbias)


def stage_nsa_sample_attend(nc, io, scr, ident, wblk, kbias, vbias):
    G = 4
    NG = NPAGE // G
    with Stage(nc, "ns") as st:
        pages = st.sb("pages", [1, NB * NPAGE], I32)
        pg = st.sb("pg", [P, 2, G, 512])
        cT = st.sb("cT", [P, 2, PAST])
        ksT = st.sb("ksT", [P, 2, 512])
        vs2 = st.sb("vs2", [P, 2, NPAGE, P])
        ssel = st.sb("ssel", [P, PAST + NT])
        kcmp = st.sb("kcmp", [P, 256])
        vcmp = st.sb("vcmp", [P, 2, 2, P])
        win = st.sb("win", [P, 2, 4, 256])
        new = st.sb("new", [NT, 2, 4, P])
        kwT = st.sb("kwT", [P, WIN])
        knT = st.sb("knT", [P, 2 * NT])
        qz = st.sb("qz", [P, 2, P])
        qT = st.sb("qT", [P, 2, P])
        gates = st.sb("gates", [P, 4, 3])
        gate = st.sb("gate", [P, 3])
        gsum = st.sb("gsum", [P, P])
        bonus = st.sb("bonus", [P, 65])
        newb = st.sb("newb", [P, NT])
        winb = st.sb("winb", [P, WIN + NT])
        pc = st.sb("pc", [P, 256])
        swin = st.sb("swin", [P, WIN + NT])
        pp = st.sb("pp", [P, 264])
        imp = st.sb("imp", [P, 65])
        top = st.sb("top", [P, 8])
        rep = st.sb("rep", [P, 65])
        mx = st.sb("mx", [P, 8])
        sums = st.sb("sums", [P, 3])
        pT = st.sb("pT", [P, 2, 512])
        o = st.sb("o", [P, HD])
        bank = [st.ps(f"b{k}") for k in range(8)]

        const_here = st.sem("const_here")
        copied = st.sem("copied")
        q_here = st.sem("q_here")
        gates_here = st.sem("gates_here")
        turns_dve = st.sem("turns_dve")
        win_here = st.sem("win_here")
        here = [st.sem(f"here{s}") for s in range(2)]
        t_done = [st.sem(f"t_done{s}") for s in range(2)]
        v_kept = [st.sem(f"v_kept{s}") for s in range(2)]
        c_kept = [st.sem(f"c_kept{s}") for s in range(2)]
        ks_ready = [st.sem(f"ks_ready{s}") for s in range(2)]
        sc_done = [st.sem(f"sc_done{s}") for s in range(2)]
        sc_kept = [st.sem(f"sc_kept{s}") for s in range(2)]
        qt_done = st.sem("qt_done")
        q_ready = st.sem("q_ready")
        cmp_done = st.sem("cmp_done")
        cmp_ready = st.sem("cmp_ready")
        cs_done = st.sem("cs_done")
        wt_done = st.sem("wt_done")
        wt_ready = st.sem("wt_ready")
        ws_done = st.sem("ws_done")
        batch_kept = st.sem("batch_kept")
        carg_ready = st.sem("carg_ready")
        cexp_done = st.sem("cexp_done")
        p_ready = st.sem("p_ready")
        imp_done = st.sem("imp_done")
        arg_ready = st.sem("arg_ready")
        exp_done = st.sem("exp_done")
        r_done = st.sem("r_done")
        r_ready = [st.sem(f"r_ready{s}") for s in range(2)]
        pv_done = st.sem("pv_done")
        o_ready = st.sem("o_ready")
        o_out = st.sem("o_out")
        turns = st.sem("turns")
        pe_turns = st.sem("pe_turns")
        turns_pool = st.sem("turns_pool")
        imp_kept = st.sem("imp_kept")
        banks_read = st.sem("banks_read")
        NR = 11
        ROUNDS = [("c", 0, 2)] + [("s", 4 * k, 4) for k in range(8)] + [("w", 0, 4), ("n", 0, 2)]

        with nc.Block() as block:

            @block.sync
            def _(sp):
                for dst, name in ((gsum, "gsum"), (bonus, "samp_bonus"), (newb, "samp_new"), (winb, "samp_win"), (pages, "pages")):
                    sp.dma_start(dst[:, :], io[name]).then_inc(const_here, 16)
                for b in range(NB):
                    sp.dma_start(io["win_s"][b, 0:WIN - NT, :], io["cache_win"][b, NT:WIN, :]).then_inc(copied, 16)
                    sp.dma_start(io["win_s"][b, WIN - NT:WIN, :], io["wrows"][SEQ + b * NT:SEQ + (b + 1) * NT, :]).then_inc(copied, 16)
                sp.wait_ge(const_here, 81)

                def tokens(bp, b2):
                    return ds(bp * 2 * NT + (SEQ + b2 * NT), NT)

                def load_q(bp):
                    for b2 in range(2):
                        for kv in range(2):
                            r = slice(64 * b2 + 32 * kv, 64 * b2 + 32 * kv + 32)
                            for n, name in enumerate(("qc", "qr")):
                                src = scr[name][tokens(bp, b2), 256 * kv:256 * (kv + 1)].rearrange("t (g d) -> g t d", g=4)
                                sp.dma_start(qz[r, n, HD * kv:HD * (kv + 1)], src).then_inc(q_here, 16)

                def load_win(bp):
                    for b2 in range(2):
                        sp.dma_start(win[:, b2, :, :], io["cache_win"][ds(bp * 2 + b2, 1), :, :]
                                     .rearrange("a (t p) n -> p (a t) n", p=P)).then_inc(win_here, 16)
                        sp.dma_start(new[:, b2, 0:2, :], io["rows"][tokens(bp, b2), 256:512].rearrange("p (a n) -> p a n", a=2)).then_inc(win_here, 16)
                        sp.dma_start(new[:, b2, 2:4, :], io["wrows"][tokens(bp, b2), :].rearrange("p (a n) -> p a n", a=2)).then_inc(win_here, 16)

                def load_pages(bp, b2, i):
                    for s in range(2):
                        n = bp * NG + (i + b2 * (NG // 2))
                        wait_turn(sp, t_done[s], n + 1, turns)
                        wait_turn(sp, v_kept[s], n + 1, turns)
                        for k in range(G):
                            at = bp * 2 * NPAGE + (i * 2 * G + (b2 * NPAGE + s * G + k))
                            page = sp.value_load(pages[0:1, ds(at, 1)], min_val=0, max_val=POOL - 1)
                            sp.dma_start(pg[:, s, k, :], io["cache_kv"][ds(page, 1), :, :]
                                         .rearrange("a p n -> p (a n)")).then_inc(here[s], 16)

                def pair(bp, last):
                    with sp.Fori(1, NG // 2) as i:
                        load_pages(bp, 0, i)
                    if not last:
                        wait_turn(sp, qt_done, bp + 1, turns)
                        load_q(bp + 1)
                    with sp.Fori(0, NG // 2) as i:
                        load_pages(bp, 1, i)
                    if not last:
                        load_pages(bp + 1, 0, 0)
                    wait_turn(sp, o_ready, bp + 1, turns)
                    for b2 in range(2):
                        for kv in range(2):
                            r = slice(64 * b2 + 32 * kv, 64 * b2 + 32 * kv + 32)
                            sp.dma_start(scr["mix"][tokens(bp, b2), 256 * kv:256 * (kv + 1)].rearrange("t (g d) -> g t d", g=4), o[r, :]).then_inc(o_out, 16)
                    if not last:
                        load_win(bp + 1)

                load_q(0)
                load_pages(0, 0, 0)
                load_win(0)
                for b in range(NB):
                    for h in range(8):
                        r = slice(64 * (b % 2) + 8 * h, 64 * (b % 2) + 8 * h + 8)
                        sp.dma_start(gates[r, b // 2, :], scr["misc"][SEQ + b * NT:SEQ + (b + 1) * NT, 3 * h:3 * h + 3]).then_inc(gates_here, 16)
                with sp.Fori(0, 3) as bp:
                    pair(bp, False)
                pair(3, True)
                sp.wait_ge(o_out, 64 * 5)
                sp.wait_ge(copied, 256)

            @block.gpsimd
            def _(pool):
                def pair(bp, later):
                    if later:
                        wait_turn(pool, o_ready, bp, turns_pool)
                    for b2 in range(2):
                        with pool.Fori(0, NG // 2) as i:
                            for s in range(2):
                                n = bp * NG + (i + b2 * (NG // 2))
                                wait_turn(pool, here[s], n * 64 + 64, turns_pool)
                                pool.tensor_copy(vs2[:, b2, ds(i * 2 * G + s * G, G), :], pg[:, s, :, 384:512]).then_inc(v_kept[s], 1)

                pair(0, False)
                with pool.Fori(1, 4) as bp:
                    pair(bp, True)

            @block.scalar
            def _(act):
                with act.Fori(0, 4) as bp:
                    act.wait_ge(qt_done, bp + 1)
                    act.activation(qT[:, :, :].rearrange("p a b -> p (a b)"), bank[0][:, 0:256], ACT.Copy, scale=HD ** -0.5).then_inc(q_ready, 1)
                    for b2 in range(2):
                        m = bp * 2 + b2
                        act.wait_ge(cmp_done, m + 1)
                        with act.Fori(0, NG // 2) as i:
                            for s in range(2):
                                n = bp * NG + (i + b2 * (NG // 2))
                                act.wait_ge(t_done[s], n + 2)
                                for c in range(2):
                                    a = act.activation(cT[:, c, ds(i * 1024 + 512 * s, 512)], bank[4 * s + c][:, :], ACT.Copy)
                                a.then_inc(c_kept[s], 1)
                        act.wait_ge(wt_done, m + 1)
                        act.activation(kwT[:, :], bank[4][:, :], ACT.Copy)
                        act.activation(knT[:, :], bank[5][:, 0:2 * NT], ACT.Copy).then_inc(wt_ready, 1)
                    act.wait_ge(carg_ready, bp + 1)
                    act.activation(pc[:, 0:255], pc[:, 0:255], ACT.Exp, bias=mx[:, 0:1], accum_out=sums[:, 0:1]).then_inc(cexp_done, 1)
                    act.wait_ge(arg_ready, bp * 2 + 1)
                    act.activation(swin[:, :], swin[:, :], ACT.Exp, bias=mx[:, 2:3], accum_out=sums[:, 2:3])
                    act.wait_ge(arg_ready, bp * 2 + 2)
                    act.activation(ssel[:, :], ssel[:, :], ACT.Exp, bias=mx[:, 1:2], accum_out=sums[:, 1:2]).then_inc(exp_done, 1)
                    for r in range(1, NR, 2):
                        act.wait_ge(r_done, bp * NR + r + 1)
                        if r >= 2:
                            act.wait_ge(pv_done, bp * NR + r - 1)
                        act.activation(pT[:, 1, :], bank[1][:, :], ACT.Copy).then_inc(r_ready[1], 1)

            @block.tensor
            def _(pe):
                pe.wait_ge(const_here, 81)
                with pe.Fori(0, 4) as bp:
                    pe.wait_ge(q_here, 128 * (bp + 1))
                    pe.transpose(bank[0][:, 0:P], qz[:, 0, :], ident[:, :])
                    pe.transpose(bank[0][:, P:2 * P], qz[:, 1, :], ident[:, :]).then_inc(qt_done, 1)
                    wait_turn(pe, q_ready, bp + 1, pe_turns)
                    wait_turn(pe, banks_read, bp + 1, pe_turns)
                    for b2 in range(2):
                        m = bp * 2 + b2
                        rows = slice(64 * b2, 64 * b2 + 64)
                        with pe.Fori(0, NG // 2) as i:
                            n = bp * NG + (i + b2 * (NG // 2))
                            for s in range(2):
                                wait_turn(pe, here[s], n * 64 + 64, pe_turns)
                                pe.wait_ge(c_kept[s], n + 1)
                                pe.wait_ge(ks_ready[s], n + 1)
                                for c in range(3):
                                    for k in range(G):
                                        t = pe.transpose(bank[4 * s + c][:, k * P:(k + 1) * P], pg[:, s, k, c * P:(c + 1) * P], ident[:, :])
                                t.then_inc(t_done[s], 1)
                            for s in range(2):
                                pe.wait_ge(ks_ready[s], n + 2)
                                pe.wait_ge(sc_kept[s], n + 1)
                                pe.matmul(bank[4 * s + 3][rows, :], qT[:, 1, rows], ksT[:, s, :], start=True, stop=True).then_inc(sc_done[s], 1)
                        done = bp * NG + (b2 + 1) * (NG // 2) + 1
                        pe.wait_ge(c_kept[0], done)
                        pe.wait_ge(c_kept[1], done)
                        pe.wait_ge(ks_ready[0], done)
                        pe.wait_ge(ks_ready[1], done)
                        for j in range(32):
                            pe.matmul(bank[0][:, 0:255], wblk[:, 0, j, :], cT[:, 0, j:j + 16 * 254 + 1:16], start=(j == 0), stop=(j == 31))
                        for part, w in ((0, 128), (1, 127)):
                            for j in range(32):
                                a = 2048 * part + j
                                x = pe.matmul(bank[1][0:w, part * P:(part + 1) * P], cT[:, 1, a:a + 16 * (w - 1) + 1:16], wblk[:, 1, j, :],
                                              start=(j == 0), stop=(j == 31))
                        x.then_inc(cmp_done, 1)
                        wait_turn(pe, win_here, 96 * (bp + 1), pe_turns)
                        for k in range(4):
                            pe.transpose(bank[4][:, k * P:(k + 1) * P], win[:, b2, k, 0:P], ident[:, :])
                        pe.transpose(bank[5][:, 0:NT], new[:, b2, 2, :], ident[0:NT, 0:NT])
                        pe.transpose(bank[5][:, NT:2 * NT], new[:, b2, 0, :], ident[0:NT, 0:NT]).then_inc(wt_done, 1)
                        pe.wait_ge(cmp_ready, m + 1)
                        pe.matmul(bank[2][rows, 0:256], qT[:, 0, rows], kcmp[:, :], start=True, stop=True)
                        pe.wait_ge(wt_ready, m + 1)
                        pe.matmul(bank[6][rows, :], qT[:, 1, rows], kwT[:, :], start=True, stop=True)
                        pe.matmul(bank[5][rows, 0:2 * NT], qT[:, 1, rows], knT[:, :], start=True, stop=True).then_inc(ws_done, 1)
                        wait_turn(pe, batch_kept, m + 1, pe_turns)
                    wait_turn(pe, p_ready, bp + 1, pe_turns)
                    pe.matmul(bank[0][:, 0:255], gsum[:, :], pc[:, 0:255], start=True, stop=True).then_inc(imp_done, 1)
                    pe.wait_ge(imp_kept, bp + 1)

                    def turn(r):
                        what, at, k = ROUNDS[r]
                        src = {"c": pc, "s": ssel, "w": swin, "n": None}[what]
                        if what == "n":
                            pe.transpose(bank[r % 2][0:NT, 0:P], ssel[:, PAST:PAST + NT], ident[:, :])
                            t = pe.transpose(bank[r % 2][0:NT, P:2 * P], swin[:, WIN:WIN + NT], ident[:, :])
                        else:
                            for x in range(k):
                                t = pe.transpose(bank[r % 2][:, x * P:(x + 1) * P], src[:, (at + x) * P:(at + x + 1) * P], ident[:, :])
                        t.then_inc(r_done, 1)

                    def use(r):
                        what, at, k = ROUNDS[r]
                        pe.wait_ge(r_ready[r % 2], bp * (6 - r % 2) + r // 2 + 1)
                        for b2 in range(2):
                            rows = slice(64 * b2, 64 * b2 + 64)
                            for x in range(k):
                                p = pT[:, r % 2, x * P + 64 * b2:x * P + 64 * b2 + 64]
                                if what == "c":
                                    mm = pe.matmul(bank[2][rows, 0:P], p, vcmp[:, b2, x, :], start=(x == 0), stop=(x == 1))
                                elif what == "s":
                                    mm = pe.matmul(bank[3][rows, 0:P], p, vs2[:, b2, at + x, :], start=(at + x == 0), stop=False, skip_group_check=True)
                                elif what == "w":
                                    mm = pe.matmul(bank[4][rows, 0:P], p, win[:, b2, x, P:2 * P], start=(x == 0), stop=False, skip_group_check=True)
                                else:
                                    pn = pT[0:NT, r % 2, x * P + 64 * b2:x * P + 64 * b2 + 64]
                                    mm = pe.matmul(bank[3 + x][rows, 0:P], pn, new[:, b2, 1 + 2 * x, :], start=False, stop=True, skip_group_check=True)
                        mm.then_inc(pv_done, 1)

                    turn(0)
                    pe.wait_ge(exp_done, bp + 1)
                    for s in range(2):
                        pe.wait_ge(v_kept[s], bp * NG + NG + 1)
                    for r in range(1, NR):
                        if r >= 2:
                            pe.wait_ge(r_ready[r % 2], bp * (6 - r % 2) + r // 2)
                        turn(r)
                        use(r - 1)
                    use(NR - 1)

            @block.vector
            def _(dve):
                dve.memset(qz[:, :, :], 0.0)
                dve.memset(pp[:, :], 0.0)
                dve.memset(pc[:, :], 0.0)
                dve.memset(kcmp[:, :], 0.0)
                dve.memset(vcmp[:, :, :, :], 0.0)
                dve.memset(imp[:, :], 0.0)
                dve.drain()
                dve.sem_inc(const_here, 1)
                for s in [cmp_done, banks_read] + t_done + v_kept + c_kept + ks_ready + sc_kept:
                    dve.sem_inc(s, 1)
                dve.sem_inc(o_out, 64)
                dve.wait_ge(const_here, 81)
                dve.wait_ge(gates_here, 1024)
                with dve.Fori(0, 4) as bp:
                    for b2 in range(2):
                        m = bp * 2 + b2
                        rows = slice(64 * b2, 64 * b2 + 64)
                        with dve.Fori(0, NG // 2) as i:
                            n = bp * NG + (i + b2 * (NG // 2))
                            for s in range(2):
                                dve.wait_ge(t_done[s], n + 2)
                                dve.tensor_copy(ksT[:, s, :], bank[4 * s + 2][:, :]).then_inc(ks_ready[s], 1)
                            for s in range(2):
                                dve.wait_ge(sc_done[s], n + 1)
                                dve.tensor_copy(ssel[rows, ds(i * 1024 + 512 * s, 512)], bank[4 * s + 3][rows, :]).then_inc(sc_kept[s], 1)
                        dve.wait_ge(cmp_done, m + 2)
                        dve.tensor_scalar(kcmp[:, 0:255], bank[0][:, 0:255], kbias[:, 0:1], None, ALU.add).then_inc(cmp_ready, 1)
                        dve.tensor_tensor(vcmp[:, b2, 0, :], bank[1][:, 0:P], vbias[:, :], ALU.add)
                        dve.tensor_tensor(vcmp[0:127, b2, 1, :], bank[1][0:127, P:2 * P], vbias[0:127, :], ALU.add)
                        dve.wait_ge(ws_done, m + 1)
                        dve.tensor_copy(pc[rows, 0:255], bank[2][rows, 0:255])
                        dve.tensor_tensor(swin[rows, 0:WIN], bank[6][rows, :], winb[rows, 0:WIN], ALU.add)
                        dve.tensor_tensor(swin[rows, WIN:], bank[5][rows, 0:NT], winb[rows, WIN:], ALU.add)
                        dve.tensor_tensor(ssel[rows, PAST:], bank[5][rows, NT:2 * NT], newb[rows, :], ALU.add)
                        dve.drain()
                        dve.sem_inc(batch_kept, 1)
                    dve.tensor_reduce(mx[:, 0:1], pc[:, 0:255], AX, ALU.max)
                    dve.drain()
                    dve.tensor_scalar(mx[:, 0:1], mx[:, 0:1], -1.0, None, ALU.mult).then_inc(carg_ready, 1)
                    dve.tensor_reduce(mx[:, 2:3], swin[:, :], AX, ALU.max)
                    dve.drain()
                    dve.tensor_scalar(mx[:, 2:3], mx[:, 2:3], -1.0, None, ALU.mult).then_inc(arg_ready, 1)
                    dve.wait_ge(cexp_done, bp + 1)
                    dve.tensor_scalar(sums[:, 0:1], sums[:, 0:1], 1e-30, None, ALU.max)
                    dve.drain()
                    dve.reciprocal(sums[:, 0:1], sums[:, 0:1])
                    dve.drain()
                    dve.tensor_scalar(pc[:, 0:255], pc[:, 0:255], sums[:, 0:1], None, ALU.mult).then_inc(p_ready, 1)
                    dve.wait_ge(imp_done, bp + 1)
                    dve.tensor_copy(pp[:, 1:256], bank[0][:, 0:255]).then_inc(imp_kept, 1)
                    dve.drain()
                    at = lambda k: pp[:, k:k + 253:4]
                    dve.tensor_tensor(imp[:, 0:64], at(0), at(1), ALU.add)
                    for k in (2, 3, 4):
                        dve.drain()
                        dve.tensor_tensor(imp[:, 0:64], imp[:, 0:64], at(k), ALU.add)
                    dve.drain()
                    dve.tensor_tensor(rep[:, :], imp[:, :], bonus[:, :], ALU.add)
                    dve.drain()
                    dve.max(top[:, :], rep[:, :])
                    dve.drain()
                    dve.match_replace(rep[:, :], top[:, :], rep[:, :], 3 * NEG)
                    dve.drain()
                    dve.tensor_scalar(rep[:, :], rep[:, :], 3 * NEG, None, ALU.not_equal)
                    dve.drain()
                    dve.tensor_scalar(rep[:, :], rep[:, :], NEG, None, ALU.mult)
                    dve.drain()
                    s3 = ssel[:, 0:PAST].rearrange("p (s n) -> p s n", n=64)
                    dve.tensor_tensor(s3, s3, rep[:, 0:64].unsqueeze(2).to_broadcast([P, 64, 64]), ALU.add)
                    dve.drain()
                    dve.tensor_reduce(mx[:, 1:2], ssel[:, :], AX, ALU.max)
                    dve.drain()
                    dve.tensor_scalar(mx[:, 1:2], mx[:, 1:2], -1.0, None, ALU.mult).then_inc(arg_ready, 1)
                    for r in range(0, NR, 2):
                        dve.wait_ge(r_done, bp * NR + r + 1)
                        if r >= 2:
                            dve.wait_ge(pv_done, bp * NR + r - 1)
                        what, a, k = ROUNDS[r]
                        if what == "n":
                            dve.tensor_copy(pT[0:NT, 0, 0:2 * P], bank[0][0:NT, 0:2 * P]).then_inc(r_ready[0], 1)
                        else:
                            dve.tensor_copy(pT[:, 0, 0:k * P], bank[0][:, 0:k * P]).then_inc(r_ready[0], 1)
                    dve.wait_ge(exp_done, bp + 1)
                    dve.tensor_scalar(sums[:, 1:3], sums[:, 1:3], 1e-30, None, ALU.max)
                    dve.drain()
                    dve.reciprocal(sums[:, 1:3], sums[:, 1:3])
                    dve.drain()
                    dve.tensor_copy(gate[:, :], gates[:, ds(bp, 1), :].rearrange("p a n -> p (a n)"))
                    dve.drain()
                    dve.tensor_tensor(sums[:, 1:3], sums[:, 1:3], gate[:, 1:3], ALU.mult)
                    dve.drain()
                    dve.wait_ge(pv_done, bp * NR + NR)
                    wait_turn(dve, o_out, 64 * (bp + 1), turns_dve)
                    for k, (b, coef) in enumerate(((2, gate), (3, sums), (4, sums))):
                        for q in range(4):
                            r = slice(32 * q, 32 * q + 32)
                            src = bank[b][r, HD * (q % 2):HD * (q % 2) + HD]
                            if k == 0:
                                dve.tensor_scalar(o[r, :], src, coef[r, 0:1], None, ALU.mult)
                            else:
                                dve.scalar_tensor_tensor(o[r, :], src, coef[r, k:k + 1], o[r, :], ALU.mult, ALU.add)
                        dve.drain()
                    dve.sem_inc(o_ready, 1)
                    dve.sem_inc(banks_read, 1)


def stage_mem(nc, io, scr, ident, half):
    with Stage(nc, "mem") as st:
        w = st.sb("w", [P, KD, 2048])
        norm_w = st.sb("norm_w", [P, D])
        k_w = st.sb("k_w", [P, XD])
        x = st.sb("x", [P, D])
        sq = st.sb("sq", [P, D])
        ss = st.sb("ss", [P, 1])
        rstd = st.sb("rstd", [P, 1])
        xn = st.sb("xn", [P, D])
        xT = st.sb("xT", [P, KD, P])
        kv = st.sb("kv", [P, 2048])
        hs = st.sb("hs", [P, XH])
        rs = st.sb("rs", [P, XH])
        turned = st.ps("turned", [P, 1024])
        acc = st.ps("acc", [P, 2048])
        w_here = st.sem("w_here")
        x_here = st.sem("x_here")
        squares = st.sem("squares")
        rstd_ready = st.sem("rstd_ready")
        xn_ready = st.sem("xn_ready")
        turn_done = st.sem("turn_done")
        xT_ready = st.sem("xT_ready")
        projected = st.sem("projected")
        kv_copied = st.sem("kv_copied")
        hs_ready = st.sem("hs_ready")
        rs_ready = st.sem("rs_ready")
        k_ready = st.sem("k_ready")
        out = st.sem("out")

        with nc.Block() as block:

            @block.sync
            def _(sp):
                sp.dma_start(x[:, :], io["mem"][0:P, :]).then_inc(x_here, 16)
                sp.dma_start(norm_w[:, :], io["mem_norm_w"].partition_broadcast(P)).then_inc(x_here, 16)
                for n, name in enumerate(("w_xk", "w_xv")):
                    for k in range(0, KD, 4):
                        sp.dma_start(w[:, k:k + 4, n * D:(n + 1) * D],
                                     io[name].rearrange("(k p) n -> p k n", p=P)[:, k:k + 4, :]).then_inc(w_here, 16)
                sp.dma_start(k_w[:, :], io["xk_norm_w"].partition_broadcast(P)).then_inc(w_here, 16)
                sp.wait_ge(xn_ready, 1)
                sp.dma_start(x[:, :], io["mem"][P:2 * P, :]).then_inc(x_here, 16)
                for t in range(2):
                    sp.wait_ge(k_ready, t + 1)
                    sp.dma_start(io["mem_kv"][t * P:(t + 1) * P, :], kv[:, :]).then_inc(out, 16)
                sp.wait_ge(out, 32)

            @block.scalar
            def _(act):
                for t in range(2):
                    act.wait_ge(x_here, 32 + 16 * t)
                    act.activation(sq[:, :], x[:, :], ACT.Square, accum_out=ss[:, :]).then_inc(squares, 1)
                    act.wait_ge(turn_done, t + 1)
                    act.activation(xT[:, :, :].rearrange("p a b -> p (a b)"), turned[:, :], ACT.Copy).then_inc(xT_ready, 1)
                    act.wait_ge(projected, t + 1)
                    if t:
                        act.wait_ge(out, 16)
                    act.activation(kv[:, :], acc[:, :], ACT.Copy)
                    act.drain()
                    act.activation(sq[:, :], kv[:, 0:D], ACT.Square).then_inc(kv_copied, 1)
                    if t == 0:
                        act.wait_ge(hs_ready, 1)

            @block.gpsimd
            def _(pool):
                for t in range(2):
                    pool.wait_ge(squares, t + 1)
                    pool_rsqrt(pool, rstd[:, :], ss[:, :], D, half[:, 0:1]).then_inc(rstd_ready, 1)
                    pool.wait_ge(hs_ready, t + 1)
                    pool_rsqrt(pool, rs[:, :], hs[:, :], XD, half[:, 0:XH]).then_inc(rs_ready, 1)

            @block.vector
            def _(dve):
                for t in range(2):
                    dve.wait_ge(rstd_ready, t + 1)
                    if t:
                        dve.wait_ge(turn_done, t)
                    dve.scalar_tensor_tensor(xn[:, :], x[:, :], rstd[:, 0:1], norm_w[:, :], ALU.mult, ALU.mult).then_inc(xn_ready, 1)
                    dve.wait_ge(kv_copied, t + 1)
                    dve.tensor_reduce(hs[:, :], sq[:, :].rearrange("p (h d) -> p h d", h=XH), AX, ALU.add).then_inc(hs_ready, 1)
                    dve.wait_ge(rs_ready, t + 1)
                    dve.wait_ge(w_here, 80)
                    k3 = kv[:, 0:D].rearrange("p (h d) -> p h d", h=XH)
                    dve.tensor_tensor(k3, k3, rs[:, :].unsqueeze(2).to_broadcast([P, XH, XD]), ALU.mult)
                    dve.drain()
                    dve.tensor_tensor(k3, k3, k_w[:, :].unsqueeze(1).to_broadcast([P, XH, XD]), ALU.mult).then_inc(k_ready, 1)

            @block.tensor
            def _(pe):
                for t in range(2):
                    pe.wait_ge(xn_ready, t + 1)
                    for k in range(KD):
                        m = pe.transpose(turned[:, k * P:(k + 1) * P], xn[:, k * P:(k + 1) * P], ident[:, :])
                    m.then_inc(turn_done, 1)
                    pe.wait_ge(xT_ready, t + 1)
                    pe.wait_ge(w_here, 80)
                    if t:
                        pe.wait_ge(kv_copied, t)
                    for g in range(4):
                        for k in range(KD):
                            m = pe.matmul(acc[:, g * 512:(g + 1) * 512], xT[:, k, :], w[:, k, g * 512:(g + 1) * 512],
                                          start=(k == 0), stop=(k == KD - 1))
                    m.then_inc(projected, 1)


def stage_rows(nc, io, scr, ident, half, first, hnT=None):
    name = "mixo" if first else "xo"
    src, w_name, resid, nw_name = (("mix", "w_out", io["x_all"], "xattn_norm_w") if first else
                                   ("xo", "w_xo", scr["h1"], "ffn_norm_w"))
    with Stage(nc, name) as st:
        w = st.sb("w", [P, KD, D])
        norm_w = st.sb("norm_w", [P, D])
        if first:
            w2 = st.sb("w2", [P, KD, D])
            q_w = st.sb("q_w", [P, XD])
            q = st.sb("q", [P, D])
            sq2 = st.sb("sq2", [P, D])
            hs = st.sb("hs", [P, XH])
            rs = st.sb("rs", [P, XH])
        else:
            hT = st.sb("hT", [P, KD, P])
        a = st.sb("a", [P, D])
        res = st.sb("res", [P, D])
        aT = st.sb("aT", [P, KD, P])
        h = st.sb("h", [P, D])
        hn = st.sb("hn", [P, D])
        sq = st.sb("sq", [P, D])
        ss = st.sb("ss", [P, 1])
        rstd = st.sb("rstd", [P, 1])
        nT = st.sb("nT", [P, KD, P])
        p_a = st.ps("p_a", [P, 1024])
        p_h = st.ps("p_h", [P, 1024])
        p_n = st.ps("p_n", [P, 1024])
        p_q = st.ps("p_q", [P, 1024])

        w_here = st.sem("w_here")
        w2_here = st.sem("w2_here")
        a_here = st.sem("a_here")
        res_here = st.sem("res_here")
        a_turned = st.sem("a_turned")
        aT_ready = st.sem("aT_ready")
        h_done = st.sem("h_done")
        h_ready = st.sem("h_ready")
        squares = st.sem("squares")
        rstd_ready = st.sem("rstd_ready")
        hn_ready = st.sem("hn_ready")
        n_turned = st.sem("n_turned")
        nT_ready = st.sem("nT_ready")
        q_done = st.sem("q_done")
        sq2_ready = st.sem("sq2_ready")
        hs_ready = st.sem("hs_ready")
        rs_ready = st.sem("rs_ready")
        q_ready = st.sem("q_ready")
        h_out = st.sem("h_out")
        q_out = st.sem("q_out")
        turns = st.sem("turns")
        pool_turns = st.sem("pool_turns")
        pe_turns = st.sem("pe_turns")

        with nc.Block() as block:

            @block.sync
            def _(sp):
                def load_a(t):
                    sp.dma_start(a[:, :], scr[src][ds(t * P, P), :]).then_inc(a_here, 16)

                def load_res(t):
                    sp.dma_start(res[:, :], resid[ds(t * P, P), :]).then_inc(res_here, 16)

                load_a(0)
                load_res(0)
                sp.dma_start(norm_w[:, :], io[nw_name].partition_broadcast(P)).then_inc(w_here, 16)
                for k in range(0, KD, 2):
                    sp.dma_start(w[:, k:k + 2, :], io[w_name].rearrange("(k p) n -> p k n", p=P)[:, k:k + 2, :]).then_inc(w_here, 16)
                if first:
                    sp.dma_start(q_w[:, :], io["xq_norm_w"].partition_broadcast(P)).then_inc(w2_here, 16)
                    for k in range(0, KD, 4):
                        sp.dma_start(w2[:, k:k + 4, :], io["w_xq"].rearrange("(k p) n -> p k n", p=P)[:, k:k + 4, :]).then_inc(w2_here, 16)

                def store_h(t):
                    wait_turn(sp, h_ready, t + 1, turns)
                    if first:
                        sp.dma_start(scr["h1"][ds(t * P, P), :], h[:, :]).then_inc(h_out, 16)

                def store_q(t):
                    wait_turn(sp, q_ready, t + 1, turns)
                    if first:
                        sp.dma_start(scr["xq"][ds(t * P, P), :], q[:, :]).then_inc(q_out, 16)
                    else:
                        sp.dma_start(scr["h2T"].rearrange("(k p) n -> p k n", p=P)[:, :, ds(t * P, P)], hT[:, :, :]).then_inc(q_out, 16)

                def next_a(t):
                    wait_turn(sp, a_turned, t, turns)
                    load_a(t)

                next_a(1)
                next_a(2)
                store_h(0)
                load_res(1)
                with sp.Fori(2, NTILE - 1) as i:
                    next_a(i + 1)
                    store_h(i - 1)
                    load_res(i)
                    store_q(i - 2)
                store_h(NTILE - 2)
                load_res(NTILE - 1)
                store_q(NTILE - 3)
                store_h(NTILE - 1)
                store_q(NTILE - 2)
                store_q(NTILE - 1)
                if first:
                    sp.wait_ge(h_out, 16 * (NTILE + 1))
                sp.wait_ge(q_out, 16 * (NTILE + 1))

            @block.scalar
            def _(act):
                def take_a(t):
                    act.wait_ge(a_turned, t + 1)
                    act.activation(aT[:, :, :].rearrange("p a b -> p (a b)"), p_a[:, :], ACT.Copy).then_inc(aT_ready, 1)

                def square_h(t):
                    act.wait_ge(h_ready, t + 1)
                    act.activation(sq[:, :], h[:, :], ACT.Square, accum_out=ss[:, :]).then_inc(squares, 1)

                def square_q(t):
                    act.wait_ge(q_done, t + 1)
                    act.activation(sq2[:, :], p_q[:, :], ACT.Square).then_inc(sq2_ready, 1)

                def take_n(t):
                    act.wait_ge(n_turned, t + 1)
                    if first:
                        act.activation(nT[:, :, :].rearrange("p a b -> p (a b)"), p_n[:, :], ACT.Copy).then_inc(nT_ready, 1)
                    else:
                        act.activation(hnT[:, :, ds(t * P, P)], p_n[:, :].rearrange("p (k n) -> p k n", k=KD), ACT.Copy).then_inc(nT_ready, 1)

                def step(i, more):
                    if more:
                        take_a(i + 2)
                    square_h(i + 1)
                    if first:
                        square_q(i)
                        take_n(i + 1)
                    else:
                        take_n(i)

                take_a(0)
                take_a(1)
                square_h(0)
                if first:
                    take_n(0)
                with act.Fori(0, NTILE - 2) as i:
                    step(i, True)
                step(NTILE - 2, False)
                if first:
                    square_q(NTILE - 1)
                else:
                    take_n(NTILE - 1)

            @block.gpsimd
            def _(pool):
                def front(t):
                    wait_turn(pool, squares, t + 1, pool_turns)
                    pool_rsqrt(pool, rstd[:, :], ss[:, :], D, half[:, 0:1]).then_inc(rstd_ready, 1)

                def back(t):
                    if first:
                        wait_turn(pool, hs_ready, t + 1, pool_turns)
                        pool_rsqrt(pool, rs[:, :], hs[:, :], XD, half[:, 0:XH]).then_inc(rs_ready, 1)

                front(0)
                with pool.Fori(0, NTILE - 1) as i:
                    front(i + 1)
                    back(i)
                back(NTILE - 1)

            @block.vector
            def _(dve):
                dve.sem_inc(h_out, 16)
                dve.sem_inc(q_out, 16)
                dve.wait_ge(w_here, 80)
                if first:
                    dve.wait_ge(w2_here, 48)

                def front(t, later):
                    dve.wait_ge(h_done, t + 1)
                    dve.wait_ge(res_here, 16 * (t + 1))
                    if first:
                        dve.wait_ge(h_out, 16 * (t + 1))
                    elif later:
                        dve.wait_ge(n_turned, t)
                    dve.tensor_tensor(h[:, :], p_h[:, :], res[:, :], ALU.add).then_inc(h_ready, 1)
                    dve.wait_ge(rstd_ready, t + 1)
                    if later:
                        dve.wait_ge(n_turned, t)
                    dve.scalar_tensor_tensor(hn[:, :], h[:, :], rstd[:, 0:1], norm_w[:, :], ALU.mult, ALU.mult).then_inc(hn_ready, 1)
                    dve.drain()

                def back(t):
                    if first:
                        dve.wait_ge(sq2_ready, t + 1)
                        dve.tensor_reduce(hs[:, :], sq2[:, :].rearrange("p (h d) -> p h d", h=XH), AX, ALU.add).then_inc(hs_ready, 1)
                        dve.wait_ge(rs_ready, t + 1)
                        dve.wait_ge(q_out, 16 * (t + 1))
                        q3 = q[:, :].rearrange("p (h d) -> p h d", h=XH)
                        dve.tensor_tensor(q3, p_q[:, :].rearrange("p (h d) -> p h d", h=XH),
                                          rs[:, :].unsqueeze(2).to_broadcast([P, XH, XD]), ALU.mult)
                        dve.drain()
                        dve.tensor_tensor(q3, q3, q_w[:, :].unsqueeze(1).to_broadcast([P, XH, XD]), ALU.mult)
                    else:
                        dve.wait_ge(n_turned, t + 1)
                        dve.wait_ge(q_out, 16 * (t + 1))
                        dve.tensor_copy(hT[:, :, :].rearrange("p a b -> p (a b)"), p_q[:, :])
                    dve.drain()
                    dve.sem_inc(q_ready, 1)

                front(0, False)
                with dve.Fori(0, NTILE - 1) as i:
                    front(i + 1, True)
                    back(i)
                back(NTILE - 1)

            @block.tensor
            def _(pe):
                def turn_a(t):
                    pe.wait_ge(a_here, 16 * (t + 1))
                    for k in range(KD):
                        m = pe.transpose(p_a[:, k * P:(k + 1) * P], a[:, k * P:(k + 1) * P], ident[:, :])
                    m.then_inc(a_turned, 1)

                def product_h(t, later=True):
                    if later:
                        wait_turn(pe, h_ready, t, pe_turns)
                    pe.wait_ge(aT_ready, t + 1)
                    for g in range(2):
                        for k in range(KD):
                            m = pe.matmul(p_h[:, g * 512:(g + 1) * 512], aT[:, k, :], w[:, k, g * 512:(g + 1) * 512],
                                          start=(k == 0), stop=(k == KD - 1))
                    m.then_inc(h_done, 1)

                def turn_n(t, later):
                    pe.wait_ge(hn_ready, t + 1)
                    if not first:
                        if later:
                            pe.wait_ge(q_ready, t)
                            pe.wait_ge(nT_ready, t)
                        for k in range(KD):
                            pe.transpose(p_q[:, k * P:(k + 1) * P], h[:, k * P:(k + 1) * P], ident[:, :])
                    for k in range(KD):
                        m = pe.transpose(p_n[:, k * P:(k + 1) * P], hn[:, k * P:(k + 1) * P], ident[:, :])
                    m.then_inc(n_turned, 1)

                def product_q(t, later):
                    pe.wait_ge(nT_ready, t + 1)
                    if later:
                        pe.wait_ge(q_ready, t)
                    for g in range(2):
                        for k in range(KD):
                            m = pe.matmul(p_q[:, g * 512:(g + 1) * 512], nT[:, k, :], w2[:, k, g * 512:(g + 1) * 512],
                                          start=(k == 0), stop=(k == KD - 1))
                    m.then_inc(q_done, 1)

                def step(i, more, later):
                    product_h(i + 1)
                    if more:
                        turn_a(i + 2)
                    if first:
                        product_q(i, later)
                        turn_n(i + 1, True)
                    else:
                        turn_n(i, later)

                turn_a(0)
                pe.wait_ge(w_here, 80)
                product_h(0, False)
                turn_a(1)
                if first:
                    turn_n(0, False)
                    pe.wait_ge(w2_here, 48)
                step(0, True, False)
                with pe.Fori(1, NTILE - 2) as i:
                    step(i, True, True)
                step(NTILE - 2, False, True)
                if first:
                    product_q(NTILE - 1, True)
                else:
                    turn_n(NTILE - 1, True)


def stage_cross_prompt(nc, io, scr, ident):
    with Stage(nc, "xp") as st:
        kn = st.sb("kn", [P, 2, D])
        v = st.sb("v", [P, 2, D])
        kT = st.sb("kT", [P, KD, MEM])
        q = st.sb("q", [P, D])
        qT = st.sb("qT", [P, KD, P])
        p = st.sb("p", [P, XH, MEM])
        mx = st.sb("mx", [P, XH])
        sums = st.sb("sums", [P, XH])
        pT = st.sb("pT", [P, XH, 2, P])
        o = st.sb("o", [P, XH, XD])
        p_q = st.ps("p_q", [P, 1024])
        p_s = st.ps("p_s", [P, 1024])
        p_t = st.ps("p_t", [P, 1024])
        p_o = st.ps("p_o", [P, 1024])
        kv_here = st.sem("kv_here")
        k_turned = st.sem("k_turned")
        k_taken = st.sem("k_taken")
        q_here = st.sem("q_here")
        q_turned = st.sem("q_turned")
        q_ready = st.sem("q_ready")
        s_done = st.sem("s_done")
        mx_ready = st.sem("mx_ready")
        exp_done = st.sem("exp_done")
        p_turned = st.sem("p_turned")
        p_ready = st.sem("p_ready")
        o_done = st.sem("o_done")
        o_ready = st.sem("o_ready")
        o_out = st.sem("o_out")
        turns = st.sem("turns")
        turns_pe = st.sem("turns_pe")
        o_ready0 = st.sem("o_ready0")

        with nc.Block() as block:

            @block.sync
            def _(sp):
                for t in range(2):
                    rows = io["mem_kv"][t * P:(t + 1) * P, :]
                    sp.dma_start(kn[:, t, :], rows[:, 0:D]).then_inc(kv_here, 16)
                    sp.dma_start(v[:, t, :], rows[:, D:2 * D]).then_inc(kv_here, 16)
                sp.dma_start(q[:, :], scr["xq"][0:P, :]).then_inc(q_here, 16)
                with sp.Fori(1, 8) as i:
                    wait_turn(sp, q_turned, i, turns)
                    sp.dma_start(q[:, :], scr["xq"][ds(i * P, P), :]).then_inc(q_here, 16)
                    wait_turn(sp, o_ready, i, turns)
                    sp.dma_start(scr["xo"][ds(i * P - P, P), :], o[:, :, :].rearrange("p a b -> p (a b)")).then_inc(o_out, 16)
                sp.wait_ge(o_ready, 8)
                sp.dma_start(scr["xo"][7 * P:8 * P, :], o[:, :, :].rearrange("p a b -> p (a b)")).then_inc(o_out, 16)
                sp.wait_ge(o_out, 16 * 9)

            @block.tensor
            def _(pe):
                pe.wait_ge(kv_here, 64)
                for c in range(KD):
                    for t in range(2):
                        m = pe.transpose((p_q if c < 4 else p_s)[:, (c % 4) * MEM + t * P:(c % 4) * MEM + (t + 1) * P],
                                         kn[:, t, c * P:(c + 1) * P], ident[:, :])
                m.then_inc(k_turned, 1)
                pe.wait_ge(k_taken, 1)

                def front(t):
                    pe.wait_ge(q_here, 16 * (t + 1))
                    for k in range(KD):
                        m = pe.transpose(p_q[:, k * P:(k + 1) * P], q[:, k * P:(k + 1) * P], ident[:, :])
                    m.then_inc(q_turned, 1)
                    pe.wait_ge(q_ready, t + 1)
                    for h in range(XH):
                        for c in range(2):
                            m = pe.matmul(p_s[:, h * MEM:(h + 1) * MEM], qT[:, 2 * h + c, :], kT[:, 2 * h + c, :], start=(c == 0), stop=(c == 1))
                    m.then_inc(s_done, 1)

                def back(t):
                    pe.wait_ge(exp_done, t + 1)
                    for h in range(XH):
                        for c in range(2):
                            m = pe.transpose(p_t[:, (2 * h + c) * P:(2 * h + c + 1) * P], p[:, h, c * P:(c + 1) * P], ident[:, :])
                    m.then_inc(p_turned, 1)
                    pe.wait_ge(p_ready, t + 1)
                    pe.wait_ge(o_ready0, t + 1)
                    for h in range(XH):
                        for c in range(2):
                            m = pe.matmul(p_o[:, h * XD:(h + 1) * XD], pT[:, h, c, :], v[:, c, h * XD:(h + 1) * XD], start=(c == 0), stop=(c == 1))
                    m.then_inc(o_done, 1)

                front(0)
                with pe.Fori(0, 7) as i:
                    pe.wait_ge(exp_done, i + 1)
                    front(i + 1)
                    back(i)
                back(7)

            @block.scalar
            def _(act):
                act.wait_ge(k_turned, 1)
                act.activation(kT[:, 0:4, :].rearrange("p a b -> p (a b)"), p_q[:, :], ACT.Copy)
                act.activation(kT[:, 4:8, :].rearrange("p a b -> p (a b)"), p_s[:, :], ACT.Copy).then_inc(k_taken, 1)

                def front(t):
                    act.wait_ge(q_turned, t + 1)
                    act.activation(qT[:, :, :].rearrange("p a b -> p (a b)"), p_q[:, :], ACT.Copy, scale=XD ** -0.5).then_inc(q_ready, 1)

                def exps(t, later):
                    act.wait_ge(mx_ready, t + 1)
                    if later:
                        act.wait_ge(p_turned, t)
                    for h in range(XH):
                        a = act.activation(p[:, h, :], p_s[:, h * MEM:(h + 1) * MEM], ACT.Exp, bias=mx[:, h:h + 1], accum_out=sums[:, h:h + 1])
                    a.then_inc(exp_done, 1)

                front(0)
                exps(0, False)
                with act.Fori(1, 8) as i:
                    front(i)
                    act.wait_ge(o_ready0, i + 1)
                    exps(i, True)

            @block.vector
            def _(dve):
                dve.sem_inc(o_ready0, 1)
                dve.sem_inc(o_out, 16)

                def front(t):
                    dve.wait_ge(s_done, t + 1)
                    dve.tensor_reduce(mx[:, :], p_s[:, :].rearrange("p (h m) -> p h m", h=XH), AX, ALU.max)
                    dve.drain()
                    dve.tensor_scalar(mx[:, :], mx[:, :], -1.0, None, ALU.mult).then_inc(mx_ready, 1)

                def back(i):
                    dve.wait_ge(p_turned, i + 1)
                    dve.tensor_copy(pT[:, :, :, :].rearrange("p a b c -> p (a b c)"), p_t[:, :]).then_inc(p_ready, 1)
                    dve.reciprocal(sums[:, :], sums[:, :])
                    dve.drain()
                    dve.wait_ge(o_done, i + 1)
                    dve.wait_ge(o_out, 16 * (i + 1))
                    dve.tensor_tensor(o[:, :, :], p_o[:, :].rearrange("p (h d) -> p h d", h=XH),
                                      sums[:, :].unsqueeze(2).to_broadcast([P, XH, XD]), ALU.mult)
                    dve.drain()
                    dve.sem_inc(o_ready, 1)
                    dve.sem_inc(o_ready0, 1)

                front(0)
                with dve.Fori(0, 7) as i:
                    back(i)
                    front(i + 1)
                back(7)


def stage_cross_sample(nc, io, scr, ident):
    with Stage(nc, "xs") as st:
        kn = st.sb("kn", [P, 2, 2, D])
        v = st.sb("v", [P, 4, 2, D])
        kT = st.sb("kT", [P, KD, MEM])
        q = st.sb("q", [SAMP, D])
        qx = st.sb("qx", [P, KD, NB, 32])
        qc = st.sb("qc", [P, KD, 4, 32])
        p = st.sb("p", [P, MEM])
        mx = st.sb("mx", [P, 1])
        sums = st.sb("sums", [P, 1])
        pT = st.sb("pT", [P, 2, P])
        o = st.sb("o", [P, D])
        zero = st.sb("zero", [64, D])
        p_k = [st.ps(f"p_k{n}", [P, 1024]) for n in range(2)]
        p_s = st.ps("p_s")
        p_t = st.ps("p_t")
        p_o = st.ps("p_o", [P, 1024])
        q_here = st.sem("q_here")
        q_turned = st.sem("q_turned")
        qx_ready = st.sem("qx_ready")
        cleared = st.sem("cleared")
        zero_out = st.sem("zero_out")
        kv_here = [st.sem(f"kv_here{s}") for s in range(2)]
        qc_ready = st.sem("qc_ready")
        k_turned = st.sem("k_turned")
        k_taken = [st.sem(f"k_taken{n}") for n in range(2)]
        s_done = st.sem("s_done")
        mx_ready = st.sem("mx_ready")
        exp_done = st.sem("exp_done")
        p_turned = st.sem("p_turned")
        p_ready = st.sem("p_ready")
        o_done = st.sem("o_done")
        o_ready = st.sem("o_ready")
        o_out = st.sem("o_out")
        turns = st.sem("turns")
        turns_pe = st.sem("turns_pe")
        o_ready0 = st.sem("o_ready0")

        with nc.Block() as block:

            @block.sync
            def _(sp):
                sp.dma_start(q[:, :], scr["xq"][SEQ:TOK, :]).then_inc(q_here, 16)
                sp.wait_ge(cleared, 1)
                sp.dma_start(scr["xo"][TOK:TOKP, :], zero[:, :]).then_inc(zero_out, 16)
                with sp.Fori(0, 2) as g:
                    for b in range(4):
                        wait_turn(sp, k_turned, g * 4 + b + 1, turns)
                        if b == 0:
                            wait_turn(sp, o_done, g + 1, turns)
                        kv = io["cache_mem"][ds(g * 4 + b, 1), :, :].rearrange("a (t p) n -> p (a t) n", p=P)
                        sp.dma_start(kn[:, b % 2, :, :], kv[:, :, 0:D]).then_inc(kv_here[b % 2], 16)
                        sp.dma_start(v[:, b, :, :], kv[:, :, D:2 * D]).then_inc(kv_here[b % 2], 16)
                    wait_turn(sp, o_ready, g + 1, turns)
                    for b in range(4):
                        for h in range(XH):
                            r = 32 * b + 8 * h
                            sp.dma_start(scr["xo"][ds(g * 32 + (SEQ + 8 * b), 8), h * XD:(h + 1) * XD], o[r:r + 8, h * XD:(h + 1) * XD]).then_inc(o_out, 16)
                    wait_turn(sp, o_out, 256 * (g + 1), turns)
                sp.wait_ge(zero_out, 16)

            @block.tensor
            def _(pe):
                pe.wait_ge(q_here, 16)
                for c in range(KD):
                    m = pe.transpose(p_s[:, c * SAMP:(c + 1) * SAMP], q[:, c * P:(c + 1) * P], ident[0:SAMP, 0:SAMP])
                m.then_inc(q_turned, 1)
                pe.wait_ge(qx_ready, 1)
                with pe.Fori(0, 2) as g:
                    pe.wait_ge(qc_ready, g + 1)
                    for b in range(4):
                        pe.wait_ge(kv_here[b % 2], g * 64 + (b // 2 + 1) * 32)
                        for n in range(2):
                            pe.wait_ge(k_taken[n], g * 4 + b + 1)
                            for c in range(4):
                                for t in range(2):
                                    m = pe.transpose(p_k[n][:, c * MEM + t * P:c * MEM + (t + 1) * P],
                                                     kn[:, b % 2, t, (4 * n + c) * P:(4 * n + c + 1) * P], ident[:, :])
                        m.then_inc(k_turned, 1)
                        for n in range(2):
                            pe.wait_ge(k_taken[n], g * 4 + b + 2)
                        for c in range(KD):
                            m = pe.matmul(p_s[32 * b:32 * b + 32, 0:MEM], qc[:, c, b, :], kT[:, c, :], start=(c == 0), stop=(c == KD - 1))
                        m.then_inc(s_done, 1)
                    wait_turn(pe, exp_done, g + 1, turns_pe)
                    for c in range(2):
                        m = pe.transpose(p_t[:, c * P:(c + 1) * P], p[:, c * P:(c + 1) * P], ident[:, :])
                    m.then_inc(p_turned, 1)
                    pe.wait_ge(p_ready, g + 1)
                    for b in range(4):
                        r = slice(32 * b, 32 * b + 32)
                        for n in range(2):
                            for c in range(2):
                                m = pe.matmul(p_o[r, n * 512:(n + 1) * 512], pT[:, c, r], v[:, b, c, n * 512:(n + 1) * 512], start=(c == 0), stop=(c == 1))
                    m.then_inc(o_done, 1)

            @block.scalar
            def _(act):
                act.wait_ge(qx_ready, 1)
                with act.Fori(0, 2) as g:
                    act.wait_ge(s_done, g * 4 + 1)
                    act.activation(qc[:, :, :, :], qx[:, :, ds(g * 4, 4), :], ACT.Copy).then_inc(qc_ready, 1)
                    for b in range(4):
                        act.wait_ge(k_turned, g * 4 + b + 3)
                        act.wait_ge(s_done, g * 4 + b + 1)
                        act.activation(kT[:, 0:4, :].rearrange("p a b -> p (a b)"), p_k[0][:, :], ACT.Copy).then_inc(k_taken[0], 1)
                    act.wait_ge(mx_ready, g + 1)
                    act.activation(p[:, :], p_s[:, 0:MEM], ACT.Exp, bias=mx[:, 0:1], accum_out=sums[:, 0:1]).then_inc(exp_done, 1)

            @block.vector
            def _(dve):
                dve.memset(qx[:, :, :, :], 0.0)
                dve.memset(zero[:, :], 0.0)
                dve.drain()
                dve.sem_inc(cleared, 1)
                dve.sem_inc(k_turned, 2)
                dve.sem_inc(o_done, 1)
                dve.sem_inc(s_done, 1)
                dve.sem_inc(k_taken[0], 1)
                dve.sem_inc(k_taken[1], 1)
                dve.wait_ge(q_turned, 1)
                for c in range(KD):
                    h = c // 2
                    dve.tensor_scalar(qx[:, c, :, 8 * h:8 * h + 8], p_s[:, c * SAMP:(c + 1) * SAMP].rearrange("p (b t) -> p b t", t=NT),
                                      XD ** -0.5, None, ALU.mult)
                dve.drain()
                dve.sem_inc(qx_ready, 1)
                with dve.Fori(0, 2) as g:
                    for b in range(4):
                        dve.wait_ge(k_turned, g * 4 + b + 3)
                        dve.wait_ge(s_done, g * 4 + b + 1)
                        dve.tensor_copy(kT[:, 4:8, :].rearrange("p a b -> p (a b)"), p_k[1][:, :]).then_inc(k_taken[1], 1)
                    dve.wait_ge(s_done, g * 4 + 5)
                    dve.tensor_reduce(mx[:, :], p_s[:, 0:MEM], AX, ALU.max)
                    dve.drain()
                    dve.tensor_scalar(mx[:, :], mx[:, :], -1.0, None, ALU.mult).then_inc(mx_ready, 1)
                    dve.wait_ge(p_turned, g + 1)
                    dve.tensor_copy(pT[:, :, :].rearrange("p a b -> p (a b)"), p_t[:, 0:2 * P]).then_inc(p_ready, 1)
                    dve.reciprocal(sums[:, :], sums[:, :])
                    dve.drain()
                    dve.wait_ge(o_done, g + 2)
                    dve.tensor_scalar(o[:, :], p_o[:, :], sums[:, 0:1], None, ALU.mult).then_inc(o_ready, 1)
                    dve.wait_ge(o_out, 256 * (g + 1))


def stage_mix(nc, io, scr, ident, half):
    with Stage(nc, "pad") as st:
        zero = st.sb("zero", [64, 512])
        cleared, out = st.sem("cleared"), st.sem("out")
        with nc.Block() as block:

            @block.vector
            def _(dve):
                dve.memset(zero[:, :], 0.0).then_inc(cleared, 1)

            @block.sync
            def _(sp):
                sp.wait_ge(cleared, 1)
                sp.dma_start(scr["mix"][TOK:TOKP, 0:512], zero[:, :]).then_inc(out, 16)
                sp.wait_ge(out, 16)
    stage_rows(nc, io, scr, ident, half, True)
    stage_cross_prompt(nc, io, scr, ident)
    stage_cross_sample(nc, io, scr, ident)


def stage_mlp(nc, io, scr, hnT):
    with ExitStack() as ctx:
        gT = ctx.enter_context(nc.sbuf_tensor("mlp_gT", [P, FT, TOK], F32))
        stage_mlp_up(nc, io, hnT, gT)
        stage_mlp_down(nc, io, scr, gT)


SPLIT = [(0, 512), (512, 1024), (1024, TOK)]


def stage_mlp_up(nc, io, hnT, gT):
    with Stage(nc, "up") as st:
        w = st.sb("w", [P, 2, 2, KD, P])
        taps = st.sb("taps", [P, 2 * FT, 4])
        buf = st.sb("buf", [P, 2 * FT, NB, 2])
        kept = st.sb("kept", [P, 2 * FT, 18])
        tap = st.sb("tap", [P, 2, 4])
        xp = [st.sb(f"xp{n}", [P, SEQ + 2]) for n in range(2)]
        xs = [st.sb(f"xs{n}", [P, NB, NT + 2]) for n in range(2)]
        y = [st.sb(f"y{n}", [P, TOK]) for n in range(2)]
        acc = [st.ps(f"acc{n}", [P, 3, 512]) for n in range(2)]
        w_here = [st.sem(f"w_here{s}") for s in range(2)]
        small_here = st.sem("small_here")
        projected = [st.sem(f"projected{n}") for n in range(2)]
        x_ready = [st.sem(f"x_ready{n}") for n in range(2)]
        x_used = [st.sem(f"x_used{n}") for n in range(2)]
        gate_ready = st.sem("gate_ready")
        y_used = st.sem("y_used")
        kept_out = st.sem("kept_out")
        turns = st.sem("turns")
        turns_pool = st.sem("turns_pool")

        with nc.Block() as block:

            @block.sync
            def _(sp):
                w_v = io["w_up"].rearrange("(k p) (a f n) -> f p a k n", p=P, a=2, n=P)

                def load(f, s):
                    for n in range(2):
                        sp.dma_start(w[:, s, n, :, :], w_v[ds(f, 1), :, n, :, :].rearrange("f p k n -> p (f k) n")).then_inc(w_here[s], 16)

                load(0, 0)
                load(1, 1)
                sp.dma_start(taps[:, :, :], io["fconv_wT"].rearrange("(c p) k -> p c k", p=P)).then_inc(small_here, 16)
                sp.dma_start(buf[:, :, :, :].rearrange("p c b k -> p c (b k)"), io["fconv_bufT"].rearrange("(c p) k -> p c k", p=P)).then_inc(small_here, 16)
                with sp.Fori(0, FT // 2 - 1) as i:
                    for s in range(2):
                        wait_turn(sp, projected[1], 2 * i + s + 1, turns)
                        load(2 * i + s + 2, s)
                sp.wait_ge(y_used, FT + 1)
                sp.dma_start(io["fconvT"].rearrange("(c p) k -> p c k", p=P), kept[:, :, :]).then_inc(kept_out, 16)
                sp.wait_ge(kept_out, 16)

            @block.tensor
            def _(pe):
                with pe.Fori(0, FT // 2) as i:
                    for s in range(2):
                        f = 2 * i + s
                        pe.wait_ge(w_here[s], 32 * (i + 1))
                        for n in range(2):
                            pe.wait_ge(x_ready[n], f + 1)
                            for g, (a, b) in enumerate(SPLIT):
                                for k in range(KD):
                                    m = pe.matmul(acc[n][:, g, 0:b - a], w[:, s, n, k, :], hnT[:, k, a:b], start=(k == 0), stop=(k == KD - 1))
                            m.then_inc(projected[n], 1)

            @block.scalar
            def _(act):
                with act.Fori(0, FT) as f:
                    for n in range(2):
                        act.wait_ge(projected[n], f + 1)
                        act.wait_ge(x_used[n], f + 1)
                        act.activation(xp[n][:, 2:], acc[n][:, 0:2, :].rearrange("p a b -> p (a b)"), ACT.Copy)
                        act.activation(xs[n][:, :, 2:], acc[n][:, 2, 0:SAMP].rearrange("p (b t) -> p b t", t=NT), ACT.Copy).then_inc(x_ready[n], 1)
                    act.wait_ge(x_used[1], f + 2)
                    act.activation(y[0][:, :], y[0][:, :], ACT.Silu).then_inc(gate_ready, 1)

            @block.gpsimd
            def _(pool):
                with pool.Fori(0, FT) as f:
                    wait_turn(pool, gate_ready, f + 1, turns_pool)
                    pool.tensor_tensor(gT[:, ds(f, 1), :].rearrange("p a n -> p (a n)"), y[0][:, :], y[1][:, :], ALU.mult).then_inc(y_used, 1)

            @block.vector
            def _(dve):
                for n in range(2):
                    dve.memset(xp[n][:, 0:2], 0.0)
                dve.drain()
                for s in x_ready + x_used + [y_used]:
                    dve.sem_inc(s, 1)
                dve.wait_ge(small_here, 32)
                with dve.Fori(0, FT) as f:
                    for n in range(2):
                        c = f + n * FT
                        dve.tensor_copy(tap[:, n, :], taps[:, ds(c, 1), :].rearrange("p a k -> p (a k)"))
                        dve.tensor_copy(xs[n][:, :, 0:2], buf[:, ds(c, 1), :, :].rearrange("p a b k -> p (a b) k"))
                        dve.drain()
                        dve.wait_ge(x_ready[n], f + 2)
                        if n == 0:
                            dve.wait_ge(y_used, f + 1)
                        yp, ys = y[n][:, 0:SEQ], y[n][:, SEQ:].rearrange("p (b t) -> p b t", t=NT)
                        dve.tensor_scalar(yp, xp[n][:, 0:SEQ], tap[:, n, 0:1], tap[:, n, 3:4], ALU.mult, ALU.add)
                        dve.tensor_scalar(ys, xs[n][:, :, 0:NT], tap[:, n, 0:1], tap[:, n, 3:4], ALU.mult, ALU.add)
                        for k in (1, 2):
                            dve.drain()
                            dve.scalar_tensor_tensor(yp, xp[n][:, k:SEQ + k], tap[:, n, k:k + 1], yp, ALU.mult, ALU.add)
                            dve.scalar_tensor_tensor(ys, xs[n][:, :, k:NT + k], tap[:, n, k:k + 1], ys, ALU.mult, ALU.add)
                        kc = kept[:, ds(c, 1), :].rearrange("p a k -> p (a k)")
                        dve.tensor_copy(kc[:, 0:2], xp[n][:, SEQ:SEQ + 2])
                        dve.tensor_copy(kc[:, 2:18].rearrange("p (b k) -> p b k", k=2), xs[n][:, :, NT:NT + 2])
                        dve.drain()
                        dve.sem_inc(x_used[n], 1)


def stage_mlp_down(nc, io, scr, gT):
    with Stage(nc, "down") as st:
        w = st.sb("w", [P, 2, FT, P])
        res = st.sb("res", [P, 2, TOK])
        yo = st.sb("yo", [P, 2, TOK])
        acc = [st.ps(f"acc{s}", [P, 3, 512]) for s in range(2)]
        w_here = [st.sem(f"w_here{s}") for s in range(2)]
        summed = st.sem("summed")
        y_ready = st.sem("y_ready")
        bank_read = st.sem("bank_read")
        y_out = [st.sem(f"y_out{s}") for s in range(2)]
        turns = st.sem("turns")
        ND = D // P

        with nc.Block() as block:

            @block.sync
            def _(sp):
                w_v = io["w_down"].rearrange("(f p) (c n) -> c p f n", p=P, n=P)
                h_v = scr["h2T"].rearrange("(c p) n -> c p n", p=P)

                def load(c, s):
                    sp.dma_start(w[:, s, :, :], w_v[ds(c, 1), :, :, :].rearrange("c p f n -> p (c f) n")).then_inc(w_here[s], 16)
                    sp.dma_start(res[:, s, :], h_v[ds(c, 1), :, 0:TOK].rearrange("c p n -> p (c n)")).then_inc(w_here[s], 16)

                def store(c, s):
                    sp.dma_start(io["yT"].rearrange("(c p) n -> c p n", p=P)[ds(c, 1), :, 0:TOK].rearrange("c p n -> p (c n)"), yo[:, s, :]).then_inc(y_out[s], 16)

                load(0, 0)
                load(1, 1)
                with sp.Fori(0, ND // 2 - 1) as i:
                    for s in range(2):
                        wait_turn(sp, y_ready, 2 * i + s + 1, turns)
                        load(2 * i + s + 2, s)
                        store(2 * i + s, s)
                for s in range(2):
                    sp.wait_ge(y_ready, ND - 1 + s)
                    store(ND - 2 + s, s)
                for s in range(2):
                    sp.wait_ge(y_out[s], 16 * (ND // 2 + 1))

            @block.tensor
            def _(pe):
                with pe.Fori(0, ND // 2) as i:
                    for s in range(2):
                        pe.wait_ge(w_here[s], 32 * (i + 1))
                        pe.wait_ge(bank_read, 2 * i + s + 1)
                        for g, (a, b) in enumerate(SPLIT):
                            for f in range(FT):
                                m = pe.matmul(acc[s][:, g, 0:b - a], w[:, s, f, :], gT[:, f, a:b], start=(f == 0), stop=(f == FT - 1))
                        m.then_inc(summed, 1)

            @block.vector
            def _(dve):
                dve.sem_inc(bank_read, 2)
                for s in range(2):
                    dve.sem_inc(y_out[s], 16)
                with dve.Fori(0, ND // 2) as i:
                    for s in range(2):
                        dve.wait_ge(w_here[s], 32 * (i + 1))
                        dve.wait_ge(y_out[s], 16 * (i + 1))
                        dve.wait_ge(summed, 2 * i + s + 1)
                        dve.tensor_tensor(yo[:, s, 0:SEQ], acc[s][:, 0:2, :].rearrange("p a b -> p (a b)"), res[:, s, 0:SEQ], ALU.add)
                        dve.tensor_tensor(yo[:, s, SEQ:], acc[s][:, 2, 0:SAMP], res[:, s, SEQ:], ALU.add)
                        dve.drain()
                        dve.sem_inc(y_ready, 1)
                        dve.sem_inc(bank_read, 1)


def program(nc, io, scr):
    with ExitStack() as ctx:
        ident = ctx.enter_context(nc.sbuf_tensor("ident", [P, P], F32))
        half = ctx.enter_context(nc.sbuf_tensor("half", [P, 32], F32))
        load_sem = nc.alloc_semaphore("ident_here")
        with nc.Block() as block:
            @block.sync
            def _(sp):
                sp.dma_start(ident[:, :], io["ident"][:, :]).then_inc(load_sem, 16)
                sp.wait_ge(load_sem, 16)

            @block.vector
            def _(dve):
                dve.memset(half[:, :], -0.5)
        with ExitStack() as front:
            xnT = front.enter_context(nc.sbuf_tensor("xnT", [P, KD, TOKP], F32))
            stage_project(nc, io, scr, xnT, ident, half)
            stage_channels_and_delta(nc, io, scr, xnT, ident, half)
        stage_nsa(nc, io, scr, ident, half)
        stage_mem(nc, io, scr, ident, half)
        stage_mix(nc, io, scr, ident, half)
        with nc.sbuf_tensor("hnT", [P, KD, TOKP], F32) as hnT:
            stage_rows(nc, io, scr, ident, half, False, hnT)
            stage_mlp(nc, io, scr, hnT)


OUTS = {
    "yT": (D, TOKP), "rows": (TOKP, 512), "wrows": (TOKP, 256), "gstate_p": (4, P, P), "gstate_s": (NB, 4, P, P),
    "gconvT": (3 * GW, 27), "fconvT": (2 * FF, 18), "mem_kv": (MEM, 2048), "win_s": (NB, WIN, 256),
}
SCRATCH = {
    "qc": (TOKP, 512), "qr": (TOKP, 512), "z": (TOKP, 512), "misc": (TOKP, 32), "mix": (TOKP, 1024),
    "xq": (TOKP, 1024), "h1": (TOKP, 1024), "xo": (TOKP, 1024), "h2T": (D, TOKP),
}


def kernel(**inputs):
    import numpy as np
    import concourse.bacc as bacc
    from concourse.bass_utils import run_bass_kernel_spmd

    f32 = np.float32
    g = {k: np.asarray(v) for k, v in inputs.items()}
    a = {}
    a["x_all"] = np.concatenate([g["x_prompt"].reshape(SEQ, D), g["x_sample"].reshape(SAMP, D),
                                 np.zeros((TOKP - TOK, D), f32)])
    a["mem"] = g["mem_prompt"].reshape(MEM, D)
    a["cache_kv"] = g["cache_nsa_kv"].reshape(POOL, PAGE, 512)
    a["cache_win"] = g["cache_nsa_win"].reshape(NB, WIN, 256)
    a["state_gdn"] = g["state_gdn"].reshape(NB, 4, P, P)
    a["gconv_bufT"] = g["cache_gdn_conv"].reshape(NB * 3, 3 * GW).T
    a["fconv_bufT"] = g["cache_ffn_conv"].reshape(NB * 2, 2 * FF).T
    a["cache_mem"] = g["cache_mem_kv"].reshape(NB, MEM, 2048)
    a["pages"] = g["page_table"].reshape(1, NB * NPAGE)
    for n in ["attn_norm_w", "w_in", "nsa_q_norm_w", "nsa_k_norm_w", "cmp_w", "gdn_a_log", "gdn_dt_bias",
              "gdn_norm_w", "w_out", "mem_norm_w", "w_xk", "w_xv", "xk_norm_w", "xattn_norm_w", "w_xq", "xq_norm_w",
              "w_xo", "ffn_norm_w", "w_up", "w_down"]:
        a[n] = g[n][0]
    a["cmp_peT"] = g["cmp_pe"][0].transpose(2, 0, 1)
    a["gconv_wT"] = g["gdn_conv_w"][0].T
    a["fconv_wT"] = np.concatenate([g["ffn_conv_w"][0], g["ffn_conv_b"]]).T
    a.update(shape_constants())
    arrays = {k: np.ascontiguousarray(v) for k, v in a.items()}

    nc = bacc.Bacc("TRN2", target_bir_lowering=False, num_devices=1)
    io = {k: nc.dram_tensor(f"in_{k}", v.shape, mybir.dt.from_np(v.dtype), kind="ExternalInput").ap()
          for k, v in arrays.items()}
    for k, shape in OUTS.items():
        io[k] = nc.dram_tensor(f"out_{k}", shape, F32, kind="ExternalOutput").ap()
    scr = {k: nc.dram_tensor(f"scr_{k}", shape, F32, kind="Internal").ap() for k, shape in SCRATCH.items()}
    program(nc, io, scr)
    r = run_bass_kernel_spmd(nc, [{f"in_{k}": v for k, v in arrays.items()}], core_ids=[0]).results[0]
    o = {k: r[f"out_{k}"] for k in OUTS}
    y = o["yT"].T
    fconv = o["fconvT"].T
    gconv = o["gconvT"].T
    c = np.ascontiguousarray
    return (
        c(y[:SEQ]).reshape(1, SEQ, D), c(y[SEQ:TOK]).reshape(NB, NT, D),
        c(o["rows"][:SEQ]).reshape(1, 1, SEQ, 4, 2, HD), c(o["wrows"][SEQ - WIN:SEQ]).reshape(1, 1, WIN, 2, 2, HD),
        c(o["gstate_p"]).reshape(1, 1, 4, P, P), c(gconv[:3]).reshape(1, 1, 3, 3 * GW),
        c(fconv[:2]).reshape(1, 1, 2, 2 * FF), c(o["mem_kv"]).reshape(1, 1, MEM, 2, XH, XD),
        c(o["rows"][SEQ:TOK]).reshape(1, NB, NT, 4, 2, HD), c(o["win_s"]).reshape(1, NB, WIN, 2, 2, HD),
        c(o["gstate_s"]).reshape(1, NB, 4, P, P), c(gconv[3:]).reshape(1, NB, 3, 3 * GW),
        c(fconv[2:]).reshape(1, NB, 2, 2 * FF),
    )


def shape_constants():
    import numpy as np

    f32 = np.float32
    out = {"ident": np.eye(P, dtype=f32)}
    pos = np.concatenate([np.arange(SEQ), np.tile(PAST + np.arange(NT), NB), np.zeros(TOKP - TOK)]).astype(f32)
    half = HD // 2
    inv = np.power(10000.0, -np.arange(half) / half).astype(f32)
    ang = (pos[:, None] * inv[None, :]).astype(f32)
    cos, sin = np.cos(ang), np.sin(ang)
    out["rope"] = np.stack([np.concatenate([cos, cos], 1), np.concatenate([-sin, sin], 1)], 1).astype(f32)
    r, c = np.arange(P)[:, None], np.arange(P)[None, :]
    for name, block in (("p", 64), ("s", NT)):
        same = (r // block) == (c // block)
        levels = [(same & (r // s % 2 == 0) & (c // (2 * s) == r // (2 * s)) & (c // s % 2 == 1)).astype(f32)
                  for s in (1, 2, 4, 8, 16, 32)]
        out["gm_" + name] = np.stack([(same & (r <= c)).astype(f32), same.astype(f32)] + levels, 1)
    out["bsel"] = (np.arange(SAMP)[:, None] // NT == np.arange(NB)[None, :]).astype(f32)
    q, n = np.arange(SEQ)[:, None], np.arange(64)[None, :]
    out["cmp_ok"] = ((16 * n + 31 <= q) & (n < 63)).astype(f32)
    blk = np.arange(16)[None, :]
    forced = (blk == 0) | (blk == q // 64) | (blk == q // 64 - 1)
    out["blk_bonus"] = np.where(blk <= q // 64, np.where(forced, 1e4, 0.0), NEG).astype(f32)
    out["key_no"] = np.broadcast_to(np.arange(SEQ, dtype=f32), (P, SEQ))
    out["q_no"] = np.arange(SEQ, dtype=f32).reshape(8, P).T
    rr, cc, b = np.arange(P)[None, :, None], np.arange(640)[None, None, :], np.arange(8)[:, None, None]
    out["win_bias"] = np.where((cc <= rr + 512) & (cc > rr) & (cc >= 512 - 128 * b), 0.0, NEG).astype(f32)
    t = np.arange(P)[:, None] % NT
    out["samp_bonus"] = np.broadcast_to(np.where(np.isin(np.arange(65), (0, 63, 64)), 1e4, 0.0), (P, 65)).astype(f32)
    out["samp_new"] = np.where(np.arange(NT)[None, :] <= t, 0.0, NEG).astype(f32)
    cw = np.arange(WIN + NT)[None, :]
    out["samp_win"] = np.where((cw > t) & (cw <= t + WIN), 0.0, NEG).astype(f32)
    rb, rg, rt = np.arange(P) // 32, np.arange(P) // 8 % 4, np.arange(P) % 8
    out["gsum"] = ((rb[:, None] == rb[None, :]) & (rt[:, None] == rt[None, :])).astype(f32)
    out["cmp_last"] = np.broadcast_to((np.arange(256) < 255).astype(f32), (P, 256))
    return out
```

```python
from contextlib import ExitStack

import concourse.bass as bass
from concourse import mybir

F32 = mybir.dt.float32
I32 = mybir.dt.int32
ALU = mybir.AluOpType
ACT = mybir.ActivationFunctionType
AX = mybir.AxisListType.X
ds = bass.ds

P = 128
D = 1024
KD = D // P
SEQ = 1024
NB, NT = 8, 8
SAMP = NB * NT
TOK = SEQ + SAMP
NTILE = 9
TOKP = NTILE * P
PAST = 4096
PAGE = 128
NPAGE = PAST // PAGE
POOL = 320
HD = 64
QW = 512
KVW = 768
NATW = QW + KVW + 24
GW = 512
ZW = GW + 8
GCH = 3 * GW // P
EPS = 1e-6
NEG = -1e30
MEM = 256
XH, XD = 4, 256
FF = 2816
FT = FF // P
WIN = 512
PART = 364
LAST = TOK - 2 * PART
SPLIT = [(0, PART), (PART, 2 * PART), (2 * PART, TOK)]


class Stage:

    def __init__(self, nc, name):
        self.nc, self.name, self.ctx, self.sems = nc, name, ExitStack(), []

    def sb(self, name, shape, dt=F32):
        return self.ctx.enter_context(self.nc.sbuf_tensor(f"{self.name}_{name}", shape, dt))

    def ps(self, name, shape=(P, 512), dt=F32):
        return self.ctx.enter_context(self.nc.psum_tensor(f"{self.name}_{name}", list(shape), dt))

    def sem(self, name):
        s = self.nc.alloc_semaphore(f"{self.name}_{name}")
        self.sems.append(s)
        return s

    def __enter__(self):
        return self

    def __exit__(self, *a):
        if a[0] is None:
            self.nc.clear_and_free_semaphores(self.sems)
            self.nc.all_engine_barrier()
        self.ctx.close()


def pool_rsqrt(pool, out, sums, n, half):
    pool.tensor_scalar(out, sums, 1.0 / n, EPS, ALU.mult, ALU.add)
    pool.drain()
    return pool.tensor_tensor(out, out, half, ALU.pow)


def wait_turn(sp, sem, value, turns):
    sp.wait_ge(sem, value)
    sp.sem_inc(turns, 1)


def stage_project(nc, io, scr, xnT, ident, half):
    with Stage(nc, "proj") as st:
        w_nat = st.sb("w_nat", [P, KD, NATW])
        w_zba = st.sb("w_zba", [P, KD, ZW])
        norm_w = st.sb("norm_w", [P, D])
        q_w = st.sb("q_w", [P, HD])
        k_w = st.sb("k_w", [P, 3, HD])
        a_log = st.sb("a_log", [P, 4])
        dt_b = st.sb("dt_b", [P, 4])
        x_in = st.sb("x_in", [P, D])
        rope = st.sb("rope", [P, 2, HD])
        xn = st.sb("xn", [P, D])
        sq = st.sb("sq", [P, QW + KVW])
        x_sq = st.sb("x_sq", [P, D])
        ss = st.sb("ss", [P, 1])
        rstd = st.sb("rstd", [P, 1])
        xT = st.sb("xT", [P, KD, P])
        nat = st.sb("nat", [P, NATW])
        z = st.sb("z", [P, GW])
        ba = st.sb("ba", [P, 8])
        misc = st.sb("misc", [P, 32])
        hs = st.sb("hs", [P, 20])
        rs = st.sb("rs", [P, 20])
        normed = st.sb("normed", [P, 14, HD])
        rot = st.sb("rot", [P, 14, HD])
        rt = st.sb("rt", [P, 14, HD])
        y = st.sb("y", [P, 4])
        ya = st.sb("ya", [P, 4])
        ps_t = [st.ps(f"t{k}") for k in range(2)]
        ps_p = [st.ps(f"p{k}") for k in range(5)]

        w_here = st.sem("w_here")
        group_here = [st.sem(f"group_here{g}") for g in range(4)]
        x_here = st.sem("x_here")
        rope_here = st.sem("rope_here")
        squares = st.sem("squares")
        rstd_ready = st.sem("rstd_ready")
        hs_ready = st.sem("hs_ready")
        rs_ready = st.sem("rs_ready")
        turns = st.sem("turns")
        pool_turns = st.sem("pool_turns")
        xn_ready = st.sem("xn_ready")
        turned = st.sem("turned")
        xT_ready = st.sem("xT_ready")
        xT_kept = st.sem("xT_kept")
        projected = st.sem("projected")
        evacuated = st.sem("evacuated")
        alog_ready = st.sem("alog_ready")
        ya_ready = st.sem("ya_ready")
        ln_ready = st.sem("ln_ready")
        rows_ready = st.sem("rows_ready")
        stored = st.sem("stored")
        NSTORE = 10
        NW = 5

        with nc.Block() as block:

            @block.sync
            def _(sp):
                w_v = io["w_in"].rearrange("(k p) n -> p k n", p=P)
                rows, wrows = io["rows"], io["wrows"]

                def load(t):
                    sp.dma_start(x_in[:, :], io["x_all"][ds(t * P, P), :]).then_inc(x_here, 16)

                def load_rope(t):
                    sp.dma_start(rope[:, :, :], io["rope"][ds(t * P, P), :, :]).then_inc(rope_here, 16)

                def store(t):
                    row = ds(t * P, P)
                    wait_turn(sp, rows_ready, t + 1, turns)
                    wait_turn(sp, evacuated, 5 * (t + 1), turns)
                    for out, src in [(scr["qc"][row, :], normed[:, 0:8, :]), (scr["qr"][row, :], rot[:, 0:8, :]),
                                     (rows[row, 0:128], normed[:, 8:10, :]), (rows[row, 256:384], rot[:, 10:12, :]),
                                     (wrows[row, 0:128], rot[:, 12:14, :])]:
                        sp.dma_start(out, src.rearrange("p a b -> p (a b)")).then_inc(stored, 16)
                    for out, src in [(rows[row, 128:256], nat[:, 640:768]), (rows[row, 384:512], nat[:, 896:1024]),
                                     (wrows[row, 128:256], nat[:, 1152:1280]), (scr["z"][row, :], z[:, :]),
                                     (scr["misc"][row, :], misc[:, :])]:
                        sp.dma_start(out, src).then_inc(stored, 16)

                load(0)
                load_rope(0)
                for dst, name in [(norm_w, "attn_norm_w"), (q_w, "nsa_q_norm_w"), (a_log, "gdn_a_log"),
                                  (dt_b, "gdn_dt_bias")]:
                    sp.dma_start(dst[:, :], io[name].partition_broadcast(P)).then_inc(w_here, 16)
                sp.dma_start(k_w[:, :, :], io["nsa_k_norm_w"].partition_broadcast(P)).then_inc(w_here, 16)
                for g, (a, b) in enumerate(((0, 512), (512, 1024), (1024, NATW))):
                    sp.dma_start(w_nat[:, :, a:b], w_v[:, :, a:b]).then_inc(group_here[g], 16)
                sp.dma_start(w_zba[:, :, :], w_v[:, :, NATW + 3 * GW:]).then_inc(group_here[3], 16)
                with sp.Fori(1, NTILE) as i:
                    wait_turn(sp, xn_ready, i, turns)
                    load(i)
                    store(i - 1)
                    load_rope(i)
                store(NTILE - 1)
                sp.wait_ge(stored, 16 * NSTORE * (NTILE + 1))

            @block.gpsimd
            def _(pool):
                def rstd_of(t):
                    wait_turn(pool, squares, t + 1, pool_turns)
                    pool_rsqrt(pool, rstd[:, :], ss[:, :], D, half[:, 0:1]).then_inc(rstd_ready, 1)

                def tile(i, last=False):
                    pool.wait_ge(xT_ready, i + 1)
                    pool.tensor_copy(xnT[:, :, ds(i * P, P)], xT[:, :, :]).then_inc(xT_kept, 1)
                    if not last:
                        rstd_of(i + 1)
                    wait_turn(pool, hs_ready, i + 1, pool_turns)
                    pool_rsqrt(pool, rs[:, :], hs[:, :], HD, half[:, 0:20]).then_inc(rs_ready, 1)

                rstd_of(0)
                with pool.Fori(0, NTILE - 1) as i:
                    tile(i)
                tile(NTILE - 1, last=True)

            @block.scalar
            def _(act):
                act.wait_ge(w_here, 16 * NW)
                act.activation(a_log[:, :], a_log[:, :], ACT.Exp).then_inc(alog_ready, 1)

                def square(t):
                    act.wait_ge(x_here, 16 * t + 16)
                    act.activation(x_sq[:, :], x_in[:, :], ACT.Square, accum_out=ss[:, :]).then_inc(squares, 1)

                def take_x(i):
                    act.wait_ge(xT_kept, i + 1)
                    act.wait_ge(turned, i + 1)
                    act.activation(xT[:, 0:4, :].rearrange("p a b -> p (a b)"), ps_t[0][:, :], ACT.Copy)
                    act.activation(xT[:, 4:8, :].rearrange("p a b -> p (a b)"), ps_t[1][:, :], ACT.Copy).then_inc(xT_ready, 1)

                def tile(i, last=False):
                    if not last:
                        square(i + 1)
                    act.wait_ge(stored, 16 * NSTORE * (i + 1))
                    act.wait_ge(projected, 5 * i + 1)
                    act.activation(nat[:, 0:512], ps_p[0][:, :], ACT.Copy).then_inc(evacuated, 1)
                    act.wait_ge(projected, 5 * i + 2)
                    act.activation(nat[:, 512:1024], ps_p[1][:, :], ACT.Copy).then_inc(evacuated, 1)
                    act.wait_ge(projected, 5 * i + 3)
                    act.activation(misc[:, 0:24], ps_p[2][:, 256:280], ACT.Sigmoid)
                    act.activation(nat[:, 1024:1280], ps_p[2][:, 0:256], ACT.Copy).then_inc(evacuated, 1)
                    act.wait_ge(projected, 5 * i + 4)
                    act.activation(z[:, 0:260], ps_p[3][:, 0:260], ACT.Silu).then_inc(evacuated, 1)
                    if not last:
                        take_x(i + 1)
                    act.wait_ge(projected, 5 * i + 5)
                    act.activation(z[:, 260:512], ps_p[4][:, 0:252], ACT.Silu)
                    act.activation(misc[:, 24:28], ps_p[4][:, 252:256], ACT.Sigmoid)
                    act.activation(ba[:, :], ps_p[4][:, 252:260], ACT.Copy).then_inc(evacuated, 1)
                    act.wait_ge(ya_ready, i + 1)
                    act.activation(ya[:, :], ya[:, :], ACT.Exp)
                    act.drain()
                    act.activation(ya[:, :], ya[:, :], ACT.Ln, bias=1.0).then_inc(ln_ready, 1)

                square(0)
                take_x(0)
                with act.Fori(0, NTILE - 1) as i:
                    tile(i)
                tile(NTILE - 1, last=True)

            @block.vector
            def _(dve):
                dve.sem_inc(xT_kept, 1)
                dve.sem_inc(stored, 16 * NSTORE)
                dve.wait_ge(alog_ready, 1)
                dve.tensor_scalar(a_log[:, :], a_log[:, :], -1.0, None, ALU.mult)
                dve.memset(misc[:, :], 0.0)
                dve.drain()

                def norm_x(t):
                    dve.wait_ge(rstd_ready, t + 1)
                    dve.scalar_tensor_tensor(xn[:, :], x_in[:, :], rstd[:, 0:1], norm_w[:, :],
                                             ALU.mult, ALU.mult).then_inc(xn_ready, 1)

                def heads(i):
                    dve.wait_ge(evacuated, 5 * (i + 1))
                    dve.wait_ge(rope_here, 16 * (i + 1))
                    dve.tensor_tensor(sq[:, :], nat[:, 0:1280], nat[:, 0:1280], ALU.mult)
                    dve.tensor_tensor(y[:, :], ba[:, 4:8], dt_b[:, :], ALU.add)
                    dve.drain()
                    dve.tensor_scalar(ya[:, :], y[:, :], -1.0, None, ALU.mult)
                    dve.drain()
                    dve.tensor_tensor(ya[:, :], ya[:, :], y[:, :], ALU.min).then_inc(ya_ready, 1)
                    dve.tensor_reduce(hs[:, :], sq[:, :].rearrange("p (a b) -> p a b", b=HD), AX, ALU.add).then_inc(hs_ready, 1)
                    dve.wait_ge(rs_ready, i + 1)
                    dve.tensor_tensor(normed[:, 0:8, :], nat[:, 0:512].rearrange("p (a b) -> p a b", b=HD),
                                      rs[:, 0:8].unsqueeze(2).to_broadcast([P, 8, HD]), ALU.mult)
                    kin = nat[:, 512:1280].rearrange("p (r c a b) -> p r c a b", r=3, c=2, b=HD)[:, :, 0]
                    kout = normed[:, 8:14, :].rearrange("p (r a) b -> p r a b", r=3)
                    krs = rs[:, 8:20].rearrange("p (r c a) -> p r c a", r=3, c=2)[:, :, 0]
                    dve.tensor_tensor(kout, kin, krs.unsqueeze(3).to_broadcast([P, 3, 2, HD]), ALU.mult)
                    dve.drain()
                    dve.tensor_tensor(normed[:, 0:8, :], normed[:, 0:8, :],
                                      q_w[:, :].unsqueeze(1).to_broadcast([P, 8, HD]), ALU.mult)
                    dve.tensor_tensor(kout, kout, k_w[:, :, :].unsqueeze(2).to_broadcast([P, 3, 2, HD]), ALU.mult)
                    dve.drain()
                    h = HD // 2
                    dve.tensor_tensor(rot[:, :, :], normed[:, :, :],
                                      rope[:, 0, :].unsqueeze(1).to_broadcast([P, 14, HD]), ALU.mult)
                    dve.tensor_tensor(rt[:, :, 0:h], normed[:, :, h:HD],
                                      rope[:, 1, 0:h].unsqueeze(1).to_broadcast([P, 14, h]), ALU.mult)
                    dve.tensor_tensor(rt[:, :, h:HD], normed[:, :, 0:h],
                                      rope[:, 1, h:HD].unsqueeze(1).to_broadcast([P, 14, h]), ALU.mult)
                    dve.drain()
                    dve.tensor_tensor(rot[:, :, :], rot[:, :, :], rt[:, :, :], ALU.add)
                    dve.wait_ge(ln_ready, i + 1)
                    dve.scalar_tensor_tensor(y[:, :], y[:, :], 0.0, ya[:, :], ALU.max, ALU.add)
                    dve.drain()
                    dve.tensor_tensor(misc[:, 28:32], y[:, :], a_log[:, :], ALU.mult).then_inc(rows_ready, 1)

                norm_x(0)
                with dve.Fori(0, NTILE - 1) as i:
                    dve.wait_ge(turned, i + 1)
                    norm_x(i + 1)
                    heads(i)
                heads(NTILE - 1)

            @block.tensor
            def _(pe):
                def tile(i, first):
                    pe.wait_ge(xn_ready, i + 1)
                    for k in range(KD):
                        t = pe.transpose(ps_t[k // 4][:, (k % 4) * P:(k % 4 + 1) * P], xn[:, k * P:(k + 1) * P], ident[:, :])
                    t.then_inc(turned, 1)
                    pe.wait_ge(xT_ready, i + 1)
                    for g, (w, a, b) in enumerate([(w_nat, 0, 512), (w_nat, 512, 1024), (w_nat, 1024, NATW),
                                                   (w_zba, 0, 260), (w_zba, 260, ZW)]):
                        if first and g < 4:
                            pe.wait_ge(group_here[g], 16)
                        if not first and g == 4:
                            pe.wait_ge(evacuated, 5 * i)
                        for k in range(KD):
                            m = pe.matmul(ps_p[g][:, 0:b - a], xT[:, k, :], w[:, k, a:b], start=(k == 0), stop=(k == KD - 1))
                        m.then_inc(projected, 1)

                tile(0, True)
                with pe.Fori(1, NTILE) as i:
                    tile(i, False)


def stage_channels(nc, io, scr, xnT, gT):
    with Stage(nc, "chan") as st:
        w = st.sb("w", [P, 2, KD, P])
        conv_w = st.sb("conv_w", [P, GCH, 4])
        conv_buf = st.sb("conv_buf", [P, GCH, NB, 3])
        tap = st.sb("tap", [P, 4])
        xp = st.sb("xp", [P, SEQ + 3])
        xs = st.sb("xs", [P, NB, NT + 3])
        sq = st.sb("sq", [P, TOK])
        nrm = st.sb("nrm", [P, TOK])
        kept = st.sb("kept", [P, GCH, 27])
        ones = st.sb("ones", [P, P])
        eps = st.sb("eps", [P, 1])
        acc = [st.ps(f"acc{s}", [P, 3, 512]) for s in range(2)]

        small_here = st.sem("small_here")
        w_here = [st.sem(f"w_here{s}") for s in range(2)]
        ones_ready = st.sem("ones_ready")
        projected = st.sem("projected")
        x_ready = st.sem("x_ready")
        conv_done = st.sem("conv_done")
        sq_ready = st.sem("sq_ready")
        sums_done = st.sem("sums_done")
        root_ready = st.sem("root_ready")
        channel_done = st.sem("channel_done")
        turns = st.sem("turns")
        kept_out = st.sem("kept_out")

        with nc.Block() as block:

            @block.sync
            def _(sp):
                w_v = io["w_in"][:, NATW:NATW + 3 * GW].rearrange("(k p) (c n) -> c p k n", p=P, n=P)

                def load(c, s):
                    sp.dma_start(w[:, s, :, :], w_v[ds(c, 1), :, :, :].rearrange("c p k n -> p (c k) n")).then_inc(w_here[s], 16)

                load(0, 0)
                load(1, 1)
                sp.dma_start(conv_w[:, :, :], io["gconv_wT"].rearrange("(c p) k -> p c k", p=P)).then_inc(small_here, 16)
                sp.dma_start(conv_buf[:, :, :, :].rearrange("p c b k -> p c (b k)"),
                             io["gconv_bufT"].rearrange("(c p) k -> p c k", p=P)).then_inc(small_here, 16)
                with sp.Fori(0, GCH // 2 - 1) as i:
                    for s in range(2):
                        wait_turn(sp, projected, 2 * i + s + 1, turns)
                        load(2 * i + s + 2, s)
                sp.wait_ge(channel_done, GCH + 1)
                sp.dma_start(io["gconvT"].rearrange("(c p) k -> p c k", p=P), kept[:, :, :]).then_inc(kept_out, 16)
                sp.wait_ge(kept_out, 16)

            @block.tensor
            def _(pe):
                pe.wait_ge(ones_ready, 1)

                def project(c, i, s):
                    pe.wait_ge(w_here[s], 16 * (i + 1))
                    for g, (a, b) in enumerate(SPLIT):
                        for k in range(KD):
                            m = pe.matmul(acc[s][:, g, 0:b - a], w[:, s, k, :], xnT[:, k, a:b],
                                          start=(k == 0), stop=(k == KD - 1))
                    m.then_inc(projected, 1)

                def sums(c, s):
                    pe.wait_ge(sq_ready, c + 1)
                    for g, (a, b) in enumerate(SPLIT):
                        m = pe.matmul(acc[s][:, g, 0:b - a], ones[:, :], sq[:, a:b], start=True, stop=True)
                    m.then_inc(sums_done, 1)

                project(0, 0, 0)
                with pe.Fori(0, 4) as i:
                    pe.wait_ge(root_ready, 2 * i + 1)
                    project(2 * i + 1, i, 1)
                    sums(2 * i, 0)
                    pe.wait_ge(root_ready, 2 * i + 2)
                    project(2 * i + 2, i + 1, 0)
                    sums(2 * i + 1, 1)
                pe.wait_ge(root_ready, 9)
                project(9, 4, 1)
                pe.wait_ge(x_ready, 9)
                project(10, 5, 0)
                pe.wait_ge(x_ready, 10)
                project(11, 5, 1)

            @block.scalar
            def _(act):
                def channel(c, s, normed):
                    act.wait_ge(conv_done, c + 1)
                    act.wait_ge(projected, c + 1)
                    act.activation(xp[:, 3:3 + 2 * PART].rearrange("p (a b) -> p a b", a=2), acc[s][:, 0:2, 0:PART], ACT.Copy)
                    act.activation(xp[:, 3 + 2 * PART:], acc[s][:, 2, 0:SEQ - 2 * PART], ACT.Copy)
                    act.activation(xs[:, :, 3:], acc[s][:, 2, SEQ - 2 * PART:LAST].rearrange("p (b t) -> p b t", t=NT),
                                   ACT.Copy).then_inc(x_ready, 1)
                    act.wait_ge(conv_done, c + 2)
                    g = gT[:, ds(c, 1), 0:TOK].rearrange("p a n -> p (a n)")
                    if not normed:
                        act.activation(g, g, ACT.Silu).then_inc(channel_done, 1)
                        return
                    act.activation(g, g, ACT.Silu)
                    act.drain()
                    act.activation(sq[:, :], g, ACT.Square).then_inc(sq_ready, 1)
                    act.wait_ge(sums_done, c + 1)
                    act.wait_ge(channel_done, c + 1)
                    act.activation(nrm[:, 0:2 * PART].rearrange("p (a b) -> p a b", a=2), acc[s][:, 0:2, 0:PART], ACT.Sqrt, bias=eps[:, 0:1])
                    act.activation(nrm[:, 2 * PART:], acc[s][:, 2, 0:LAST], ACT.Sqrt, bias=eps[:, 0:1]).then_inc(root_ready, 1)

                act.sem_inc(root_ready, 1)
                act.wait_ge(ones_ready, 1)
                with act.Fori(0, 4) as i:
                    for s in range(2):
                        channel(2 * i + s, s, True)
                with act.Fori(4, 6) as i:
                    for s in range(2):
                        channel(2 * i + s, s, False)

            @block.vector
            def _(dve):
                dve.memset(ones[:, :], 1.0)
                dve.memset(eps[:, :], EPS)
                dve.memset(xp[:, 0:3], 0.0)
                dve.memset(gT[:, :, TOK:TOKP], 0.0)
                dve.drain()
                dve.sem_inc(ones_ready, 1)
                dve.sem_inc(conv_done, 1)
                dve.sem_inc(channel_done, 1)
                dve.wait_ge(small_here, 32)

                def convolve(c):
                    dve.tensor_copy(tap[:, :], conv_w[:, ds(c, 1), :].rearrange("p a k -> p (a k)"))
                    dve.tensor_copy(xs[:, :, 0:3], conv_buf[:, ds(c, 1), :, :].rearrange("p a b k -> p (a b) k"))
                    dve.drain()
                    dve.wait_ge(x_ready, c + 1)
                    g = gT[:, ds(c, 1), 0:SEQ].rearrange("p a n -> p (a n)")
                    gs = gT[:, ds(c, 1), SEQ:TOK].rearrange("p a (b t) -> p (a b) t", t=NT)
                    dve.tensor_scalar(g, xp[:, 0:SEQ], tap[:, 0:1], None, ALU.mult)
                    dve.tensor_scalar(gs, xs[:, :, 0:NT], tap[:, 0:1], None, ALU.mult)
                    for k in range(1, 4):
                        dve.drain()
                        dve.scalar_tensor_tensor(g, xp[:, k:SEQ + k], tap[:, k:k + 1], g, ALU.mult, ALU.add)
                        dve.scalar_tensor_tensor(gs, xs[:, :, k:NT + k], tap[:, k:k + 1], gs, ALU.mult, ALU.add)
                    kc = kept[:, ds(c, 1), :].rearrange("p a k -> p (a k)")
                    dve.tensor_copy(kc[:, 0:3], xp[:, SEQ:SEQ + 3])
                    dve.tensor_copy(kc[:, 3:27].rearrange("p (b k) -> p b k", k=3), xs[:, :, NT:NT + 3])
                    dve.drain()
                    dve.sem_inc(conv_done, 1)

                def normalise(c, scale):
                    dve.wait_ge(root_ready, c + 2)
                    dve.reciprocal(nrm[:, :], nrm[:, :])
                    dve.drain()
                    ga = gT[:, ds(c, 1), 0:TOK].rearrange("p a n -> p (a n)")
                    dve.scalar_tensor_tensor(ga, ga, scale, nrm[:, :], ALU.mult, ALU.mult).then_inc(channel_done, 1)

                convolve(0)
                for lo, hi, scale in ((0, 4, P ** -0.5), (4, 8, 1.0)):
                    with dve.Fori(lo, hi) as c:
                        convolve(c + 1)
                        normalise(c, scale)
                with dve.Fori(9, GCH) as c:
                    convolve(c)


def stage_delta_sample(nc, io, scr, gT, ident, half):
    H, L = 4, 3
    with Stage(nc, "delta_s") as st:
        masks = st.sb("masks", [P, 8, P])
        ones = st.sb("ones", [P, P])
        norm_w = st.sb("norm_w", [P, P])
        gates = st.sb("gates", [P, NTILE, 32])
        cur = st.sb("cur", [P, 12, P])
        bg = st.sb("bg", [P, 8])
        ug = st.sb("ug", [P, H, P])
        bd = st.sb("bd", [P, H, P])
        gsm = st.sb("gsm", [P, 8])
        dec = st.sb("dec", [P, H, P])
        er = st.sb("er", [P, H, P])
        ex = st.sb("ex", [P, 8])
        qkT = st.sb("qkT", [P, H, P])
        bm = st.sb("bm", [P, H, P])
        wr = st.sb("wr", [P, H, P])
        kd = st.sb("kd", [P, H, P])
        vb = st.sb("vb", [P, H, P])
        tm = st.sb("tm", [P, H, P])
        X = st.sb("X", [P, H, P])
        Z = st.sb("Z", [P, H, P])
        Y = st.sb("Y", [P, H, P])
        u = st.sb("u", [P, H, P])
        wq = st.sb("wq", [P, H, 2, P])
        vn = st.sb("vn", [P, H, P])
        S = st.sb("S", [P, H, NB, P])
        zt = st.sb("zt", [P, H, P])
        o = st.sb("o", [P, H, P])
        osq = st.sb("osq", [P, H, P])
        oss = st.sb("oss", [P, H])
        ors = st.sb("ors", [P, H])
        bsel = st.sb("bsel", [SAMP, NB])
        vx = st.sb("vx", [SAMP, 2, NB, P])
        back = st.sb("back", [P, H, 2, SAMP])
        o_in = st.sb("o_in", [SAMP, H, P])
        bank = [st.ps(f"b{k}") for k in range(8)]

        here = st.sem("here")
        z_here = st.sem("z_here")
        ones_ready = st.sem("ones_ready")
        cur_ready = st.sem("cur_ready")
        src_ready = st.sem("src_ready")
        pairs_done = st.sem("pairs_done")
        gsm_ready = st.sem("gsm_ready")
        er_ready = st.sem("er_ready")
        arg_ready = st.sem("arg_ready")
        dec_ready = st.sem("dec_ready")
        mats_ready = st.sem("mats_ready")
        tm_ready = st.sem("tm_ready")
        y_done = st.sem("y_done")
        y_ready = st.sem("y_ready")
        step_done = st.sem("step_done")
        xz_ready = st.sem("xz_ready")
        uw_done = st.sem("uw_done")
        w_ready = st.sem("w_ready")
        qd_ready = st.sem("qd_ready")
        ws_done = st.sem("ws_done")
        vn_ready = st.sem("vn_ready")
        chunk_done = st.sem("chunk_done")
        oss_ready = st.sem("oss_ready")
        ors_ready = st.sem("ors_ready")
        o_ready = st.sem("o_ready")
        o_out = st.sem("o_out")
        pool_turns = st.sem("pool_turns")
        back_ready = st.sem("back_ready")

        def col(ap, h=H, n=P):
            return ap.unsqueeze(2).to_broadcast([P, h, n])

        def head(ap):
            return ap.unsqueeze(1).to_broadcast([P, H, P])

        def flat(t):
            return t[:, :, :].rearrange("p a b -> p (a b)")

        with nc.Block() as block:

            @block.sync
            def _(sp):
                sp.dma_start(masks[:, :, :], io["gm_s"]).then_inc(here, 16)
                sp.dma_start(norm_w[:, :], io["gdn_norm_w"].partition_broadcast(P)).then_inc(here, 16)
                sp.dma_start(gates[:, :, :], scr["misc"].rearrange("(t p) n -> p t n", p=P)).then_inc(here, 16)
                sp.dma_start(bsel[:, :], io["bsel"]).then_inc(here, 16)
                for h in range(H):
                    sp.dma_start(S[:, h, :, :], io["state_gdn"][:, h].rearrange("b k d -> k b d")).then_inc(here, 16)

                sp.dma_start(flat(zt), scr["z"][SEQ:SEQ + P, :]).then_inc(z_here, 16)
                sp.wait_ge(o_ready, 1)
                sp.dma_start(scr["mix"][SEQ:SEQ + P, 512:1024], flat(o)).then_inc(o_out, 16)
                for h in range(H):
                    sp.dma_start(io["gstate_s"][:, h].rearrange("b k d -> k b d"), S[:, h, :, :]).then_inc(o_out, 16)
                sp.wait_ge(o_out, 80)

            @block.scalar
            def _(act):
                act.activation(cur[:, :, :], gT[:, :, SEQ:SEQ + P], ACT.Copy).then_inc(cur_ready, 1)
                act.wait_ge(gsm_ready, 1)
                act.activation(flat(er), bank[0][:, :], ACT.Exp)
                act.activation(ex[:, :], gsm[:, :], ACT.Exp).then_inc(er_ready, 1)
                act.wait_ge(arg_ready, 1)
                act.activation(flat(dec), flat(dec), ACT.Exp).then_inc(dec_ready, 1)
                act.wait_ge(uw_done, 1)
                act.activation(wq[:, :, 0, :], bank[6][:, :].rearrange("p (h n) -> p h n", h=H), ACT.Copy).then_inc(w_ready, 1)
                act.wait_ge(ws_done, 1)
                act.activation(back[:, :, :, :].rearrange("p a b c -> p (a b c)"), bank[0][:, :], ACT.Copy).then_inc(back_ready, 1)

            @block.gpsimd
            def _(pool):
                pool.wait_ge(here, 128)

                for l in range(L):
                    wait_turn(pool, mats_ready, 1, pool_turns)
                    if l == 1:
                        wait_turn(pool, xz_ready, 1, pool_turns)
                    elif l:
                        wait_turn(pool, y_done, l, pool_turns)
                    pool.tensor_tensor(tm[:, :, :], bm[:, :, :], head(masks[:, 2 + l, :]), ALU.mult).then_inc(tm_ready, 1)
                    if l == 0:
                        pool.tensor_tensor(wq[:, :, 1, :], cur[:, 0:4, :], er[:, :, :], ALU.mult).then_inc(qd_ready, 1)
                wait_turn(pool, oss_ready, 1, pool_turns)
                pool_rsqrt(pool, ors[:, :], oss[:, :], P, half[:, 0:H]).then_inc(ors_ready, 1)

            @block.tensor
            def _(pe):
                pe.wait_ge(here, 128)
                pe.wait_ge(ones_ready, 1)

                def per_head(out, lhs, rhs):
                    for h in range(H):
                        m = pe.matmul(out[:, h * P:(h + 1) * P], lhs(h), rhs(h), start=True, stop=True)
                    return m

                pe.wait_ge(src_ready, 1)
                pe.matmul(bank[0][:, :], ones[:, :], flat(ug), start=True, stop=True)
                pe.matmul(bank[1][:, :], ones[:, :], flat(bd), start=True, stop=True)
                pe.matmul(bank[2][:, 0:4], masks[:, 0, :], bg[:, 4:8], start=True, stop=True)
                pe.matmul(bank[2][:, 4:8], masks[:, 1, :], bg[:, 4:8], start=True, stop=True)
                pe.wait_ge(cur_ready, 1)
                for h in range(H):
                    pe.transpose(bank[3][:, h * P:(h + 1) * P], cur[:, 4 + h, :], ident[:, :])
                for h in range(H):
                    pe.transpose(bank[4][:, h * P:(h + 1) * P], cur[:, 8 + h, :], ident[:, :])
                per_head(bank[5], lambda h: cur[:, 4 + h, :], lambda h: cur[:, 4 + h, :])
                per_head(bank[6], lambda h: cur[:, 4 + h, :], lambda h: cur[:, h, :]).then_inc(pairs_done, 1)
                for l in range(L):
                    pe.wait_ge(tm_ready, l + 1)
                    if l:
                        pe.wait_ge(xz_ready, l)
                    per_head(bank[7], lambda h: tm[:, h, :],
                             lambda h: X[:, h, :] if l else ident[:, :]).then_inc(y_done, 1)
                    if l:
                        pe.wait_ge(y_ready, l + 1)
                        per_head(bank[3], lambda h: Z[:, h, :], lambda h: Y[:, h, :])
                        per_head(bank[4], lambda h: Y[:, h, :], lambda h: Z[:, h, :]).then_inc(step_done, 1)
                pe.wait_ge(xz_ready, L)
                per_head(bank[5], lambda h: Z[:, h, :], lambda h: vb[:, h, :])
                per_head(bank[6], lambda h: wr[:, h, :], lambda h: Z[:, h, :]).then_inc(uw_done, 1)
                pe.wait_ge(w_ready, 1)
                pe.wait_ge(qd_ready, 1)
                for h in range(H):
                    for b in range(NB):
                        t = slice(b * NT, (b + 1) * NT)
                        out = bank[0][:, h * P:(h + 1) * P].rearrange("p (w t) -> p w t", w=2)[:, :, t]
                        m = pe.matmul(out, S[:, h, b, :], wq[:, h, :, t], start=True, stop=True)
                m.then_inc(ws_done, 1)
                pe.wait_ge(back_ready, 1)
                for h in range(H):
                    pe.transpose(bank[2][0:SAMP, h * P:(h + 1) * P], back[:, h, 0, :], ident[:, :])
                for h in range(H):
                    m = pe.transpose(bank[3][0:SAMP, h * P:(h + 1) * P], back[:, h, 1, :], ident[:, :])
                m.then_inc(back_ready, 1)
                pe.wait_ge(vn_ready, 1)
                for h in range(H):
                    m = pe.matmul(bank[1][0:SAMP, h * P:(h + 1) * P], qkT[0:SAMP, h, 0:SAMP], vn[0:SAMP, h, :], start=True, stop=True)
                m.then_inc(chunk_done, 1)
                for h in range(H):
                    pe.wait_ge(vn_ready, 2 + h)
                    for k in range(2):
                        m = pe.matmul(bank[4 + 2 * (h % 2) + k][:, :], kd[0:SAMP, h, :],
                                      vx[:, h % 2, 4 * k:4 * k + 4, :].rearrange("p a b -> p (a b)"), start=True, stop=True)
                    m.then_inc(chunk_done, 1)

            @block.vector
            def _(dve):
                dve.memset(ones[:, :], 1.0)
                dve.drain()
                dve.sem_inc(ones_ready, 1)
                dve.wait_ge(here, 128)

                t = slice(NTILE - 1, NTILE)
                dve.tensor_copy(bg[:, :], gates[:, t, 24:32].rearrange("p a n -> p (a n)"))
                dve.drain()
                dve.tensor_tensor(ug[:, :, :], head(masks[:, 0, :]), col(bg[:, 4:8]), ALU.mult)
                dve.tensor_tensor(bd[:, :, :], head(ident[:, :]), col(bg[:, 0:4]), ALU.mult)
                dve.drain()
                dve.sem_inc(src_ready, 1)
                dve.wait_ge(pairs_done, 1)
                dve.tensor_copy(gsm[:, 0:4], bank[2][:, 0:4])
                dve.drain()
                dve.tensor_tensor(gsm[:, 4:8], bank[2][:, 4:8], gsm[:, 0:4], ALU.subtract)
                dve.tensor_tensor(dec[:, :, :], bank[0][:, :].rearrange("p (h n) -> p h n", h=H), col(gsm[:, 0:4]), ALU.subtract)
                dve.drain()
                dve.tensor_scalar(dec[:, :, :], dec[:, :, :], 0.0, None, ALU.min).then_inc(arg_ready, 1)
                dve.sem_inc(gsm_ready, 1)
                dve.wait_ge(er_ready, 1)
                dve.wait_ge(dec_ready, 1)
                dve.tensor_tensor(ex[:, 0:4], ex[:, 0:4], bg[:, 0:4], ALU.mult)
                dve.tensor_tensor(dec[:, :, :], dec[:, :, :], head(masks[:, 0, :]), ALU.mult)
                dve.drain()
                dve.tensor_tensor(bm[:, :, :], bank[5][:, :].rearrange("p (h n) -> p h n", h=H), dec[:, :, :], ALU.mult)
                dve.tensor_tensor(qkT[:, :, :], bank[6][:, :].rearrange("p (h n) -> p h n", h=H), dec[:, :, :], ALU.mult)
                dve.drain()
                dve.tensor_tensor(flat(bm), flat(bm), bank[1][:, :], ALU.mult).then_inc(mats_ready, 1)
                dve.tensor_tensor(wr[:, :, :], bank[3][:, :].rearrange("p (h n) -> p h n", h=H), col(ex[:, 0:4]), ALU.mult)
                dve.tensor_tensor(kd[:, :, :], bank[3][:, :].rearrange("p (h n) -> p h n", h=H), col(ex[:, 4:8]), ALU.mult)
                dve.tensor_tensor(vb[:, :, :], bank[4][:, :].rearrange("p (h n) -> p h n", h=H), col(bg[:, 0:4]), ALU.mult)
                for l in range(L):
                    dve.wait_ge(y_done, l + 1)
                    if l == 0:
                        dve.tensor_tensor(X[:, :, :], head(ident[:, :]), bank[7][:, :].rearrange("p (h n) -> p h n", h=H), ALU.subtract)
                        dve.tensor_tensor(Z[:, :, :], head(ident[:, :]), tm[:, :, :], ALU.subtract)
                        dve.drain()
                        dve.sem_inc(y_ready, 1)
                        dve.sem_inc(xz_ready, 1)
                        continue
                    dve.tensor_copy(flat(Y), bank[7][:, :]).then_inc(y_ready, 1)
                    dve.wait_ge(step_done, l)
                    dve.tensor_tensor(flat(X), flat(X), bank[3][:, :], ALU.subtract)
                    dve.tensor_tensor(flat(Z), flat(Z), bank[4][:, :], ALU.subtract)
                    dve.drain()
                    dve.sem_inc(xz_ready, 1)
                dve.wait_ge(uw_done, 1)
                dve.tensor_copy(flat(u), bank[5][:, :])
                dve.drain()
                n = SAMP
                dve.wait_ge(back_ready, 2)
                v3 = lambda b: b[0:n, :].rearrange("p (h n) -> p h n", h=H)
                dve.tensor_tensor(vn[0:n, :, :], u[0:n, :, :], v3(bank[2]), ALU.subtract).then_inc(vn_ready, 1)
                dve.tensor_copy(o_in[:, :, :], v3(bank[3]))
                dve.drain()
                dve.wait_ge(chunk_done, 1)
                dve.tensor_tensor(o_in[:, :, :], o_in[:, :, :], v3(bank[1]), ALU.add)
                dve.drain()
                dve.memset(oss[:, :], 1.0)
                dve.memset(o[:, :, :], 0.0)
                dve.tensor_tensor(osq[0:n, :, :], o_in[:, :, :], o_in[:, :, :], ALU.mult)

                def spread(h):
                    dve.tensor_tensor(vx[:, h % 2, :, :], vn[0:n, h, :].unsqueeze(1).to_broadcast([n, NB, P]),
                                      bsel[:, :].unsqueeze(2).to_broadcast([n, NB, P]), ALU.mult).then_inc(vn_ready, 1)

                spread(0)
                for h in range(H):
                    if h < H - 1:
                        spread(h + 1)
                    keep = er[:, h, 0:SAMP].rearrange("p (b t) -> p b t", t=NT)[:, :, NT - 1]
                    dve.tensor_tensor(S[:, h, :, :], S[:, h, :, :], keep.unsqueeze(2).to_broadcast([P, NB, P]), ALU.mult)
                    dve.drain()
                    dve.wait_ge(chunk_done, 2 + h)
                    for k in range(2):
                        dve.tensor_tensor(S[:, h, 4 * k:4 * k + 4, :], S[:, h, 4 * k:4 * k + 4, :],
                                          bank[4 + 2 * (h % 2) + k][:, :].rearrange("p (h n) -> p h n", h=4), ALU.add)
                    dve.drain()
                dve.tensor_reduce(oss[0:n, :], osq[0:n, :, :], AX, ALU.add).then_inc(oss_ready, 1)
                dve.wait_ge(ors_ready, 1)
                dve.wait_ge(z_here, 16)
                dve.tensor_tensor(o[0:n, :, :], o_in[:, :, :], ors[0:n, :].unsqueeze(2).to_broadcast([n, H, P]), ALU.mult)
                dve.drain()
                dve.tensor_tensor(o[0:n, :, :], o[0:n, :, :], norm_w[0:n, :].unsqueeze(1).to_broadcast([n, H, P]), ALU.mult)
                dve.drain()
                dve.tensor_tensor(o[0:n, :, :], o[0:n, :, :], zt[0:n, :, :], ALU.mult)
                dve.drain()
                dve.sem_inc(o_ready, 1)


def stage_delta_prompt(nc, io, scr, gT, ident, half):
    H, L, C = 4, 6, 64
    ROUNDS = SEQ // P // 2
    with Stage(nc, "delta_p") as st:
        masks = st.sb("masks", [P, 8, P])
        ones = st.sb("ones", [P, P])
        norm_w = st.sb("norm_w", [P, P])
        gates = st.sb("gates", [P, NTILE, 32])
        S = st.sb("S", [P, 2, H, P])

        def slots(name, shape):
            return [st.sb(f"{name}{s}", shape) for s in range(2)]

        cur = slots("cur", [P, 12, P])
        bg = slots("bg", [P, 8])
        ug_y = slots("ug_y", [P, H, P])
        bd_vn = slots("bd_vn", [P, H, P])
        dec_sq = slots("dec_sq", [P, H, P])
        gsm = slots("gsm", [P, 8])
        er = slots("er", [P, H, P])
        ex = slots("ex", [P, 8])
        qkT = slots("qkT", [P, H, P])
        bm = slots("bm", [P, H, P])
        wr = slots("wr", [P, H, P])
        kd = slots("kd", [P, H, P])
        vb = slots("vb", [P, H, P])
        tm = slots("tm", [P, H, P])
        X = slots("X", [P, H, P])
        Z = slots("Z", [P, H, P])
        u = slots("u", [P, H, P])
        wq = slots("wq", [P, H, 2, P])
        zt = slots("zt", [P, H, P])
        o = slots("o", [P, H, P])
        oss = slots("oss", [P, H])
        ors = slots("ors", [P, H])
        bank = [st.ps(f"b{k}") for k in range(8)]
        Y_BANK, X_BANK, Z_BANK = (7, 0), (3, 1), (4, 2)
        U_BANK, W_BANK, O_BANK = (5, 3), (6, 7), (1, 7)

        here = st.sem("here")
        ones_ready = st.sem("ones_ready")

        def by_slot(name):
            return [st.sem(f"{name}{s}") for s in range(2)]

        z_here = by_slot("z_here")
        cur_ready = by_slot("cur_ready")
        src_ready = by_slot("src_ready")
        pairs_done = by_slot("pairs_done")
        gsm_ready = by_slot("gsm_ready")
        ex_ready = by_slot("ex_ready")
        er_ready = by_slot("er_ready")
        arg_ready = by_slot("arg_ready")
        dec_ready = by_slot("dec_ready")
        mats_ready = by_slot("mats_ready")
        banks_read = by_slot("banks_read")
        tm_ready = by_slot("tm_ready")
        y_done = by_slot("y_done")
        y_ready = by_slot("y_ready")
        step_done = by_slot("step_done")
        xz_ready = by_slot("xz_ready")
        uw_done = by_slot("uw_done")
        w_ready = by_slot("w_ready")
        qd_ready = by_slot("qd_ready")
        out_done = by_slot("out_done")
        sq_ready = by_slot("sq_ready")
        oss_ready = by_slot("oss_ready")
        ors_ready = by_slot("ors_ready")
        o_ready = by_slot("o_ready")
        ws_done = st.sem("ws_done")
        vn_ready = st.sem("vn_ready")
        kv_done = st.sem("kv_done")
        S_ready = st.sem("S_ready")
        o_out = st.sem("o_out")
        turns = st.sem("turns")
        pool_turns = st.sem("pool_turns")

        def col(ap, h=H, n=P):
            return ap.unsqueeze(2).to_broadcast([P, h, n])

        def head(ap):
            return ap.unsqueeze(1).to_broadcast([P, H, P])

        def flat(t):
            return t[:, :, :].rearrange("p a b -> p (a b)")

        def heads_of(b, r=slice(0, P)):
            return bank[b][r, :].rearrange("p (h n) -> p h n", h=H)

        def run(eng, two_tiles):
            with eng.Fori(0, ROUNDS - 1) as i:
                two_tiles(i, False)
            two_tiles(ROUNDS - 1, True)

        with nc.Block() as block:

            @block.sync
            def _(sp):
                sp.dma_start(masks[:, :, :], io["gm_p"]).then_inc(here, 16)
                sp.dma_start(norm_w[:, :], io["gdn_norm_w"].partition_broadcast(P)).then_inc(here, 16)
                sp.dma_start(gates[:, :, :], scr["misc"].rearrange("(t p) n -> p t n", p=P)).then_inc(here, 16)
                with sp.Fori(0, ROUNDS) as i:
                    for s in range(2):
                        row = ds((2 * i + s) * P, P)
                        wait_turn(sp, o_ready[s], i + 1, turns)
                        sp.dma_start(flat(zt[s]), scr["z"][row, :]).then_inc(z_here[s], 16)
                    for s in range(2):
                        row = ds((2 * i + s) * P, P)
                        wait_turn(sp, o_ready[s], i + 2, turns)
                        sp.dma_start(scr["mix"][row, 512:1024], flat(o[s])).then_inc(o_out, 16)
                    wait_turn(sp, o_out, 32 * (i + 1), turns)
                sp.wait_ge(S_ready, 4 * ROUNDS + 1)
                sp.dma_start(io["gstate_p"].rearrange("h k d -> k h d"), S[:, 0, :, :]).then_inc(o_out, 16)
                sp.wait_ge(o_out, 32 * ROUNDS + 16)

            @block.scalar
            def _(act):
                def take(j, s):
                    act.activation(cur[s][:, :, :], gT[:, :, ds(j * P, P)], ACT.Copy).then_inc(cur_ready[s], 1)

                def two_tiles(i, last):
                    for s in range(2):
                        act.wait_ge(gsm_ready[s], i + 1)
                        act.activation(ex[s][:, :], gsm[s][:, :], ACT.Exp).then_inc(ex_ready[s], 1)
                        act.wait_ge(arg_ready[s], i + 1)
                        act.activation(flat(dec_sq[s]), flat(dec_sq[s]), ACT.Exp).then_inc(dec_ready[s], 1)
                        act.activation(flat(er[s]), bank[0][:, :], ACT.Exp).then_inc(er_ready[s], 1)
                    for l in range(1, L):
                        for s in range(2):
                            act.wait_ge(y_done[s], L * i + l + 1)
                            act.activation(flat(ug_y[s]), bank[Y_BANK[s]][:, :], ACT.Copy).then_inc(y_ready[s], 1)
                    for s in range(2):
                        act.wait_ge(uw_done[s], i + 1)
                        act.activation(wq[s][:, :, 0, :], heads_of(W_BANK[s]), ACT.Copy).then_inc(w_ready[s], 1)
                    if not last:
                        for s in range(2):
                            act.wait_ge(qd_ready[s], i + 1)
                            take(2 * i + 2 + s, s)
                    for s in range(2):
                        act.wait_ge(out_done[s], 2 * (i + 1))
                        act.activation(flat(dec_sq[s]), bank[O_BANK[s]][:, :], ACT.Square).then_inc(sq_ready[s], 1)

                for s in range(2):
                    take(s, s)
                run(act, two_tiles)

            @block.gpsimd
            def _(pool):
                pool.wait_ge(here, 48)
                with pool.Fori(0, ROUNDS) as i:
                    for l in range(L):
                        for s in range(2):
                            if l == 0:
                                wait_turn(pool, mats_ready[s], i + 1, pool_turns)
                            elif l == 1:
                                wait_turn(pool, xz_ready[s], L * i + 1, pool_turns)
                            else:
                                wait_turn(pool, y_done[s], L * i + l, pool_turns)
                            pool.tensor_tensor(tm[s][:, :, :], bm[s][:, :, :], head(masks[:, 2 + l, :]), ALU.mult).then_inc(tm_ready[s], 1)
                            if l == 0:
                                pool.tensor_tensor(wq[s][:, :, 1, :], cur[s][:, 0:4, :], er[s][:, :, :], ALU.mult).then_inc(qd_ready[s], 1)
                    for s in range(2):
                        wait_turn(pool, oss_ready[s], i + 1, pool_turns)
                        pool_rsqrt(pool, ors[s][:, :], oss[s][:, :], P, half[:, 0:H]).then_inc(ors_ready[s], 1)

            @block.tensor
            def _(pe):
                pe.wait_ge(here, 48)
                pe.wait_ge(ones_ready, 1)

                def per_head(out, lhs, rhs):
                    for h in range(H):
                        m = pe.matmul(bank[out][:, h * P:(h + 1) * P], lhs(h), rhs(h), start=True, stop=True)
                    return m

                def prepare(i, s):
                    c = cur[s]
                    pe.wait_ge(src_ready[s], i + 1)
                    if s:
                        pe.wait_ge(banks_read[0], i + 1)
                    pe.matmul(bank[0][:, :], ones[:, :], flat(ug_y[s]), start=True, stop=True)
                    pe.matmul(bank[2][:, 0:4], masks[:, 0, :], bg[s][:, 4:8], start=True, stop=True)
                    pe.matmul(bank[2][:, 4:8], masks[:, 1, :], bg[s][:, 4:8], start=True, stop=True)
                    pe.wait_ge(cur_ready[s], i + 1)
                    for h in range(H):
                        pe.transpose(bank[3][:, h * P:(h + 1) * P], c[:, 4 + h, :], ident[:, :])
                    for h in range(H):
                        pe.transpose(bank[4][:, h * P:(h + 1) * P], c[:, 8 + h, :], ident[:, :])
                    per_head(5, lambda h: c[:, 4 + h, :], lambda h: c[:, 4 + h, :])
                    per_head(6, lambda h: c[:, 4 + h, :], lambda h: c[:, h, :])
                    if s == 0:
                        pe.wait_ge(o_ready[0], i + 1)
                    pe.matmul(bank[1][:, :], ones[:, :], flat(bd_vn[s]), start=True, stop=True).then_inc(pairs_done[s], 1)

                def scan(i, s):
                    pe.wait_ge(w_ready[s], i + 1)
                    pe.wait_ge(qd_ready[s], i + 1)
                    for c in range(2):
                        r = slice(C * c, C * c + C)
                        n = 4 * i + 2 * s + c
                        each = [slice(h * P, (h + 1) * P) for h in range(H)]
                        pe.wait_ge(S_ready, n + 1)
                        for h in range(H):
                            m = pe.matmul(bank[0][r, each[h]], wq[s][:, h, 0, r], S[:, c, h, :], start=True, stop=True)
                        m.then_inc(ws_done, 1)
                        for h in range(H):
                            pe.matmul(bank[O_BANK[s]][r, each[h]], wq[s][:, h, 1, r], S[:, c, h, :], start=(h == 0), stop=False,
                                      skip_group_check=True)
                        pe.wait_ge(vn_ready, n + 1)
                        for h in range(H):
                            m = pe.matmul(bank[4][:, each[h]], kd[s][r, h, :], bd_vn[s][r, h, :], start=True, stop=True)
                        m.then_inc(kv_done, 1)
                        for h in range(H):
                            m = pe.matmul(bank[O_BANK[s]][r, each[h]], qkT[s][r, h, r], bd_vn[s][r, h, :], start=False, stop=True,
                                          skip_group_check=True)
                        m.then_inc(out_done[s], 1)

                with pe.Fori(0, ROUNDS) as i:
                    prepare(i, 0)
                    prepare(i, 1)
                    for l in range(L):
                        for s in range(2):
                            if l == 0 and s == 0:
                                pe.wait_ge(o_ready[1], i + 1)
                            if l:
                                pe.wait_ge(xz_ready[s], L * i + l)
                            pe.wait_ge(tm_ready[s], L * i + l + 1)
                            per_head(Y_BANK[s], lambda h: tm[s][:, h, :],
                                     lambda h: X[s][:, h, :] if l else ident[:, :]).then_inc(y_done[s], 1)
                        if l == 1:
                            pe.wait_ge(banks_read[1], i + 1)
                        for s in range(2):
                            if l:
                                pe.wait_ge(y_ready[s], (L - 1) * i + l)
                                if l < L - 1:
                                    per_head(X_BANK[s], lambda h: Z[s][:, h, :], lambda h: ug_y[s][:, h, :])
                                per_head(Z_BANK[s], lambda h: ug_y[s][:, h, :], lambda h: Z[s][:, h, :]).then_inc(step_done[s], 1)
                    for s in range(2):
                        pe.wait_ge(xz_ready[s], L * i + L)
                        per_head(W_BANK[s], lambda h: wr[s][:, h, :], lambda h: Z[s][:, h, :])
                        per_head(U_BANK[s], lambda h: Z[s][:, h, :], lambda h: vb[s][:, h, :]).then_inc(uw_done[s], 1)
                    for s in range(2):
                        scan(i, s)

            @block.vector
            def _(dve):
                dve.memset(ones[:, :], 1.0)
                dve.memset(S[:, :, :, :], 0.0)
                dve.drain()
                dve.sem_inc(ones_ready, 1)
                dve.sem_inc(S_ready, 1)
                for s in range(2):
                    dve.sem_inc(o_ready[s], 1)
                dve.wait_ge(here, 48)

                def begin(i, s):
                    j = 2 * i + s
                    dve.tensor_copy(bg[s][:, :], gates[:, ds(j, 1), 24:32].rearrange("p a n -> p (a n)"))
                    dve.drain()
                    dve.tensor_tensor(ug_y[s][:, :, :], head(masks[:, 0, :]), col(bg[s][:, 4:8]), ALU.mult)
                    dve.tensor_tensor(bd_vn[s][:, :, :], head(ident[:, :]), col(bg[s][:, 0:4]), ALU.mult)
                    dve.drain()
                    dve.sem_inc(src_ready[s], 1)

                def matrices(i, s):
                    dec, g, e = dec_sq[s], gsm[s], ex[s]
                    dve.wait_ge(pairs_done[s], i + 1)
                    dve.tensor_copy(g[:, 0:4], bank[2][:, 0:4])
                    dve.drain()
                    dve.tensor_tensor(g[:, 4:8], bank[2][:, 4:8], g[:, 0:4], ALU.subtract)
                    dve.tensor_tensor(dec[:, :, :], heads_of(0), col(g[:, 0:4]), ALU.subtract)
                    dve.drain()
                    dve.sem_inc(gsm_ready[s], 1)
                    dve.tensor_scalar(dec[:, :, :], dec[:, :, :], 0.0, None, ALU.min).then_inc(arg_ready[s], 1)
                    dve.wait_ge(ex_ready[s], i + 1)
                    dve.tensor_tensor(e[:, 0:4], e[:, 0:4], bg[s][:, 0:4], ALU.mult)
                    dve.tensor_tensor(kd[s][:, :, :], heads_of(3), col(e[:, 4:8]), ALU.mult)
                    dve.drain()
                    dve.tensor_tensor(wr[s][:, :, :], heads_of(3), col(e[:, 0:4]), ALU.mult)
                    dve.wait_ge(dec_ready[s], i + 1)
                    dve.tensor_tensor(dec[:, :, :], dec[:, :, :], head(masks[:, 0, :]), ALU.mult)
                    dve.drain()
                    dve.tensor_tensor(bm[s][:, :, :], heads_of(5), dec[:, :, :], ALU.mult)
                    dve.tensor_tensor(qkT[s][:, :, :], heads_of(6), dec[:, :, :], ALU.mult)
                    dve.drain()
                    dve.wait_ge(er_ready[s], i + 1)
                    dve.tensor_tensor(flat(bm[s]), flat(bm[s]), bank[1][:, :], ALU.mult).then_inc(mats_ready[s], 1)
                    dve.tensor_tensor(vb[s][:, :, :], heads_of(4), col(bg[s][:, 0:4]), ALU.mult)
                    dve.drain()
                    dve.sem_inc(banks_read[s], 1)

                def scan(i, s):
                    for c in range(2):
                        r = slice(C * c, C * c + C)
                        n = 4 * i + 2 * s + c
                        dve.wait_ge(ws_done, n + 1)
                        dve.tensor_tensor(bd_vn[s][r, :, :], u[s][r, :, :], heads_of(0, r), ALU.subtract).then_inc(vn_ready, 1)
                        dve.tensor_tensor(S[:, 1 - c, :, :], S[:, c, :, :], col(er[s][:, :, C * c + C - 1]), ALU.mult)
                        dve.drain()
                        dve.wait_ge(kv_done, n + 1)
                        dve.tensor_tensor(S[:, 1 - c, :, :], S[:, 1 - c, :, :], heads_of(4), ALU.add).then_inc(S_ready, 1)

                def finish(i, s):
                    dve.wait_ge(ors_ready[s], i + 1)
                    dve.wait_ge(z_here[s], 16 * (i + 1))
                    dve.tensor_tensor(o[s][:, :, :], heads_of(O_BANK[s]), col(ors[s][:, :]), ALU.mult)
                    dve.drain()
                    dve.tensor_tensor(o[s][:, :, :], o[s][:, :, :], head(norm_w[:, :]), ALU.mult)
                    dve.drain()
                    dve.tensor_tensor(o[s][:, :, :], o[s][:, :, :], zt[s][:, :, :], ALU.mult).then_inc(o_ready[s], 1)

                def two_tiles(i, last):
                    matrices(i, 0)
                    matrices(i, 1)
                    for s in range(2):
                        dve.wait_ge(y_done[s], L * i + 1)
                        dve.tensor_tensor(X[s][:, :, :], head(ident[:, :]), heads_of(Y_BANK[s]), ALU.subtract)
                        dve.tensor_tensor(Z[s][:, :, :], head(ident[:, :]), tm[s][:, :, :], ALU.subtract)
                        dve.drain()
                        dve.sem_inc(xz_ready[s], 1)
                    for l in range(1, L):
                        for s in range(2):
                            dve.wait_ge(step_done[s], (L - 1) * i + l)
                            if l < L - 1:
                                dve.tensor_tensor(flat(X[s]), flat(X[s]), bank[X_BANK[s]][:, :], ALU.subtract)
                            dve.tensor_tensor(flat(Z[s]), flat(Z[s]), bank[Z_BANK[s]][:, :], ALU.subtract)
                            dve.drain()
                            dve.sem_inc(xz_ready[s], 1)
                    for s in range(2):
                        dve.wait_ge(uw_done[s], i + 1)
                        dve.tensor_copy(flat(u[s]), bank[U_BANK[s]][:, :])
                    dve.drain()
                    scan(i, 0)
                    scan(i, 1)
                    for s in range(2):
                        dve.wait_ge(sq_ready[s], i + 1)
                        dve.tensor_reduce(oss[s][:, :], dec_sq[s][:, :, :], AX, ALU.add).then_inc(oss_ready[s], 1)
                    if not last:
                        begin(i + 1, 0)
                        begin(i + 1, 1)
                    finish(i, 0)
                    finish(i, 1)

                begin(0, 0)
                begin(0, 1)
                run(dve, two_tiles)


def stage_channels_and_delta(nc, io, scr, xnT, ident, half):
    with nc.sbuf_tensor("gT", [P, GCH, TOKP], F32) as gT:
        stage_channels(nc, io, scr, xnT, gT)
        stage_delta_prompt(nc, io, scr, gT, ident, half)
        stage_delta_sample(nc, io, scr, gT, ident, half)


def stage_prompt_keys(nc, io, scr, ident, wblk, kbias, vbias, ks, kw, kc, vs, vw, vc):
    with Stage(nc, "pk") as st:
        peT = st.sb("peT", [P, 2, 32])
        rows = st.sb("rows", [P, 2, 512])
        wk = st.sb("wk", [P, 2, P])
        cT = st.sb("cT", [P, 2, SEQ])
        turned = [st.ps(f"turned{s}") for s in range(2)]
        acc = [st.ps(f"acc{s}") for s in range(2)]
        bias_k = st.ps("bias_k")
        bias_v = st.ps("bias_v")
        here = [st.sem(f"here{s}") for s in range(2)]
        v_here = st.sem("v_here")
        cleared = st.sem("cleared")
        w_here = st.sem("w_here")
        bias_done = st.sem("bias_done")
        turn_done = st.sem("turn_done")
        taken = st.sem("taken")
        summed = st.sem("summed")
        turns = st.sem("turns")
        with nc.Block() as block:

            @block.sync
            def _(sp):
                def load(t, s):
                    row = ds(t * P, P)
                    sp.dma_start(rows[:, s, :], io["rows"][row, :]).then_inc(here[s], 16)
                    sp.dma_start(wk[:, s, :], io["wrows"][row, 0:P]).then_inc(here[s], 16)

                load(0, 0)
                load(1, 1)
                sp.dma_start(vs[:, :, :], io["rows"][0:SEQ, 384:512].rearrange("(t p) n -> p t n", p=P)).then_inc(v_here, 16)
                sp.dma_start(vw[:, 4:, :], io["wrows"][0:SEQ, 128:256].rearrange("(t p) n -> p t n", p=P)).then_inc(v_here, 16)
                with sp.Fori(0, 3) as i:
                    for s in range(2):
                        wait_turn(sp, turn_done, 2 * i + s + 1, turns)
                        load(2 * i + s + 2, s)
                sp.wait_ge(cleared, 2)
                for half in range(2):
                    r = slice(HD * half, HD * (half + 1))
                    for c in range(2):
                        sp.dma_start(wblk[r, c, :, r], io["cmp_w"][c].rearrange("j d e -> d j e")).then_inc(w_here, 16)
                    sp.dma_start(peT[r, :, :], io["cmp_peT"]).then_inc(w_here, 16)
                sp.wait_ge(v_here, 32)

            @block.tensor
            def _(pe):
                with pe.Fori(0, 4) as i:
                    for s in range(2):
                        pe.wait_ge(here[s], 32 * (i + 1))
                        pe.wait_ge(taken, 2 * i + s + 1)
                        pe.transpose(turned[s][:, 0:P], rows[:, s, 0:P], ident[:, :])
                        pe.transpose(turned[s][:, P:2 * P], rows[:, s, P:2 * P], ident[:, :])
                        pe.transpose(turned[s][:, 2 * P:3 * P], rows[:, s, 2 * P:3 * P], ident[:, :])
                        pe.transpose(turned[s][:, 3 * P:4 * P], wk[:, s, :], ident[:, :]).then_inc(turn_done, 1)
                pe.wait_ge(w_here, 96)
                for j in range(32):
                    pe.matmul(bias_k[:, 0:1], wblk[:, 0, j, :], peT[:, 0, j:j + 1], start=(j == 0), stop=(j == 31))
                for j in range(32):
                    m = pe.matmul(bias_v[:, 0:P], peT[:, 1, j:j + 1].to_broadcast([P, P]), wblk[:, 1, j, :],
                                  start=(j == 0), stop=(j == 31))
                m.then_inc(bias_done, 1)
                pe.wait_ge(taken, 10)
                for j in range(32):
                    pe.matmul(acc[0][:, 0:63], wblk[:, 0, j, :], cT[:, 0, j:j + 16 * 62 + 1:16], start=(j == 0), stop=(j == 31))
                for j in range(32):
                    m = pe.matmul(acc[1][0:63, 0:P], cT[:, 1, j:j + 16 * 62 + 1:16], wblk[:, 1, j, :], start=(j == 0), stop=(j == 31))
                m.then_inc(summed, 1)

            @block.scalar
            def _(act):
                act.sem_inc(taken, 2)
                with act.Fori(0, 4) as i:
                    for s in range(2):
                        t = 2 * i + s
                        act.wait_ge(turn_done, t + 1)
                        act.activation(cT[:, :, ds(t * P, P)], turned[s][:, 0:2 * P].rearrange("p (a n) -> p a n", a=2), ACT.Copy)
                        act.activation(ks[:, ds(t * P, P)], turned[s][:, 2 * P:3 * P], ACT.Copy)
                        act.activation(kw[:, ds(t * P + WIN, P)], turned[s][:, 3 * P:4 * P], ACT.Copy).then_inc(taken, 1)

            @block.gpsimd
            def _(pool):
                pool.memset(wblk[0:HD, :, :, HD:P], 0.0).then_inc(cleared, 1)

            @block.vector
            def _(dve):
                dve.memset(wblk[HD:P, :, :, 0:HD], 0.0).then_inc(cleared, 1)
                dve.memset(kw[:, 0:WIN], 0.0)
                dve.memset(vw[:, 0:4, :], 0.0)
                dve.memset(kc[:, 63:64], 0.0)
                dve.memset(vc[:, :], 0.0)
                dve.wait_ge(bias_done, 1)
                dve.tensor_copy(kbias[:, :], bias_k[:, 0:1])
                dve.tensor_copy(vbias[:, :], bias_v[:, 0:P])
                dve.drain()
                dve.wait_ge(summed, 1)
                dve.tensor_scalar(kc[:, 0:63], acc[0][:, 0:63], kbias[:, 0:1], None, ALU.add)
                dve.tensor_tensor(vc[0:63, :], acc[1][0:63, 0:P], vbias[0:63, :], ALU.add)


def stage_nsa_prompt_attend(nc, io, scr, ident, ks, kw, kc, vs, vw, vc):
    with Stage(nc, "pa") as st:
        qz = st.sb("qz", [P, 2, 8, P])
        qT = st.sb("qT", [P, 2, 2, 8, P])
        key_no = st.sb("key_no", [P, SEQ])
        q_no = st.sb("q_no", [P, 8])
        qn = st.sb("qn", [P, 1])
        gates = st.sb("gates", [P, 2, 32])
        bonus = st.sb("bonus", [P, 16])
        ok = st.sb("ok", [P, 64])
        okb = st.sb("okb", [P, 64])
        wbias = st.sb("wbias", [P, 2, 640])
        sc = st.sb("sc", [P, 8, 64])
        mx = st.sb("mx", [P, 8])
        sm = st.sb("sm", [P, 8])
        pg = st.sb("pg", [P, 2, 64])
        pp = st.sb("pp", [P, 2, 68])
        imp = st.sb("imp", [P, 2, 16])
        top = st.sb("top", [P, 2, 8])
        rep = st.sb("rep", [P, 2, 16])
        cm = st.sb("cm", [P, SEQ])
        mk = st.sb("mk", [P, 2, 2, SEQ])
        s_sel = st.sb("s_sel", [P, 2, SEQ])
        s_win = st.sb("s_win", [P, 2, 640])
        hm = st.sb("hm", [P, 8, 2])
        sums = st.sb("sums", [P, 8, 2])
        pT = st.sb("pT", [P, 2, 512])
        pcT = st.sb("pcT", [64, 2, 8, P])
        o = st.sb("o", [P, 2, 8, HD])
        psel = st.ps("psel", [P, 1024])
        pwin = st.ps("pwin", [P, 1024])
        pt = [st.ps(f"pt{k}") for k in range(2)]
        pcmp = st.ps("pcmp")
        po = st.ps("po")

        const_here = st.sem("const_here")
        q_here = st.sem("q_here")
        ok_here = st.sem("ok_here")
        late_here = [st.sem(f"late_here{k}") for k in range(2)]
        front_done = st.sem("front_done")
        turned = st.sem("turned")
        turned_read = st.sem("turned_read")
        cs_done = st.sem("cs_done")
        carg_ready = st.sem("carg_ready")
        cexp_done = st.sem("cexp_done")
        p_ready = st.sem("p_ready")
        imp_ready = st.sem("imp_ready")
        rep_ready = st.sem("rep_ready")
        mk_ready = st.sem("mk_ready")
        cm_ready = st.sem("cm_ready")
        pool_turns = st.sem("pool_turns")
        qk_done = st.sem("qk_done")
        taken = st.sem("taken")
        exp_done = st.sem("exp_done")
        wexp_done = st.sem("wexp_done")
        t_done = [st.sem(f"t_done{k}") for k in range(2)]
        t_ready = [st.sem(f"t_ready{k}") for k in range(2)]
        t_used = [st.sem(f"t_used{k}") for k in range(2)]
        dve_turns = st.sem("dve_turns")
        pe_turns = st.sem("pe_turns")
        o_taken = st.sem("o_taken")
        block_done = st.sem("block_done")
        o_out = st.sem("o_out")
        turns = st.sem("turns")

        ROUNDS = {False: [("s", 0, 4), ("w", 1, 5)],
                  True: [("s", 0, 4), ("s", 4, 8), ("w", 0, 4), ("w", 4, 5)]}

        def turns_before(n, wide):
            return 2 * n - 32 if wide else n

        def span(h, p, wide):
            return (SEQ, 0) if wide or (h == 0 and p == 0) else (SEQ // 2, P)

        def run(eng, pair):
            with eng.Fori(0, 2) as i:
                pair(i, False, False)
            pair(2, True, False)
            pair(3, True, True)

        def heads(i, wide, last):
            for p in range(2):
                b = 2 * i + p
                for h in range(8):
                    nxt = None
                    if h < 7:
                        nxt = (b, p, h + 1, 8 * b + h + 1)
                    elif not (last and p == 1):
                        nxt = (b + 1, 1 - p, 0, 8 * b + 8)
                    yield b, p, h, 8 * b + h, nxt, not (last and p == 1)

        with nc.Block() as block:

            @block.sync
            def _(sp):
                def load_q(b):
                    for n, name in enumerate(("qc", "qr")):
                        src = scr[name][ds(b * P, P), :].rearrange("p (h d) -> p h d", d=HD)
                        sp.dma_start(qz[:, n, 0:4, 0:HD], src[:, 0:4, :]).then_inc(q_here, 16)
                        sp.dma_start(qz[:, n, 4:8, HD:P], src[:, 4:8, :]).then_inc(q_here, 16)

                def load_ok(b):
                    sp.dma_start(bonus[:, :], io["blk_bonus"][ds(b * P, P), :]).then_inc(ok_here, 16)
                    sp.dma_start(ok[:, :], io["cmp_ok"][ds(b * P, P), :]).then_inc(ok_here, 16)

                def load_late(b, p):
                    sp.dma_start(gates[:, p, :], scr["misc"][ds(b * P, P), :]).then_inc(late_here[p], 16)
                    sp.dma_start(wbias[:, p, :], io["win_bias"][ds(b, 1), :, :].rearrange("a p n -> p (a n)")).then_inc(late_here[p], 16)

                def step(b, p, more, late):
                    if more:
                        wait_turn(sp, cs_done, b + 1, turns)
                        load_q(b + 1)
                        wait_turn(sp, front_done, b + 1, turns)
                        load_ok(b + 1)
                    wait_turn(sp, block_done, b + 1, turns)
                    sp.dma_start(scr["mix"][ds(b * P, P), 0:512], o[:, p, :, :].rearrange("p a b -> p (a b)")).then_inc(o_out, 16)
                    if late:
                        load_late(b + 2, p)

                sp.dma_start(key_no[:, :], io["key_no"]).then_inc(const_here, 16)
                sp.dma_start(q_no[:, :], io["q_no"]).then_inc(const_here, 16)
                load_ok(0)
                load_late(0, 0)
                load_late(1, 1)
                sp.wait_ge(const_here, 33)
                load_q(0)
                with sp.Fori(0, 3) as i:
                    for p in range(2):
                        step(2 * i + p, p, True, True)
                step(6, 0, True, False)
                step(7, 1, False, False)
                sp.wait_ge(o_out, 16 * 10)

            @block.tensor
            def _(pe):
                def scores(b, p, h, wide):
                    q = qT[:, p, 1, h, :]
                    keys, skip = span(h, p, wide)
                    for k in range(0, keys, 512):
                        pe.matmul(psel[:, k:k + 512], q, ks[:, k:k + 512], start=True, stop=True)
                    if skip:
                        m = pe.matmul(pwin[:, 0:512], q, kw[:, ds(b * P + P, 512)], start=True, stop=True)
                    else:
                        pe.matmul(pwin[:, 0:512], q, kw[:, ds(b * P, 512)], start=True, stop=True)
                        m = pe.matmul(pwin[:, 512:640], q, kw[:, ds(b * P + 512, P)], start=True, stop=True)
                    m.then_inc(qk_done, 1)

                def front(f, fp, step):
                    if step < 4:
                        if step == 0:
                            pe.wait_ge(q_here, 64 * (f + 1))
                        wait_turn(pe, turned_read, 6 * f + step + 1, pe_turns)
                        for h in range(4):
                            t = pe.transpose(pcmp[:, h * P:(h + 1) * P], qz[:, step // 2, 4 * (step % 2) + h, :], ident[:, :])
                        t.then_inc(turned, 1)
                    elif step == 4:
                        pe.wait_ge(turned_read, 6 * f + 5)
                        for h in range(8):
                            m = pe.matmul(pcmp[:, h * 64:(h + 1) * 64], qT[:, fp, 0, h, :], kc[:, :], start=True, stop=True)
                        m.then_inc(cs_done, 1)
                    elif step >= 6:
                        if step == 6:
                            wait_turn(pe, p_ready, f + 1, pe_turns)
                        else:
                            wait_turn(pe, turned_read, 6 * f + 6, pe_turns)
                        for h in range(4):
                            t = pe.transpose(pcmp[0:64, h * P:(h + 1) * P], sc[:, 4 * (step - 6) + h, :], ident[:, :])
                        t.then_inc(turned, 1)

                def pair(i, wide, last):
                    for b, p, h, n, nxt, fronts in heads(i, wide, last):
                        before = turns_before(n, wide)

                        def turn(r):
                            what, lo, hi = ROUNDS[wide][r]
                            shift = span(h, p, wide)[1] // P if what == "w" else 0
                            src = (s_sel if what == "s" else s_win)[:, h % 2]
                            for k in range(lo, hi):
                                c = k - shift
                                t = pe.transpose(pt[r % 2][:, (k - lo) * P:(k - lo + 1) * P], src[:, c * P:(c + 1) * P], ident[:, :])
                            t.then_inc(t_done[r % 2], 1)

                        def use(r):
                            what, lo, hi = ROUNDS[wide][r]
                            pe.wait_ge(t_ready[r % 2], before + r // 2 + 1)
                            first, end = (0, 8 if wide else 4) if what == "s" else (0 if wide else 1, 5)
                            for k in range(lo, hi):
                                v, c = (vs[:, k, :], 128) if what == "s" else (vw[:, ds(b + k, 1), :].rearrange("p a n -> p (a n)"), 256)
                                m = pe.matmul(po[:, c:c + P], pT[:, r % 2, (k - lo) * P:(k - lo + 1) * P], v,
                                              start=(k == first), stop=(k == end - 1))
                            m.then_inc(t_used[r % 2], 1)

                        pe.wait_ge(exp_done, n + 1)
                        turn(0)
                        if not wide:
                            pe.wait_ge(wexp_done, n + 1)
                        turn(1)
                        if nxt:
                            scores(*nxt[:3], wide)
                        if h == 0:
                            wait_turn(pe, turned_read, 6 * b + 7, pe_turns)
                        pe.wait_ge(o_taken, n + 1)
                        pe.matmul(po[:, 0:P], pcT[:, p, h, :], vc[:, :], start=True, stop=True)
                        use(0)
                        if wide:
                            pe.wait_ge(wexp_done, n + 1)
                            turn(2)
                        use(1)
                        if fronts:
                            front(b + 1, 1 - p, h)
                        if wide:
                            turn(3)
                            use(2)
                            use(3)

                for step in range(8):
                    front(0, 0, step)
                scores(0, 0, 0, True)
                run(pe, pair)

            @block.scalar
            def _(act):
                def exps(b, p, h, n, wide):
                    keys, skip = span(h, p, wide)
                    act.wait_ge(taken, n + 1)
                    act.activation(s_sel[:, h % 2, 0:keys], s_sel[:, h % 2, 0:keys], ACT.Exp, bias=hm[:, h, 0:1],
                                   accum_out=sums[:, h, 0:1]).then_inc(exp_done, 1)
                    act.activation(s_win[:, h % 2, 0:640 - skip], s_win[:, h % 2, 0:640 - skip], ACT.Exp, bias=hm[:, h, 1:2],
                                   accum_out=sums[:, h, 1:2]).then_inc(wexp_done, 1)

                def front(f, fp, step):
                    if step == 5:
                        act.wait_ge(carg_ready, f + 1)
                        act.activation(sc[:, :, :], sc[:, :, :], ACT.Exp).then_inc(cexp_done, 1)
                    elif step < 4:
                        act.wait_ge(turned, 6 * f + step + 1)
                        k = 4 * (step % 2)
                        act.activation(qT[:, fp, step // 2, k:k + 4].rearrange("p a b -> p (a b)"), pcmp[:, :], ACT.Copy,
                                       scale=HD ** -0.5).then_inc(turned_read, 1)
                    elif step >= 6:
                        act.wait_ge(turned, 6 * f + step - 1)
                        k = 4 * (step - 6)
                        act.activation(pcT[:, fp, k:k + 4, :].rearrange("p a b -> p (a b)"), pcmp[0:64, :], ACT.Copy).then_inc(turned_read, 1)

                def pair(i, wide, last):
                    for b, p, h, n, nxt, fronts in heads(i, wide, last):
                        before = turns_before(n, wide)
                        for r in (0, 2) if wide else (0,):
                            act.wait_ge(t_done[0], before + r // 2 + 1)
                            act.wait_ge(t_used[0], before + r // 2 + 1)
                            act.activation(pT[:, 0, :], pt[0][:, :], ACT.Copy).then_inc(t_ready[0], 1)
                            if r == 0 and fronts and h == 5:
                                front(b + 1, 1 - p, h)
                        if nxt:
                            exps(*nxt, wide)
                        if fronts and h != 5:
                            front(b + 1, 1 - p, h)

                act.sem_inc(turned_read, 1)
                for step in range(8):
                    front(0, 0, step)
                exps(0, 0, 0, 0, True)
                run(act, pair)

            @block.gpsimd
            def _(pool):
                def front(f, fp):
                    wait_turn(pool, p_ready, f + 1, pool_turns)
                    p4 = sc[:, :, :].rearrange("p (k g) n -> p k g n", k=2)
                    pool.tensor_tensor(pg[:, :, :], p4[:, :, 0, :], p4[:, :, 1, :], ALU.add)
                    pool.drain()
                    pool.tensor_tensor(pg[:, :, :], pg[:, :, :], p4[:, :, 2, :], ALU.add)
                    pool.drain()
                    pool.tensor_tensor(pp[:, :, 1:65], pg[:, :, :], p4[:, :, 3, :], ALU.add)
                    pool.drain()
                    at = lambda k: pp[:, :, k:k + 61:4]
                    pool.tensor_tensor(imp[:, :, :], at(0), at(1), ALU.add)
                    for k in (2, 3, 4):
                        pool.drain()
                        pool.tensor_tensor(imp[:, :, :], imp[:, :, :], at(k), ALU.add)
                    pool.drain()
                    pool.tensor_tensor(imp[:, :, :], imp[:, :, :], bonus[:, :].unsqueeze(1).to_broadcast([P, 2, 16]), ALU.add).then_inc(imp_ready, 1)
                    wait_turn(pool, rep_ready, f + 1, pool_turns)
                    wait_turn(pool, cm_ready, f + 1, pool_turns)
                    for k in range(2):
                        pool.tensor_tensor(mk[:, fp, k, :].rearrange("p (s n) -> p s n", n=64), cm[:, :].rearrange("p (s n) -> p s n", n=64),
                                           rep[:, k, :].unsqueeze(2).to_broadcast([P, 16, 64]), ALU.add)
                    pool.drain()
                    pool.sem_inc(mk_ready, 1)
                    pool.sem_inc(front_done, 1)

                pool.wait_ge(const_here, 33)
                with pool.Fori(0, 4) as i:
                    for fp in range(2):
                        front(2 * i + fp, fp)

            @block.vector
            def _(dve):
                h8 = lambda ap: ap.unsqueeze(1).to_broadcast([P, 8, 64])
                c8 = lambda ap: ap.unsqueeze(2).to_broadcast([P, 8, 64])

                def take(b, p, h, n, wide):
                    keys, skip = span(h, p, wide)
                    if h == 0:
                        wait_turn(dve, late_here[p], 16 * (b - p) + 32, dve_turns)
                        wait_turn(dve, mk_ready, b + 1, dve_turns)
                    wait_turn(dve, qk_done, n + 1, dve_turns)
                    dve.tensor_tensor_reduce(s_sel[:, h % 2, 0:keys], psel[:, 0:keys], mk[:, p, h // 4, 0:keys], 1.0, NEG, ALU.add,
                                             ALU.max, hm[:, h, 0:1])
                    dve.tensor_tensor_reduce(s_win[:, h % 2, 0:640 - skip], pwin[:, 0:640 - skip], wbias[:, p, skip:640], 1.0, NEG,
                                             ALU.add, ALU.max, hm[:, h, 1:2])
                    dve.drain()
                    dve.tensor_scalar(hm[:, h, :], hm[:, h, :], -1.0, None, ALU.mult).then_inc(taken, 1)

                def front(f, fp, step):
                    if step == 3:
                        dve.wait_ge(ok_here, 32 * (f + 1))
                        dve.tensor_scalar(okb[:, :], ok[:, :], 1.0, -NEG, ALU.subtract, ALU.mult)
                        dve.tensor_copy(qn[:, :], q_no[:, ds(f, 1)])
                        dve.drain()
                        dve.tensor_scalar(cm[:, :], key_no[:, :], qn[:, 0:1], NEG, ALU.is_gt, ALU.mult).then_inc(cm_ready, 1)
                    elif step == 4:
                        dve.wait_ge(cs_done, f + 1)
                        dve.tensor_tensor(sc[:, :, :], pcmp[:, :].rearrange("p (a b) -> p a b", a=8), h8(okb[:, :]), ALU.add)
                        dve.drain()
                        dve.tensor_reduce(mx[:, :], sc[:, :, :], AX, ALU.max)
                        dve.drain()
                        dve.tensor_tensor(sc[:, :, :], sc[:, :, :], c8(mx[:, :]), ALU.subtract).then_inc(carg_ready, 1)
                    elif step == 5:
                        dve.wait_ge(cexp_done, f + 1)
                        dve.tensor_tensor(sc[:, :, :], sc[:, :, :], h8(ok[:, :]), ALU.mult)
                        dve.drain()
                        dve.tensor_reduce(sm[:, :], sc[:, :, :], AX, ALU.add)
                        dve.drain()
                        dve.tensor_scalar(sm[:, :], sm[:, :], 1e-30, None, ALU.max)
                        dve.drain()
                        dve.reciprocal(sm[:, :], sm[:, :])
                        dve.drain()
                        dve.tensor_tensor(sc[:, :, :], sc[:, :, :], c8(sm[:, :]), ALU.mult).then_inc(p_ready, 1)
                    elif step == 6:
                        wait_turn(dve, imp_ready, f + 1, dve_turns)
                        for k in range(2):
                            dve.max(top[:, k, :], imp[:, k, :])
                        dve.drain()
                        for k in range(2):
                            dve.match_replace(rep[:, k, :], top[:, k, :], imp[:, k, :], 3 * NEG)
                        dve.drain()
                        dve.tensor_scalar(rep[:, :, :], rep[:, :, :], 3 * NEG, NEG, ALU.not_equal, ALU.mult).then_inc(rep_ready, 1)

                def pair(i, wide, last):
                    for b, p, h, n, nxt, fronts in heads(i, wide, last):
                        before = turns_before(n, wide)
                        for r in (1, 3) if wide else (1,):
                            w = P if r == 3 else 512
                            if r == 3 and nxt:
                                take(*nxt, wide)
                            dve.wait_ge(t_done[1], before + r // 2 + 1)
                            dve.wait_ge(t_used[1], before + r // 2 + 1)
                            dve.tensor_copy(pT[:, 1, 0:w], pt[1][:, 0:w]).then_inc(t_ready[1], 1)
                        if not wide:
                            take(*nxt, wide)
                        dve.wait_ge(t_used[1], before + (3 if wide else 2))
                        if h == 0:
                            wait_turn(dve, o_out, 16 * b + 16, dve_turns)
                        c = HD * (h // 4)
                        dve.tensor_scalar(sums[:, h, :], sums[:, h, :], 1e-30, None, ALU.max)
                        dve.tensor_scalar(o[:, p, h, :], po[:, c:c + HD], gates[:, p, 3 * h:3 * h + 1], None, ALU.mult)
                        dve.drain()
                        dve.reciprocal(sums[:, h, :], sums[:, h, :])
                        dve.drain()
                        dve.tensor_tensor(sums[:, h, :], sums[:, h, :], gates[:, p, 3 * h + 1:3 * h + 3], ALU.mult)
                        dve.drain()
                        dve.scalar_tensor_tensor(o[:, p, h, :], po[:, P + c:P + c + HD], sums[:, h, 0:1], o[:, p, h, :], ALU.mult, ALU.add)
                        dve.drain()
                        dve.scalar_tensor_tensor(o[:, p, h, :], po[:, 2 * P + c:2 * P + c + HD], sums[:, h, 1:2], o[:, p, h, :],
                                                 ALU.mult, ALU.add).then_inc(o_taken, 1)
                        if fronts:
                            front(b + 1, 1 - p, h)
                        if h == 7:
                            dve.drain()
                            dve.sem_inc(block_done, 1)

                dve.memset(qz[:, :, :, :], 0.0)
                dve.memset(pp[:, :, :], 0.0)
                dve.drain()
                dve.sem_inc(const_here, 1)
                dve.sem_inc(o_taken, 1)
                dve.sem_inc(o_out, 32)
                dve.sem_inc(t_used[0], 1)
                dve.sem_inc(t_used[1], 1)
                dve.wait_ge(const_here, 33)
                for step in range(8):
                    front(0, 0, step)
                take(0, 0, 0, 0, True)
                run(dve, pair)


def stage_nsa_prompt(nc, io, scr, ident, kbias, vbias):
    with ExitStack() as ctx:
        def sb(name, shape):
            return ctx.enter_context(nc.sbuf_tensor(name, shape, F32))

        wblk = sb("wblk", [P, 2, 32, P])
        ks, kw, kc = sb("ks", [P, SEQ]), sb("kw", [P, SEQ + WIN]), sb("kc", [P, 64])
        vs, vw, vc = sb("vs", [P, 8, P]), sb("vw", [P, 12, P]), sb("vc", [64, P])
        stage_prompt_keys(nc, io, scr, ident, wblk, kbias, vbias, ks, kw, kc, vs, vw, vc)
        stage_nsa_prompt_attend(nc, io, scr, ident, ks, kw, kc, vs, vw, vc)


def stage_nsa(nc, io, scr, ident, half):
    with ExitStack() as ctx:
        def sb(name, shape):
            return ctx.enter_context(nc.sbuf_tensor(name, shape, F32))

        kbias, vbias = sb("kbias", [P, 1]), sb("vbias", [P, P])
        stage_nsa_prompt(nc, io, scr, ident, kbias, vbias)
        stage_nsa_sample_attend(nc, io, scr, ident, kbias, vbias)


def stage_nsa_sample_attend(nc, io, scr, ident, kbias, vbias):
    G = 4
    NS = NPAGE // G
    with Stage(nc, "ns") as st:
        pages = st.sb("pages", [1, NB * NPAGE], I32)
        pg = st.sb("pg", [P, NS, G, 512])
        cT = st.sb("cT", [P, 2, 2, PAST // 2])
        wab = st.sb("wab", [P, 2, 8, 2, P])
        second = st.sb("second", [P, 256])
        vT = st.sb("vT", [P, 256])
        ksT = st.sb("ksT", [P, 2, 512])
        vs2 = st.sb("vs2", [P, 2, NPAGE, P])
        ssel = st.sb("ssel", [P, PAST + NT])
        kcmp = st.sb("kcmp", [P, 256])
        vcmp = st.sb("vcmp", [P, 2, 2, P])
        win = st.sb("win", [P, 2, 4, 256])
        new = st.sb("new", [NT, 2, 4, P])
        kwT = st.sb("kwT", [P, WIN])
        knT = st.sb("knT", [P, 2 * NT])
        qz = st.sb("qz", [P, 2, P])
        qT = st.sb("qT", [P, 2, P])
        gates = st.sb("gates", [P, 4, 3])
        gate = st.sb("gate", [P, 3])
        gsum = st.sb("gsum", [P, P])
        bonus = st.sb("bonus", [P, 65])
        newb = st.sb("newb", [P, NT])
        winb = st.sb("winb", [P, WIN + NT])
        pc = st.sb("pc", [P, 256])
        swin = st.sb("swin", [P, WIN + NT])
        pp = st.sb("pp", [P, 264])
        imp = st.sb("imp", [P, 65])
        top = st.sb("top", [P, 8])
        rep = st.sb("rep", [P, 65])
        mx = st.sb("mx", [P, 8])
        sums = st.sb("sums", [P, 3])
        parts = st.sb("parts", [P, 4])
        pT = st.sb("pT", [P, 2, 512])
        o = st.sb("o", [P, HD])
        bank = [st.ps(f"b{k}") for k in range(8)]

        const_here = st.sem("const_here")
        copied = st.sem("copied")
        q_here = st.sem("q_here")
        gates_here = st.sem("gates_here")
        turns_dve = st.sem("turns_dve")
        win_here = st.sem("win_here")
        here = [st.sem(f"here{s}") for s in range(NS)]
        t_done = [st.sem(f"t_done{s}") for s in range(NS)]
        v_kept = [st.sem(f"v_kept{s}") for s in range(NS)]
        c_kept = [st.sem(f"c_kept{s}") for s in range(NS)]
        ks_ready = [st.sem(f"ks_ready{s}") for s in range(NS)]
        sc_done = [st.sem(f"sc_done{s}") for s in range(NS)]
        sc_kept = [st.sem(f"sc_kept{s}") for s in range(NS)]
        qt_done = st.sem("qt_done")
        q_ready = st.sem("q_ready")
        cmp_done = st.sem("cmp_done")
        cmp_ready = st.sem("cmp_ready")
        kc_done = st.sem("kc_done")
        v_ready = st.sem("v_ready")
        vt_ready = st.sem("vt_ready")
        v_turned = st.sem("v_turned")
        wab_here = st.sem("wab_here")
        wab_ready = st.sem("wab_ready")
        wt_done = st.sem("wt_done")
        wt_ready = st.sem("wt_ready")
        ws_done = st.sem("ws_done")
        batch_kept = st.sem("batch_kept")
        carg_ready = st.sem("carg_ready")
        cexp_done = st.sem("cexp_done")
        p_ready = st.sem("p_ready")
        imp_done = st.sem("imp_done")
        arg_ready = st.sem("arg_ready")
        exp_done = st.sem("exp_done")
        r_done = st.sem("r_done")
        r_ready = [st.sem(f"r_ready{s}") for s in range(2)]
        pv_done = st.sem("pv_done")
        o_ready = st.sem("o_ready")
        o_out = st.sem("o_out")
        turns = st.sem("turns")
        pe_turns = st.sem("pe_turns")
        turns_pool = st.sem("turns_pool")
        imp_kept = st.sem("imp_kept")
        banks_read = st.sem("banks_read")
        NR = 11
        ROUNDS = [("c", 0, 2)] + [("s", 4 * k, 4) for k in range(8)] + [("w", 0, 4), ("n", 0, 2)]

        with nc.Block() as block:

            @block.sync
            def _(sp):
                for dst, name in ((gsum, "gsum"), (bonus, "samp_bonus"), (newb, "samp_new"), (winb, "samp_win"), (pages, "pages")):
                    sp.dma_start(dst[:, :], io[name]).then_inc(const_here, 16)
                sp.wait_ge(const_here, 81)

                def tokens(bp, b2):
                    return ds(bp * 2 * NT + (SEQ + b2 * NT), NT)

                def load_q(bp):
                    for b2 in range(2):
                        for kv in range(2):
                            r = slice(64 * b2 + 32 * kv, 64 * b2 + 32 * kv + 32)
                            for n, name in enumerate(("qc", "qr")):
                                src = scr[name][tokens(bp, b2), 256 * kv:256 * (kv + 1)].rearrange("t (g d) -> g t d", g=4)
                                sp.dma_start(qz[r, n, HD * kv:HD * (kv + 1)], src).then_inc(q_here, 16)

                def load_win(bp):
                    for b2 in range(2):
                        sp.dma_start(win[:, b2, :, :], io["cache_win"][ds(bp * 2 + b2, 1), :, :]
                                     .rearrange("a (t p) n -> p (a t) n", p=P)).then_inc(win_here, 16)
                        sp.dma_start(new[:, b2, 0:2, :], io["rows"][tokens(bp, b2), 256:512].rearrange("p (a n) -> p a n", a=2)).then_inc(win_here, 16)
                        sp.dma_start(new[:, b2, 2:4, :], io["wrows"][tokens(bp, b2), :].rearrange("p (a n) -> p a n", a=2)).then_inc(win_here, 16)

                def load_pages(bp, b2):
                    n = bp * 2 + b2
                    for s in range(NS):
                        wait_turn(sp, t_done[s], n + 1, turns)
                        wait_turn(sp, v_kept[s], n + 1, turns)
                        for k in range(G):
                            at = bp * 2 * NPAGE + (b2 * NPAGE + s * G + k)
                            page = sp.value_load(pages[0:1, ds(at, 1)], min_val=0, max_val=POOL - 1)
                            sp.dma_start(pg[:, s, k, :], io["cache_kv"][ds(page, 1), :, :]
                                         .rearrange("a p n -> p (a n)")).then_inc(here[s], 16)

                def pair(bp, last):
                    if not last:
                        wait_turn(sp, qt_done, bp + 1, turns)
                        load_q(bp + 1)
                    load_pages(bp, 1)
                    if not last:
                        load_pages(bp + 1, 0)
                    wait_turn(sp, o_ready, bp + 1, turns)
                    for b2 in range(2):
                        for kv in range(2):
                            r = slice(64 * b2 + 32 * kv, 64 * b2 + 32 * kv + 32)
                            sp.dma_start(scr["mix"][tokens(bp, b2), 256 * kv:256 * (kv + 1)].rearrange("t (g d) -> g t d", g=4), o[r, :]).then_inc(o_out, 16)
                    if not last:
                        load_win(bp + 1)

                load_q(0)
                load_pages(0, 0)
                for c in range(2):
                    w_v = io["cmp_w"][c].rearrange("(r p q) d e -> q r d p e", r=2, q=2)
                    for q in range(2):
                        for run in range(2):
                            sp.dma_start(wab[HD * q:HD * (q + 1), c, :, 0, HD * run:HD * (run + 1)], w_v[q, run]).then_inc(wab_here, 16)
                load_win(0)
                with sp.Fori(0, 3) as bp:
                    pair(bp, False)
                pair(3, True)
                sp.wait_ge(o_out, 64 * 5)
                sp.wait_ge(copied, 256)

            @block.gpsimd
            def _(pool):
                def swap():
                    pool.wait_ge(wab_here, 128)
                    pool.tensor_copy(wab[:, :, :, 1, 0:HD], wab[:, :, :, 0, HD:P])
                    pool.tensor_copy(wab[:, :, :, 1, HD:P], wab[:, :, :, 0, 0:HD]).then_inc(wab_ready, 1)

                def pair(bp, later):
                    if later:
                        wait_turn(pool, o_ready, bp, turns_pool)
                    for b2 in range(2):
                        for s in range(NS):
                            n = bp * 2 + b2
                            wait_turn(pool, here[s], n * 64 + 64, turns_pool)
                            pool.tensor_copy(vs2[:, b2, s * G:(s + 1) * G, :], pg[:, s, :, 384:512]).then_inc(v_kept[s], 1)
                        if b2 == 0 and not later:
                            swap()

                pair(0, False)
                with pool.Fori(1, 4) as bp:
                    pair(bp, True)

            @block.scalar
            def _(act):
                for b in range(NB):
                    tok = slice(SEQ + b * NT, SEQ + (b + 1) * NT)
                    r = slice(64 * (b % 2), 64 * (b % 2) + 64)
                    act.dma_start(gates[r, b // 2, :], scr["misc"][tok, 0:24].rearrange("t (h c) -> h t c", c=3)).then_inc(gates_here, 16)
                for b in range(NB):
                    act.dma_start(io["win_s"][b, 0:WIN - NT, :], io["cache_win"][b, NT:WIN, :]).then_inc(copied, 16)
                    act.dma_start(io["win_s"][b, WIN - NT:WIN, :], io["wrows"][SEQ + b * NT:SEQ + (b + 1) * NT, :]).then_inc(copied, 16)
                with act.Fori(0, 4) as bp:
                    act.wait_ge(qt_done, bp + 1)
                    act.activation(qT[:, :, :].rearrange("p a b -> p (a b)"), bank[0][:, 0:256], ACT.Copy, scale=HD ** -0.5).then_inc(q_ready, 1)
                    for b2 in range(2):
                        m = bp * 2 + b2
                        act.wait_ge(cmp_done, m + 1)
                        for s in range(NS):
                            n = bp * 2 + b2
                            act.wait_ge(t_done[s], n + 2)
                            for c in range(2):
                                for kv in range(2):
                                    for q in range(2):
                                        a = act.activation(cT[HD * q:HD * (q + 1), c, kv, 256 * s:256 * (s + 1)],
                                                           bank[4 * (s % 2) + c][HD * kv:HD * (kv + 1), q:512:2], ACT.Copy)
                            a.then_inc(c_kept[s], 1)
                        act.wait_ge(wt_done, m + 1)
                        act.activation(kwT[:, :], bank[4][:, :], ACT.Copy)
                        act.activation(knT[:, :], bank[5][:, 0:2 * NT], ACT.Copy).then_inc(wt_ready, 1)
                    act.wait_ge(carg_ready, bp + 1)
                    act.activation(pc[:, 0:255], pc[:, 0:255], ACT.Exp, bias=mx[:, 0:1], accum_out=sums[:, 0:1]).then_inc(cexp_done, 1)
                    act.wait_ge(arg_ready, bp * 2 + 1)
                    act.activation(swin[:, :], swin[:, :], ACT.Exp, bias=mx[:, 2:3], accum_out=sums[:, 2:3])
                    act.wait_ge(arg_ready, bp * 2 + 2)
                    for k in range(4):
                        part = ssel[:, 1024 * k:1024 * (k + 1) if k < 3 else PAST + NT]
                        act.activation(part, part, ACT.Exp, bias=mx[:, 1:2], accum_out=parts[:, k:k + 1]).then_inc(exp_done, 1)
                    for r in range(1, NR, 2):
                        act.wait_ge(r_done, bp * NR + r + 1)
                        if r >= 2:
                            act.wait_ge(pv_done, bp * NR + r - 1)
                        act.activation(pT[:, 1, :], bank[1][:, :], ACT.Copy).then_inc(r_ready[1], 1)

            @block.tensor
            def _(pe):
                pe.wait_ge(const_here, 81)

                def compress(c):
                    for kv in range(2):
                        for p in range(8):
                            x = pe.matmul(bank[c][:, kv * 256:(kv + 1) * 256], wab[:, c, p, kv, :], cT[:, c, kv, p:PAST // 2:8],
                                          start=(p == 0), stop=(p == 7))
                    return x

                with pe.Fori(0, 4) as bp:
                    pe.wait_ge(q_here, 128 * (bp + 1))
                    pe.transpose(bank[0][:, 0:P], qz[:, 0, :], ident[:, :])
                    pe.transpose(bank[0][:, P:2 * P], qz[:, 1, :], ident[:, :]).then_inc(qt_done, 1)
                    wait_turn(pe, q_ready, bp + 1, pe_turns)
                    wait_turn(pe, banks_read, bp + 1, pe_turns)
                    for b2 in range(2):
                        m = bp * 2 + b2
                        rows = slice(64 * b2, 64 * b2 + 64)
                        n = bp * 2 + b2
                        for s2 in range(0, NS, 2):
                            for s in (s2, s2 + 1):
                                wait_turn(pe, here[s], n * 64 + 64, pe_turns)
                                u, m_u = (s - 2, n + 2) if s >= 2 else (s + NS - 2, n + 1)
                                pe.wait_ge(c_kept[u], m_u)
                                pe.wait_ge(ks_ready[u], m_u)
                                for c in range(3):
                                    for k in range(G):
                                        t = pe.transpose(bank[4 * (s % 2) + c][:, k * P:(k + 1) * P], pg[:, s, k, c * P:(c + 1) * P], ident[:, :])
                                t.then_inc(t_done[s], 1)
                            for s in (s2, s2 + 1):
                                u, m_u = (s - 2, n + 2) if s >= 2 else (s + NS - 2, n + 1)
                                pe.wait_ge(ks_ready[s], n + 2)
                                pe.wait_ge(sc_kept[u], m_u)
                                pe.matmul(bank[4 * (s % 2) + 3][rows, :], qT[:, 1, rows], ksT[:, s % 2, :], start=True, stop=True).then_inc(sc_done[s], 1)
                        for s in range(NS):
                            pe.wait_ge(c_kept[s], bp * 2 + b2 + 2)
                            pe.wait_ge(ks_ready[s], bp * 2 + b2 + 2)
                        pe.wait_ge(wab_ready, 1)
                        compress(0).then_inc(kc_done, 1)
                        wait_turn(pe, win_here, 96 * (bp + 1), pe_turns)
                        for k in range(4):
                            pe.transpose(bank[4][:, k * P:(k + 1) * P], win[:, b2, k, 0:P], ident[:, :])
                        pe.transpose(bank[5][:, 0:NT], new[:, b2, 2, :], ident[0:NT, 0:NT])
                        pe.transpose(bank[5][:, NT:2 * NT], new[:, b2, 0, :], ident[0:NT, 0:NT]).then_inc(wt_done, 1)
                        pe.wait_ge(cmp_ready, m + 1)
                        pe.matmul(bank[2][rows, 0:256], qT[:, 0, rows], kcmp[:, :], start=True, stop=True)
                        pe.wait_ge(wt_ready, m + 1)
                        pe.matmul(bank[6][rows, :], qT[:, 1, rows], kwT[:, :], start=True, stop=True)
                        pe.matmul(bank[5][rows, 0:2 * NT], qT[:, 1, rows], knT[:, :], start=True, stop=True).then_inc(ws_done, 1)
                        compress(1).then_inc(cmp_done, 1)
                        if b2 == 1:
                            wait_turn(pe, p_ready, bp + 1, pe_turns)
                            pe.matmul(bank[0][:, 0:255], gsum[:, :], pc[:, 0:255], start=True, stop=True).then_inc(imp_done, 1)
                        wait_turn(pe, vt_ready, m + 1, pe_turns)
                        pe.transpose(bank[7][:, 0:P], vT[:, 0:P], ident[:, :])
                        pe.transpose(bank[7][0:P - 1, P:2 * P], vT[:, P:2 * P - 1], ident[:, :]).then_inc(v_turned, 1)
                        wait_turn(pe, batch_kept, m + 1, pe_turns)
                        if b2 == 0:
                            wait_turn(pe, v_ready, m + 1, pe_turns)
                    pe.wait_ge(imp_kept, bp + 1)

                    def turn(r):
                        what, at, k = ROUNDS[r]
                        src = {"c": pc, "s": ssel, "w": swin, "n": None}[what]
                        if what == "n":
                            pe.transpose(bank[r % 2][0:NT, 0:P], ssel[:, PAST:PAST + NT], ident[:, :])
                            t = pe.transpose(bank[r % 2][0:NT, P:2 * P], swin[:, WIN:WIN + NT], ident[:, :])
                        else:
                            for x in range(k):
                                t = pe.transpose(bank[r % 2][:, x * P:(x + 1) * P], src[:, (at + x) * P:(at + x + 1) * P], ident[:, :])
                        t.then_inc(r_done, 1)

                    def use(r):
                        what, at, k = ROUNDS[r]
                        pe.wait_ge(r_ready[r % 2], bp * (6 - r % 2) + r // 2 + 1)
                        for b2 in range(2):
                            rows = slice(64 * b2, 64 * b2 + 64)
                            for x in range(k):
                                p = pT[:, r % 2, x * P + 64 * b2:x * P + 64 * b2 + 64]
                                if what == "c":
                                    mm = pe.matmul(bank[2][rows, 0:P], p, vcmp[:, b2, x, :], start=(x == 0), stop=(x == 1))
                                elif what == "s":
                                    mm = pe.matmul(bank[3][rows, 0:P], p, vs2[:, b2, at + x, :], start=(at + x == 0), stop=False, skip_group_check=True)
                                elif what == "w":
                                    mm = pe.matmul(bank[4][rows, 0:P], p, win[:, b2, x, P:2 * P], start=(x == 0), stop=False, skip_group_check=True)
                                else:
                                    pn = pT[0:NT, r % 2, x * P + 64 * b2:x * P + 64 * b2 + 64]
                                    mm = pe.matmul(bank[3 + x][rows, 0:P], pn, new[:, b2, 1 + 2 * x, :], start=False, stop=True, skip_group_check=True)
                        mm.then_inc(pv_done, 1)

                    turn(0)
                    for s in range(NS):
                        pe.wait_ge(v_kept[s], bp * 2 + 3)
                    wait_turn(pe, v_ready, bp * 2 + 2, pe_turns)
                    for r in range(1, NR):
                        if r >= 2:
                            pe.wait_ge(r_ready[r % 2], bp * (6 - r % 2) + r // 2)
                        if r < 9 and r % 2:
                            wait_turn(pe, exp_done, bp * 4 + r // 2 + 1, pe_turns)
                        turn(r)
                        use(r - 1)
                    use(NR - 1)

            @block.vector
            def _(dve):
                dve.memset(qz[:, :, :], 0.0)
                dve.memset(pp[:, :], 0.0)
                dve.memset(pc[:, :], 0.0)
                dve.memset(kcmp[:, :], 0.0)
                dve.memset(vcmp[:, :, :, :], 0.0)
                dve.memset(imp[:, :], 0.0)
                dve.drain()
                dve.sem_inc(const_here, 1)
                for s in [cmp_done, banks_read] + t_done + v_kept + c_kept + ks_ready + sc_kept:
                    dve.sem_inc(s, 1)
                def join(dst, c):
                    lo, hi = slice(0, HD), slice(HD, P)
                    dve.tensor_copy(second[lo, 0:255], bank[c][hi, 1:256])
                    dve.tensor_copy(second[hi, 0:255], bank[c][lo, 257:512])
                    dve.drain()
                    dve.tensor_tensor(dst[lo, 0:255], bank[c][lo, 0:255], second[lo, 0:255], ALU.add)
                    dve.tensor_tensor(dst[hi, 0:255], bank[c][hi, 256:511], second[hi, 0:255], ALU.add)
                    dve.drain()

                def join_values(m):
                    dve.wait_ge(cmp_done, m + 2)
                    join(vT, 1)
                    dve.sem_inc(vt_ready, 1)

                def keep_values(m, b2):
                    dve.wait_ge(v_turned, m + 1)
                    dve.tensor_tensor(vcmp[:, b2, 0, :], bank[7][:, 0:P], vbias[:, :], ALU.add)
                    dve.tensor_tensor(vcmp[0:127, b2, 1, :], bank[7][0:127, P:2 * P], vbias[0:127, :], ALU.add)
                    dve.drain()
                    dve.sem_inc(v_ready, 1)

                dve.sem_inc(o_out, 64)
                dve.wait_ge(const_here, 81)
                dve.wait_ge(gates_here, 128)
                with dve.Fori(0, 4) as bp:
                    for b2 in range(2):
                        m = bp * 2 + b2
                        rows = slice(64 * b2, 64 * b2 + 64)
                        n = bp * 2 + b2
                        for s2 in range(0, NS, 2):
                            for s in (s2, s2 + 1):
                                dve.wait_ge(t_done[s], n + 2)
                                dve.tensor_copy(ksT[:, s % 2, :], bank[4 * (s % 2) + 2][:, :]).then_inc(ks_ready[s], 1)
                            for s in (s2, s2 + 1):
                                dve.wait_ge(sc_done[s], n + 1)
                                dve.tensor_copy(ssel[rows, 512 * s:512 * (s + 1)], bank[4 * (s % 2) + 3][rows, :]).then_inc(sc_kept[s], 1)
                        dve.wait_ge(kc_done, m + 1)
                        join(kcmp, 0)
                        dve.tensor_scalar(kcmp[:, 0:255], kcmp[:, 0:255], kbias[:, 0:1], None, ALU.add).then_inc(cmp_ready, 1)
                        dve.wait_ge(ws_done, m + 1)
                        dve.tensor_copy(pc[rows, 0:255], bank[2][rows, 0:255])
                        dve.tensor_tensor(swin[rows, 0:WIN], bank[6][rows, :], winb[rows, 0:WIN], ALU.add)
                        dve.tensor_tensor(swin[rows, WIN:], bank[5][rows, 0:NT], winb[rows, WIN:], ALU.add)
                        dve.tensor_tensor(ssel[rows, PAST:], bank[5][rows, NT:2 * NT], newb[rows, :], ALU.add)
                        dve.drain()
                        dve.sem_inc(batch_kept, 1)
                        if b2 == 0:
                            join_values(m)
                            keep_values(m, 0)
                    dve.tensor_reduce(mx[:, 0:1], pc[:, 0:255], AX, ALU.max)
                    dve.drain()
                    dve.tensor_scalar(mx[:, 0:1], mx[:, 0:1], -1.0, None, ALU.mult).then_inc(carg_ready, 1)
                    dve.tensor_reduce(mx[:, 2:3], swin[:, :], AX, ALU.max)
                    dve.drain()
                    dve.tensor_scalar(mx[:, 2:3], mx[:, 2:3], -1.0, None, ALU.mult).then_inc(arg_ready, 1)
                    dve.wait_ge(cexp_done, bp + 1)
                    dve.tensor_scalar(sums[:, 0:1], sums[:, 0:1], 1e-30, None, ALU.max)
                    dve.drain()
                    dve.reciprocal(sums[:, 0:1], sums[:, 0:1])
                    dve.drain()
                    dve.tensor_scalar(pc[:, 0:255], pc[:, 0:255], sums[:, 0:1], None, ALU.mult).then_inc(p_ready, 1)
                    join_values(bp * 2 + 1)
                    dve.wait_ge(imp_done, bp + 1)
                    dve.tensor_copy(pp[:, 1:256], bank[0][:, 0:255]).then_inc(imp_kept, 1)
                    dve.drain()
                    at = lambda k: pp[:, k:k + 253:4]
                    dve.tensor_tensor(imp[:, 0:64], at(0), at(1), ALU.add)
                    for k in (2, 3, 4):
                        dve.drain()
                        dve.tensor_tensor(imp[:, 0:64], imp[:, 0:64], at(k), ALU.add)
                    dve.drain()
                    dve.tensor_tensor(rep[:, :], imp[:, :], bonus[:, :], ALU.add)
                    dve.drain()
                    dve.max(top[:, :], rep[:, :])
                    dve.drain()
                    dve.match_replace(rep[:, :], top[:, :], rep[:, :], 3 * NEG)
                    dve.drain()
                    dve.tensor_scalar(rep[:, :], rep[:, :], 3 * NEG, None, ALU.not_equal)
                    dve.drain()
                    dve.tensor_scalar(rep[:, :], rep[:, :], NEG, None, ALU.mult)
                    dve.drain()
                    s3 = ssel[:, 0:PAST].rearrange("p (s n) -> p s n", n=64)
                    dve.tensor_tensor_reduce(s3, s3, rep[:, 0:64].unsqueeze(2).to_broadcast([P, 64, 64]), 1.0, NEG, ALU.add, ALU.max,
                                             mx[:, 1:2])
                    dve.tensor_reduce(mx[:, 3:4], ssel[:, PAST:], AX, ALU.max)
                    dve.drain()
                    dve.tensor_scalar(mx[:, 1:2], mx[:, 1:2], mx[:, 3:4], -1.0, ALU.max, ALU.mult).then_inc(arg_ready, 1)
                    keep_values(bp * 2 + 1, 1)
                    for r in range(0, NR, 2):
                        dve.wait_ge(r_done, bp * NR + r + 1)
                        if r >= 2:
                            dve.wait_ge(pv_done, bp * NR + r - 1)
                        what, a, k = ROUNDS[r]
                        if what == "n":
                            dve.tensor_copy(pT[0:NT, 0, 0:2 * P], bank[0][0:NT, 0:2 * P]).then_inc(r_ready[0], 1)
                        else:
                            dve.tensor_copy(pT[:, 0, 0:k * P], bank[0][:, 0:k * P]).then_inc(r_ready[0], 1)
                    dve.wait_ge(exp_done, bp * 4 + 4)
                    dve.tensor_reduce(sums[:, 1:2], parts[:, :], AX, ALU.add)
                    dve.drain()
                    dve.tensor_scalar(sums[:, 1:3], sums[:, 1:3], 1e-30, None, ALU.max)
                    dve.drain()
                    dve.reciprocal(sums[:, 1:3], sums[:, 1:3])
                    dve.drain()
                    dve.tensor_copy(gate[:, :], gates[:, ds(bp, 1), :].rearrange("p a n -> p (a n)"))
                    dve.drain()
                    dve.tensor_tensor(sums[:, 1:3], sums[:, 1:3], gate[:, 1:3], ALU.mult)
                    dve.drain()
                    dve.wait_ge(pv_done, bp * NR + NR)
                    wait_turn(dve, o_out, 64 * (bp + 1), turns_dve)
                    for k, (b, coef) in enumerate(((2, gate), (3, sums), (4, sums))):
                        for q in range(4):
                            r = slice(32 * q, 32 * q + 32)
                            src = bank[b][r, HD * (q % 2):HD * (q % 2) + HD]
                            if k == 0:
                                dve.tensor_scalar(o[r, :], src, coef[r, 0:1], None, ALU.mult)
                            else:
                                dve.scalar_tensor_tensor(o[r, :], src, coef[r, k:k + 1], o[r, :], ALU.mult, ALU.add)
                        dve.drain()
                    dve.sem_inc(o_ready, 1)
                    dve.sem_inc(banks_read, 1)


def stage_mem(nc, io, scr, ident, half, w_out, w_xq):
    with Stage(nc, "mem") as st:
        w = st.sb("w", [P, KD, 2048])
        norm_w = st.sb("norm_w", [P, D])
        k_w = st.sb("k_w", [P, XD])
        x = st.sb("x", [P, D])
        sq = st.sb("sq", [P, D])
        ss = st.sb("ss", [P, 1])
        rstd = st.sb("rstd", [P, 1])
        xn = st.sb("xn", [P, D])
        xT = st.sb("xT", [P, KD, P])
        kv = st.sb("kv", [P, 2048])
        hs = st.sb("hs", [P, XH])
        rs = st.sb("rs", [P, XH])
        zero = st.sb("zero", [TOKP - TOK, 512])
        turned = st.ps("turned", [P, 1024])
        acc = st.ps("acc", [P, 2048])
        w_here = [st.sem(f"w_here{n}") for n in range(2)]
        x_here = st.sem("x_here")
        next_here = st.sem("next_here")
        cleared = st.sem("cleared")
        zero_out = st.sem("zero_out")
        squares = st.sem("squares")
        rstd_ready = st.sem("rstd_ready")
        xn_ready = st.sem("xn_ready")
        turn_done = st.sem("turn_done")
        xT_ready = st.sem("xT_ready")
        projected = st.sem("projected")
        kv_copied = st.sem("kv_copied")
        hs_ready = st.sem("hs_ready")
        rs_ready = st.sem("rs_ready")
        k_ready = st.sem("k_ready")
        out = st.sem("out")

        with nc.Block() as block:

            @block.sync
            def _(sp):
                sp.dma_start(x[:, :], io["mem"][0:P, :]).then_inc(x_here, 16)
                sp.dma_start(norm_w[:, :], io["mem_norm_w"].partition_broadcast(P)).then_inc(x_here, 16)
                for n, name in enumerate(("w_xk", "w_xv")):
                    for k in range(0, KD, 4):
                        sp.dma_start(w[:, k:k + 4, n * D:(n + 1) * D],
                                     io[name].rearrange("(k p) n -> p k n", p=P)[:, k:k + 4, :]).then_inc(w_here[n], 16)
                sp.dma_start(k_w[:, :], io["xk_norm_w"].partition_broadcast(P)).then_inc(w_here[1], 16)
                for dst, name in ((w_out, "w_out"), (w_xq, "w_xq")):
                    for k in range(0, KD, 4):
                        sp.dma_start(dst[:, k:k + 4, :], io[name].rearrange("(k p) n -> p k n", p=P)[:, k:k + 4, :]).then_inc(next_here, 16)
                sp.wait_ge(cleared, 1)
                sp.dma_start(scr["mix"][TOK:TOKP, 0:512], zero[:, :]).then_inc(zero_out, 16)
                sp.wait_ge(xn_ready, 1)
                sp.dma_start(x[:, :], io["mem"][P:2 * P, :]).then_inc(x_here, 16)
                for t in range(2):
                    sp.wait_ge(k_ready, t + 1)
                    sp.dma_start(io["mem_kv"][t * P:(t + 1) * P, :], kv[:, :]).then_inc(out, 16)
                sp.wait_ge(out, 32)
                sp.wait_ge(next_here, 64)
                sp.wait_ge(zero_out, 16)

            @block.scalar
            def _(act):
                for t in range(2):
                    act.wait_ge(x_here, 32 + 16 * t)
                    act.activation(sq[:, :], x[:, :], ACT.Square, accum_out=ss[:, :]).then_inc(squares, 1)
                    act.wait_ge(turn_done, t + 1)
                    act.activation(xT[:, :, :].rearrange("p a b -> p (a b)"), turned[:, :], ACT.Copy).then_inc(xT_ready, 1)
                    act.wait_ge(projected, t + 1)
                    if t:
                        act.wait_ge(out, 16)
                    act.activation(kv[:, :], acc[:, :], ACT.Copy)
                    act.drain()
                    act.activation(sq[:, :], kv[:, 0:D], ACT.Square).then_inc(kv_copied, 1)
                    if t == 0:
                        act.wait_ge(hs_ready, 1)

            @block.gpsimd
            def _(pool):
                for t in range(2):
                    pool.wait_ge(squares, t + 1)
                    pool_rsqrt(pool, rstd[:, :], ss[:, :], D, half[:, 0:1]).then_inc(rstd_ready, 1)
                    pool.wait_ge(hs_ready, t + 1)
                    pool_rsqrt(pool, rs[:, :], hs[:, :], XD, half[:, 0:XH]).then_inc(rs_ready, 1)

            @block.vector
            def _(dve):
                dve.memset(zero[:, :], 0.0).then_inc(cleared, 1)
                for t in range(2):
                    dve.wait_ge(rstd_ready, t + 1)
                    if t:
                        dve.wait_ge(turn_done, t)
                    dve.scalar_tensor_tensor(xn[:, :], x[:, :], rstd[:, 0:1], norm_w[:, :], ALU.mult, ALU.mult).then_inc(xn_ready, 1)
                    dve.wait_ge(kv_copied, t + 1)
                    dve.tensor_reduce(hs[:, :], sq[:, :].rearrange("p (h d) -> p h d", h=XH), AX, ALU.add).then_inc(hs_ready, 1)
                    dve.wait_ge(rs_ready, t + 1)
                    dve.wait_ge(w_here[1], 48)
                    k3 = kv[:, 0:D].rearrange("p (h d) -> p h d", h=XH)
                    dve.tensor_tensor(k3, k3, rs[:, :].unsqueeze(2).to_broadcast([P, XH, XD]), ALU.mult)
                    dve.drain()
                    dve.tensor_tensor(k3, k3, k_w[:, :].unsqueeze(1).to_broadcast([P, XH, XD]), ALU.mult).then_inc(k_ready, 1)

            @block.tensor
            def _(pe):
                for t in range(2):
                    pe.wait_ge(xn_ready, t + 1)
                    for k in range(KD):
                        m = pe.transpose(turned[:, k * P:(k + 1) * P], xn[:, k * P:(k + 1) * P], ident[:, :])
                    m.then_inc(turn_done, 1)
                    pe.wait_ge(xT_ready, t + 1)
                    if t:
                        pe.wait_ge(kv_copied, t)
                    for g in range(4):
                        if t == 0 and g % 2 == 0:
                            pe.wait_ge(w_here[g // 2], 32 + 16 * (g // 2))
                        for k in range(KD):
                            m = pe.matmul(acc[:, g * 512:(g + 1) * 512], xT[:, k, :], w[:, k, g * 512:(g + 1) * 512],
                                          start=(k == 0), stop=(k == KD - 1))
                    m.then_inc(projected, 1)


def stage_rows(nc, io, scr, ident, half, first, w, w2=None, hnT=None):
    name = "mixo" if first else "xo"
    src, resid, nw_name = ("mix", io["x_all"], "xattn_norm_w") if first else ("xo", scr["h1"], "ffn_norm_w")
    with Stage(nc, name) as st:
        norm_w = st.sb("norm_w", [P, D])
        if first:
            q_w = st.sb("q_w", [P, XD])
            q = st.sb("q", [P, D])
            sq2 = st.sb("sq2", [P, D])
            hs = st.sb("hs", [P, XH])
            rs = st.sb("rs", [P, XH])
        else:
            hT = st.sb("hT", [P, KD, P])
        a = st.sb("a", [P, D])
        res = st.sb("res", [P, D])
        aT = st.sb("aT", [P, KD, P])
        h = st.sb("h", [P, D])
        hn = st.sb("hn", [P, D])
        sq = st.sb("sq", [P, D])
        ss = st.sb("ss", [P, 1])
        rstd = st.sb("rstd", [P, 1])
        nT = st.sb("nT", [P, KD, P])
        p_a = st.ps("p_a", [P, 1024])
        p_h = st.ps("p_h", [P, 1024])
        p_n = st.ps("p_n", [P, 1024])
        p_q = st.ps("p_q", [P, 1024])

        w_here = st.sem("w_here")
        a_here = st.sem("a_here")
        res_here = st.sem("res_here")
        a_turned = st.sem("a_turned")
        aT_ready = st.sem("aT_ready")
        h_done = st.sem("h_done")
        h_ready = st.sem("h_ready")
        squares = st.sem("squares")
        rstd_ready = st.sem("rstd_ready")
        hn_ready = st.sem("hn_ready")
        n_turned = st.sem("n_turned")
        nT_ready = st.sem("nT_ready")
        q_done = st.sem("q_done")
        sq2_ready = st.sem("sq2_ready")
        hs_ready = st.sem("hs_ready")
        rs_ready = st.sem("rs_ready")
        q_ready = st.sem("q_ready")
        h_out = st.sem("h_out")
        q_out = st.sem("q_out")
        turns = st.sem("turns")
        pool_turns = st.sem("pool_turns")
        pe_turns = st.sem("pe_turns")

        with nc.Block() as block:

            @block.sync
            def _(sp):
                def load_a(t):
                    sp.dma_start(a[:, :], scr[src][ds(t * P, P), :]).then_inc(a_here, 16)

                def load_res(t):
                    sp.dma_start(res[:, :], resid[ds(t * P, P), :]).then_inc(res_here, 16)

                load_a(0)
                load_res(0)
                sp.dma_start(norm_w[:, :], io[nw_name].partition_broadcast(P)).then_inc(w_here, 16)
                if first:
                    sp.dma_start(q_w[:, :], io["xq_norm_w"].partition_broadcast(P)).then_inc(w_here, 16)

                def store_h(t):
                    wait_turn(sp, h_ready, t + 1, turns)
                    if first:
                        sp.dma_start(scr["h1"][ds(t * P, P), :], h[:, :]).then_inc(h_out, 16)

                def store_q(t):
                    wait_turn(sp, q_ready, t + 1, turns)
                    if first:
                        sp.dma_start(scr["xq"][ds(t * P, P), :], q[:, :]).then_inc(q_out, 16)
                    else:
                        sp.dma_start(scr["h2T"].rearrange("(k p) n -> p k n", p=P)[:, :, ds(t * P, P)], hT[:, :, :]).then_inc(q_out, 16)

                def next_a(t):
                    wait_turn(sp, a_turned, t, turns)
                    load_a(t)

                next_a(1)
                next_a(2)
                store_h(0)
                load_res(1)
                with sp.Fori(2, NTILE - 1) as i:
                    next_a(i + 1)
                    store_h(i - 1)
                    load_res(i)
                    store_q(i - 2)
                store_h(NTILE - 2)
                load_res(NTILE - 1)
                store_q(NTILE - 3)
                store_h(NTILE - 1)
                store_q(NTILE - 2)
                store_q(NTILE - 1)
                if first:
                    sp.wait_ge(h_out, 16 * (NTILE + 1))
                sp.wait_ge(q_out, 16 * (NTILE + 1))

            @block.scalar
            def _(act):
                def take_a(t):
                    act.wait_ge(a_turned, t + 1)
                    act.activation(aT[:, :, :].rearrange("p a b -> p (a b)"), p_a[:, :], ACT.Copy).then_inc(aT_ready, 1)

                def square_h(t):
                    act.wait_ge(h_ready, t + 1)
                    act.activation(sq[:, :], h[:, :], ACT.Square, accum_out=ss[:, :]).then_inc(squares, 1)

                def square_q(t):
                    act.wait_ge(q_done, t + 1)
                    act.activation(sq2[:, :], p_q[:, :], ACT.Square).then_inc(sq2_ready, 1)

                def take_n(t):
                    act.wait_ge(n_turned, t + 1)
                    if first:
                        act.activation(nT[:, :, :].rearrange("p a b -> p (a b)"), p_n[:, :], ACT.Copy).then_inc(nT_ready, 1)
                    else:
                        act.activation(hnT[:, :, ds(t * P, P)], p_n[:, :].rearrange("p (k n) -> p k n", k=KD), ACT.Copy).then_inc(nT_ready, 1)

                def step(i, more):
                    if more:
                        take_a(i + 2)
                    square_h(i + 1)
                    if first:
                        square_q(i)
                        take_n(i + 1)
                    else:
                        take_n(i)

                take_a(0)
                take_a(1)
                square_h(0)
                if first:
                    take_n(0)
                with act.Fori(0, NTILE - 2) as i:
                    step(i, True)
                step(NTILE - 2, False)
                if first:
                    square_q(NTILE - 1)
                else:
                    take_n(NTILE - 1)

            @block.gpsimd
            def _(pool):
                def front(t):
                    wait_turn(pool, squares, t + 1, pool_turns)
                    pool_rsqrt(pool, rstd[:, :], ss[:, :], D, half[:, 0:1]).then_inc(rstd_ready, 1)

                def back(t):
                    if first:
                        wait_turn(pool, hs_ready, t + 1, pool_turns)
                        pool_rsqrt(pool, rs[:, :], hs[:, :], XD, half[:, 0:XH]).then_inc(rs_ready, 1)

                front(0)
                with pool.Fori(0, NTILE - 1) as i:
                    front(i + 1)
                    back(i)
                back(NTILE - 1)

            @block.vector
            def _(dve):
                dve.sem_inc(h_out, 16)
                dve.sem_inc(q_out, 16)
                dve.wait_ge(w_here, 32 if first else 16)

                def front(t, later):
                    dve.wait_ge(h_done, t + 1)
                    dve.wait_ge(res_here, 16 * (t + 1))
                    if first:
                        dve.wait_ge(h_out, 16 * (t + 1))
                    elif later:
                        dve.wait_ge(n_turned, t)
                    dve.tensor_tensor(h[:, :], p_h[:, :], res[:, :], ALU.add).then_inc(h_ready, 1)
                    dve.wait_ge(rstd_ready, t + 1)
                    if later:
                        dve.wait_ge(n_turned, t)
                    dve.scalar_tensor_tensor(hn[:, :], h[:, :], rstd[:, 0:1], norm_w[:, :], ALU.mult, ALU.mult).then_inc(hn_ready, 1)
                    dve.drain()

                def back(t):
                    if first:
                        dve.wait_ge(sq2_ready, t + 1)
                        dve.tensor_reduce(hs[:, :], sq2[:, :].rearrange("p (h d) -> p h d", h=XH), AX, ALU.add).then_inc(hs_ready, 1)
                        dve.wait_ge(rs_ready, t + 1)
                        dve.wait_ge(q_out, 16 * (t + 1))
                        q3 = q[:, :].rearrange("p (h d) -> p h d", h=XH)
                        dve.tensor_tensor(q3, p_q[:, :].rearrange("p (h d) -> p h d", h=XH),
                                          rs[:, :].unsqueeze(2).to_broadcast([P, XH, XD]), ALU.mult)
                        dve.drain()
                        dve.tensor_tensor(q3, q3, q_w[:, :].unsqueeze(1).to_broadcast([P, XH, XD]), ALU.mult)
                    else:
                        dve.wait_ge(n_turned, t + 1)
                        dve.wait_ge(q_out, 16 * (t + 1))
                        dve.tensor_copy(hT[:, :, :].rearrange("p a b -> p (a b)"), p_q[:, :])
                    dve.drain()
                    dve.sem_inc(q_ready, 1)

                front(0, False)
                with dve.Fori(0, NTILE - 1) as i:
                    front(i + 1, True)
                    back(i)
                back(NTILE - 1)

            @block.tensor
            def _(pe):
                def turn_a(t):
                    pe.wait_ge(a_here, 16 * (t + 1))
                    for k in range(KD):
                        m = pe.transpose(p_a[:, k * P:(k + 1) * P], a[:, k * P:(k + 1) * P], ident[:, :])
                    m.then_inc(a_turned, 1)

                def product_h(t, later=True):
                    if later:
                        wait_turn(pe, h_ready, t, pe_turns)
                    pe.wait_ge(aT_ready, t + 1)
                    for g in range(2):
                        for k in range(KD):
                            m = pe.matmul(p_h[:, g * 512:(g + 1) * 512], aT[:, k, :], w[:, k, g * 512:(g + 1) * 512],
                                          start=(k == 0), stop=(k == KD - 1))
                    m.then_inc(h_done, 1)

                def turn_n(t, later):
                    pe.wait_ge(hn_ready, t + 1)
                    if not first:
                        if later:
                            pe.wait_ge(q_ready, t)
                            pe.wait_ge(nT_ready, t)
                        for k in range(KD):
                            pe.transpose(p_q[:, k * P:(k + 1) * P], h[:, k * P:(k + 1) * P], ident[:, :])
                    for k in range(KD):
                        m = pe.transpose(p_n[:, k * P:(k + 1) * P], hn[:, k * P:(k + 1) * P], ident[:, :])
                    m.then_inc(n_turned, 1)

                def product_q(t, later):
                    pe.wait_ge(nT_ready, t + 1)
                    if later:
                        pe.wait_ge(q_ready, t)
                    for g in range(2):
                        for k in range(KD):
                            m = pe.matmul(p_q[:, g * 512:(g + 1) * 512], nT[:, k, :], w2[:, k, g * 512:(g + 1) * 512],
                                          start=(k == 0), stop=(k == KD - 1))
                    m.then_inc(q_done, 1)

                def step(i, more, later):
                    product_h(i + 1)
                    if more:
                        turn_a(i + 2)
                    if first:
                        product_q(i, later)
                        turn_n(i + 1, True)
                    else:
                        turn_n(i, later)

                turn_a(0)
                product_h(0, False)
                turn_a(1)
                if first:
                    turn_n(0, False)
                step(0, True, False)
                with pe.Fori(1, NTILE - 2) as i:
                    step(i, True, True)
                step(NTILE - 2, False, True)
                if first:
                    product_q(NTILE - 1, True)
                else:
                    turn_n(NTILE - 1, True)


def stage_cross_prompt(nc, io, scr, ident, w_xo):
    with Stage(nc, "xp") as st:
        kn = st.sb("kn", [P, 2, D])
        v = st.sb("v", [P, 2, D])
        kT = st.sb("kT", [P, KD, MEM])
        q = st.sb("q", [P, D])
        qT = st.sb("qT", [P, KD, P])
        p = st.sb("p", [P, XH, MEM])
        mx = st.sb("mx", [P, XH])
        sums = st.sb("sums", [P, XH])
        rs = st.sb("rs", [P, XH])
        pT = st.sb("pT", [P, XH, 2, P])
        o = st.sb("o", [P, XH, XD])
        p_q = st.ps("p_q", [P, 1024])
        p_s = st.ps("p_s", [P, 1024])
        p_t = st.ps("p_t", [P, 1024])
        p_o = st.ps("p_o", [P, 1024])
        NQ = SEQ // P
        kv_here = st.sem("kv_here")
        k_turned = st.sem("k_turned")
        k_taken = st.sem("k_taken")
        q_here = st.sem("q_here")
        q_turned = st.sem("q_turned")
        q_ready = st.sem("q_ready")
        s_done = st.sem("s_done")
        mx_ready = st.sem("mx_ready")
        exp_done = st.sem("exp_done")
        p_turned = st.sem("p_turned")
        p_ready = st.sem("p_ready")
        o_done = st.sem("o_done")
        o_ready = st.sem("o_ready")
        o_out = st.sem("o_out")
        turns = st.sem("turns")
        sums_used = st.sem("sums_used")
        next_here = st.sem("next_here")
        o_ready0 = st.sem("o_ready0")

        with nc.Block() as block:

            @block.sync
            def _(sp):
                for t in range(2):
                    rows = io["mem_kv"][t * P:(t + 1) * P, :]
                    sp.dma_start(kn[:, t, :], rows[:, 0:D]).then_inc(kv_here, 16)
                    sp.dma_start(v[:, t, :], rows[:, D:2 * D]).then_inc(kv_here, 16)
                def load_q(t):
                    sp.dma_start(q[:, :], scr["xq"][ds(t * P, P), :]).then_inc(q_here, 16)

                def store_o(t):
                    sp.dma_start(scr["xo"][ds(t * P, P), :], o[:, :, :].rearrange("p a b -> p (a b)")).then_inc(o_out, 16)

                load_q(0)
                sp.wait_ge(q_turned, 1)
                load_q(1)
                for k in range(0, KD, 4):
                    sp.dma_start(w_xo[:, k:k + 4, :], io["w_xo"].rearrange("(k p) n -> p k n", p=P)[:, k:k + 4, :]).then_inc(next_here, 16)
                with sp.Fori(1, NQ - 1) as i:
                    wait_turn(sp, q_turned, i + 1, turns)
                    load_q(i + 1)
                    wait_turn(sp, o_ready, i, turns)
                    store_o(i - 1)
                for t in (NQ - 2, NQ - 1):
                    sp.wait_ge(o_ready, t + 1)
                    store_o(t)
                sp.wait_ge(o_out, 16 * (NQ + 1))
                sp.wait_ge(next_here, 32)

            @block.tensor
            def _(pe):
                pe.wait_ge(kv_here, 64)
                for c in range(KD):
                    for t in range(2):
                        m = pe.transpose((p_q if c < 4 else p_s)[:, (c % 4) * MEM + t * P:(c % 4) * MEM + (t + 1) * P],
                                         kn[:, t, c * P:(c + 1) * P], ident[:, :])
                m.then_inc(k_turned, 1)
                pe.wait_ge(k_taken, 1)

                def turn_q(t):
                    pe.wait_ge(q_here, 16 * (t + 1))
                    for k in range(KD):
                        m = pe.transpose(p_q[:, k * P:(k + 1) * P], q[:, k * P:(k + 1) * P], ident[:, :])
                    m.then_inc(q_turned, 1)

                def scores(t):
                    pe.wait_ge(q_ready, t + 1)
                    for h in range(XH):
                        for c in range(2):
                            m = pe.matmul(p_s[:, h * MEM:(h + 1) * MEM], qT[:, 2 * h + c, :], kT[:, 2 * h + c, :], start=(c == 0), stop=(c == 1))
                    m.then_inc(s_done, 1)

                def turn_p(t):
                    pe.wait_ge(exp_done, t + 1)
                    for h in range(XH):
                        for c in range(2):
                            m = pe.transpose(p_t[:, (2 * h + c) * P:(2 * h + c + 1) * P], p[:, h, c * P:(c + 1) * P], ident[:, :])
                    m.then_inc(p_turned, 1)

                def values(t):
                    pe.wait_ge(p_ready, t + 1)
                    pe.wait_ge(o_ready0, t + 1)
                    for h in range(XH):
                        for c in range(2):
                            m = pe.matmul(p_o[:, h * XD:(h + 1) * XD], pT[:, h, c, :], v[:, c, h * XD:(h + 1) * XD], start=(c == 0), stop=(c == 1))
                    m.then_inc(o_done, 1)

                turn_q(0)
                scores(0)
                turn_q(1)
                turn_p(0)
                with pe.Fori(1, NQ - 1) as i:
                    scores(i)
                    turn_q(i + 1)
                    values(i - 1)
                    turn_p(i)
                scores(NQ - 1)
                values(NQ - 2)
                turn_p(NQ - 1)
                values(NQ - 1)

            @block.scalar
            def _(act):
                act.wait_ge(k_turned, 1)
                act.activation(kT[:, 0:4, :].rearrange("p a b -> p (a b)"), p_q[:, :], ACT.Copy)
                act.activation(kT[:, 4:8, :].rearrange("p a b -> p (a b)"), p_s[:, :], ACT.Copy).then_inc(k_taken, 1)

                def take_q(t):
                    act.wait_ge(q_turned, t + 1)
                    act.activation(qT[:, :, :].rearrange("p a b -> p (a b)"), p_q[:, :], ACT.Copy, scale=XD ** -0.5).then_inc(q_ready, 1)

                def exps(t):
                    act.wait_ge(mx_ready, t + 1)
                    act.wait_ge(sums_used, t + 1)
                    for h in range(XH):
                        a = act.activation(p[:, h, :], p_s[:, h * MEM:(h + 1) * MEM], ACT.Exp, bias=mx[:, h:h + 1], accum_out=sums[:, h:h + 1])
                    a.then_inc(exp_done, 1)

                take_q(0)
                with act.Fori(0, NQ - 1) as i:
                    exps(i)
                    take_q(i + 1)
                exps(NQ - 1)

            @block.vector
            def _(dve):
                dve.sem_inc(o_ready0, 1)
                dve.sem_inc(o_out, 16)

                dve.sem_inc(sums_used, 1)

                def maxima(t):
                    dve.wait_ge(s_done, t + 1)
                    dve.tensor_reduce(mx[:, :], p_s[:, :].rearrange("p (h m) -> p h m", h=XH), AX, ALU.max)
                    dve.drain()
                    dve.tensor_scalar(mx[:, :], mx[:, :], -1.0, None, ALU.mult).then_inc(mx_ready, 1)

                def take_p(t):
                    dve.wait_ge(p_turned, t + 1)
                    dve.tensor_copy(pT[:, :, :, :].rearrange("p a b c -> p (a b c)"), p_t[:, :]).then_inc(p_ready, 1)
                    dve.reciprocal(rs[:, :], sums[:, :]).then_inc(sums_used, 1)
                    dve.drain()

                def outputs(t):
                    dve.wait_ge(o_done, t + 1)
                    dve.wait_ge(o_out, 16 * (t + 1))
                    dve.tensor_tensor(o[:, :, :], p_o[:, :].rearrange("p (h d) -> p h d", h=XH),
                                      rs[:, :].unsqueeze(2).to_broadcast([P, XH, XD]), ALU.mult)
                    dve.drain()
                    dve.sem_inc(o_ready, 1)
                    dve.sem_inc(o_ready0, 1)

                maxima(0)
                with dve.Fori(0, NQ - 1) as i:
                    take_p(i)
                    maxima(i + 1)
                    outputs(i)
                take_p(NQ - 1)
                outputs(NQ - 1)


def stage_cross_sample(nc, io, scr, ident):
    with Stage(nc, "xs") as st:
        kn = st.sb("kn", [P, 2, 2, D])
        v = st.sb("v", [P, NB, 2, D])
        kT = st.sb("kT", [P, KD, MEM])
        q = st.sb("q", [SAMP, D])
        qx = st.sb("qx", [P, KD, NB, 32])
        qc = st.sb("qc", [P, KD, 4, 32])
        p = st.sb("p", [P, MEM])
        mx = st.sb("mx", [P, 1])
        sums = st.sb("sums", [P, 1])
        pT = st.sb("pT", [P, 2, P])
        o = st.sb("o", [P, D])
        zero = st.sb("zero", [64, D])
        p_k = [st.ps(f"p_k{n}", [P, 1024]) for n in range(2)]
        p_s = st.ps("p_s")
        p_t = st.ps("p_t")
        p_o = st.ps("p_o", [P, 1024])
        q_here = st.sem("q_here")
        q_turned = st.sem("q_turned")
        qx_ready = st.sem("qx_ready")
        cleared = st.sem("cleared")
        zero_out = st.sem("zero_out")
        kv_here = [st.sem(f"kv_here{s}") for s in range(2)]
        qc_ready = st.sem("qc_ready")
        k_turned = st.sem("k_turned")
        k_taken = [st.sem(f"k_taken{n}") for n in range(2)]
        s_done = st.sem("s_done")
        mx_ready = st.sem("mx_ready")
        exp_done = st.sem("exp_done")
        p_turned = st.sem("p_turned")
        p_ready = st.sem("p_ready")
        o_done = st.sem("o_done")
        o_ready = st.sem("o_ready")
        o_out = st.sem("o_out")
        turns = st.sem("turns")
        turns_pe = st.sem("turns_pe")

        with nc.Block() as block:

            @block.sync
            def _(sp):
                sp.dma_start(q[:, :], scr["xq"][SEQ:TOK, :]).then_inc(q_here, 16)
                sp.wait_ge(cleared, 1)
                sp.dma_start(scr["xo"][TOK:TOKP, :], zero[:, :]).then_inc(zero_out, 16)
                for g in range(2):
                    for b in range(4):
                        wait_turn(sp, k_turned, g * 4 + b + 1, turns)
                        kv = io["cache_mem"][4 * g + b].rearrange("(t p) n -> p t n", p=P)
                        sp.dma_start(kn[:, b % 2, :, :], kv[:, :, 0:D]).then_inc(kv_here[b % 2], 16)
                        sp.dma_start(v[:, 4 * g + b, :, :], kv[:, :, D:2 * D]).then_inc(kv_here[b % 2], 16)
                for g in range(2):
                    sp.wait_ge(o_ready, g + 1)
                    for b in range(4):
                        for h in range(XH):
                            r = 32 * b + 8 * h
                            sp.dma_start(scr["xo"][SEQ + 32 * g + 8 * b:SEQ + 32 * g + 8 * b + 8, h * XD:(h + 1) * XD], o[r:r + 8, h * XD:(h + 1) * XD]).then_inc(o_out, 16)
                sp.wait_ge(o_out, 512)
                sp.wait_ge(zero_out, 16)

            @block.tensor
            def _(pe):
                pe.wait_ge(q_here, 16)
                for c in range(KD):
                    m = pe.transpose(p_s[:, c * SAMP:(c + 1) * SAMP], q[:, c * P:(c + 1) * P], ident[0:SAMP, 0:SAMP])
                m.then_inc(q_turned, 1)
                pe.wait_ge(qx_ready, 1)
                for g in range(2):
                    pe.wait_ge(qc_ready, g + 1)
                    for b in range(4):
                        pe.wait_ge(kv_here[b % 2], g * 64 + (b // 2 + 1) * 32)
                        for n in range(2):
                            pe.wait_ge(k_taken[n], g * 4 + b + 1)
                            for c in range(4):
                                for t in range(2):
                                    m = pe.transpose(p_k[n][:, c * MEM + t * P:c * MEM + (t + 1) * P],
                                                     kn[:, b % 2, t, (4 * n + c) * P:(4 * n + c + 1) * P], ident[:, :])
                        m.then_inc(k_turned, 1)
                        for n in range(2):
                            pe.wait_ge(k_taken[n], g * 4 + b + 2)
                        for c in range(KD):
                            m = pe.matmul(p_s[32 * b:32 * b + 32, 0:MEM], qc[:, c, b, :], kT[:, c, :], start=(c == 0), stop=(c == KD - 1))
                        m.then_inc(s_done, 1)
                    wait_turn(pe, exp_done, g + 1, turns_pe)
                    for c in range(2):
                        m = pe.transpose(p_t[:, c * P:(c + 1) * P], p[:, c * P:(c + 1) * P], ident[:, :])
                    m.then_inc(p_turned, 1)
                    pe.wait_ge(p_ready, g + 1)
                    for b in range(4):
                        r = slice(32 * b, 32 * b + 32)
                        for n in range(2):
                            for c in range(2):
                                m = pe.matmul(p_o[r, n * 512:(n + 1) * 512], pT[:, c, r], v[:, 4 * g + b, c, n * 512:(n + 1) * 512], start=(c == 0), stop=(c == 1))
                    m.then_inc(o_done, 1)

            @block.scalar
            def _(act):
                act.wait_ge(qx_ready, 1)
                for g in range(2):
                    act.wait_ge(s_done, g * 4 + 1)
                    act.activation(qc[:, :, :, :], qx[:, :, 4 * g:4 * g + 4, :], ACT.Copy).then_inc(qc_ready, 1)
                    for b in range(4):
                        act.wait_ge(k_turned, g * 4 + b + 3)
                        act.wait_ge(s_done, g * 4 + b + 1)
                        act.activation(kT[:, 0:4, :].rearrange("p a b -> p (a b)"), p_k[0][:, :], ACT.Copy).then_inc(k_taken[0], 1)
                    act.wait_ge(mx_ready, g + 1)
                    act.activation(p[:, :], p_s[:, 0:MEM], ACT.Exp, bias=mx[:, 0:1], accum_out=sums[:, 0:1]).then_inc(exp_done, 1)

            @block.vector
            def _(dve):
                dve.memset(qx[:, :, :, :], 0.0)
                dve.memset(zero[:, :], 0.0)
                dve.drain()
                dve.sem_inc(cleared, 1)
                dve.sem_inc(k_turned, 2)
                dve.sem_inc(o_done, 1)
                dve.sem_inc(s_done, 1)
                dve.sem_inc(k_taken[0], 1)
                dve.sem_inc(k_taken[1], 1)
                dve.wait_ge(q_turned, 1)
                for c in range(KD):
                    h = c // 2
                    dve.tensor_scalar(qx[:, c, :, 8 * h:8 * h + 8], p_s[:, c * SAMP:(c + 1) * SAMP].rearrange("p (b t) -> p b t", t=NT),
                                      XD ** -0.5, None, ALU.mult)
                dve.drain()
                dve.sem_inc(qx_ready, 1)
                for g in range(2):
                    for b in range(4):
                        dve.wait_ge(k_turned, g * 4 + b + 3)
                        dve.wait_ge(s_done, g * 4 + b + 1)
                        dve.tensor_copy(kT[:, 4:8, :].rearrange("p a b -> p (a b)"), p_k[1][:, :]).then_inc(k_taken[1], 1)
                    dve.wait_ge(s_done, g * 4 + 5)
                    dve.tensor_reduce(mx[:, :], p_s[:, 0:MEM], AX, ALU.max)
                    dve.drain()
                    dve.tensor_scalar(mx[:, :], mx[:, :], -1.0, None, ALU.mult).then_inc(mx_ready, 1)
                    dve.wait_ge(p_turned, g + 1)
                    dve.tensor_copy(pT[:, :, :].rearrange("p a b -> p (a b)"), p_t[:, 0:2 * P]).then_inc(p_ready, 1)
                    dve.reciprocal(sums[:, :], sums[:, :])
                    dve.drain()
                    dve.wait_ge(o_done, g + 2)
                    if g:
                        dve.wait_ge(o_out, 256)
                    dve.tensor_scalar(o[:, :], p_o[:, :], sums[:, 0:1], None, ALU.mult).then_inc(o_ready, 1)


def stage_mlp(nc, io, scr, hnT):
    with ExitStack() as ctx:
        gT = ctx.enter_context(nc.sbuf_tensor("mlp_gT", [P, FT, TOK], F32))
        stage_mlp_up(nc, io, hnT, gT)
        stage_mlp_down(nc, io, scr, gT)


def stage_mlp_up(nc, io, hnT, gT):
    with Stage(nc, "up") as st:
        w = st.sb("w", [P, 2, 2, KD, P])
        taps = st.sb("taps", [P, 2 * FT, 4])
        buf = st.sb("buf", [P, 2 * FT, NB, 2])
        kept = st.sb("kept", [P, 2 * FT, 18])
        tap = st.sb("tap", [P, 2, 4])
        xp = [st.sb(f"xp{n}", [P, SEQ + 2]) for n in range(2)]
        xs = [st.sb(f"xs{n}", [P, NB, NT + 2]) for n in range(2)]
        y = [st.sb(f"y{n}", [P, TOK]) for n in range(2)]
        acc = [st.ps(f"acc{n}", [P, 3, 512]) for n in range(2)]
        w_here = [st.sem(f"w_here{s}") for s in range(2)]
        small_here = st.sem("small_here")
        projected = [st.sem(f"projected{n}") for n in range(2)]
        x_ready = [st.sem(f"x_ready{n}") for n in range(2)]
        x_used = [st.sem(f"x_used{n}") for n in range(2)]
        gate_ready = st.sem("gate_ready")
        y_used = st.sem("y_used")
        kept_out = st.sem("kept_out")
        turns = st.sem("turns")
        turns_pool = st.sem("turns_pool")

        with nc.Block() as block:

            @block.sync
            def _(sp):
                w_v = io["w_up"].rearrange("(k p) (a f n) -> f p a k n", p=P, a=2, n=P)

                def load(f, s):
                    for n in range(2):
                        sp.dma_start(w[:, s, n, :, :], w_v[ds(f, 1), :, n, :, :].rearrange("f p k n -> p (f k) n")).then_inc(w_here[s], 16)

                load(0, 0)
                load(1, 1)
                sp.dma_start(taps[:, :, :], io["fconv_wT"].rearrange("(c p) k -> p c k", p=P)).then_inc(small_here, 16)
                sp.dma_start(buf[:, :, :, :].rearrange("p c b k -> p c (b k)"), io["fconv_bufT"].rearrange("(c p) k -> p c k", p=P)).then_inc(small_here, 16)
                with sp.Fori(0, FT // 2 - 1) as i:
                    for s in range(2):
                        wait_turn(sp, projected[1], 2 * i + s + 1, turns)
                        load(2 * i + s + 2, s)
                sp.wait_ge(y_used, FT + 1)
                sp.dma_start(io["fconvT"].rearrange("(c p) k -> p c k", p=P), kept[:, :, :]).then_inc(kept_out, 16)
                sp.wait_ge(kept_out, 16)

            @block.tensor
            def _(pe):
                with pe.Fori(0, FT // 2) as i:
                    for s in range(2):
                        f = 2 * i + s
                        pe.wait_ge(w_here[s], 32 * (i + 1))
                        for n in range(2):
                            pe.wait_ge(x_ready[n], f + 1)
                            for g, (a, b) in enumerate(SPLIT):
                                for k in range(KD):
                                    m = pe.matmul(acc[n][:, g, 0:b - a], w[:, s, n, k, :], hnT[:, k, a:b], start=(k == 0), stop=(k == KD - 1))
                            m.then_inc(projected[n], 1)

            @block.scalar
            def _(act):
                with act.Fori(0, FT) as f:
                    for n in range(2):
                        act.wait_ge(projected[n], f + 1)
                        act.wait_ge(x_used[n], f + 1)
                        act.activation(xp[n][:, 2:2 + 2 * PART].rearrange("p (a b) -> p a b", a=2), acc[n][:, 0:2, 0:PART], ACT.Copy)
                        act.activation(xp[n][:, 2 + 2 * PART:], acc[n][:, 2, 0:SEQ - 2 * PART], ACT.Copy)
                        act.activation(xs[n][:, :, 2:], acc[n][:, 2, SEQ - 2 * PART:LAST].rearrange("p (b t) -> p b t", t=NT), ACT.Copy).then_inc(x_ready[n], 1)
                    act.wait_ge(x_used[1], f + 2)
                    act.activation(y[0][:, :], y[0][:, :], ACT.Silu).then_inc(gate_ready, 1)

            @block.gpsimd
            def _(pool):
                with pool.Fori(0, FT) as f:
                    wait_turn(pool, gate_ready, f + 1, turns_pool)
                    pool.tensor_tensor(gT[:, ds(f, 1), :].rearrange("p a n -> p (a n)"), y[0][:, :], y[1][:, :], ALU.mult).then_inc(y_used, 1)

            @block.vector
            def _(dve):
                for n in range(2):
                    dve.memset(xp[n][:, 0:2], 0.0)
                dve.drain()
                for s in x_ready + x_used + [y_used]:
                    dve.sem_inc(s, 1)
                dve.wait_ge(small_here, 32)
                with dve.Fori(0, FT) as f:
                    for n in range(2):
                        c = f + n * FT
                        dve.tensor_copy(tap[:, n, :], taps[:, ds(c, 1), :].rearrange("p a k -> p (a k)"))
                        dve.tensor_copy(xs[n][:, :, 0:2], buf[:, ds(c, 1), :, :].rearrange("p a b k -> p (a b) k"))
                        dve.drain()
                        dve.wait_ge(x_ready[n], f + 2)
                        if n == 0:
                            dve.wait_ge(y_used, f + 1)
                        yp, ys = y[n][:, 0:SEQ], y[n][:, SEQ:].rearrange("p (b t) -> p b t", t=NT)
                        dve.tensor_scalar(yp, xp[n][:, 0:SEQ], tap[:, n, 0:1], tap[:, n, 3:4], ALU.mult, ALU.add)
                        dve.tensor_scalar(ys, xs[n][:, :, 0:NT], tap[:, n, 0:1], tap[:, n, 3:4], ALU.mult, ALU.add)
                        for k in (1, 2):
                            dve.drain()
                            dve.scalar_tensor_tensor(yp, xp[n][:, k:SEQ + k], tap[:, n, k:k + 1], yp, ALU.mult, ALU.add)
                            dve.scalar_tensor_tensor(ys, xs[n][:, :, k:NT + k], tap[:, n, k:k + 1], ys, ALU.mult, ALU.add)
                        kc = kept[:, ds(c, 1), :].rearrange("p a k -> p (a k)")
                        dve.tensor_copy(kc[:, 0:2], xp[n][:, SEQ:SEQ + 2])
                        dve.tensor_copy(kc[:, 2:18].rearrange("p (b k) -> p b k", k=2), xs[n][:, :, NT:NT + 2])
                        dve.drain()
                        dve.sem_inc(x_used[n], 1)


def stage_mlp_down(nc, io, scr, gT):
    with Stage(nc, "down") as st:
        w = st.sb("w", [P, 2, FT, P])
        res = st.sb("res", [P, 2, TOK])
        yo = st.sb("yo", [P, 2, TOK])
        acc = [st.ps(f"acc{s}", [P, 3, 512]) for s in range(2)]
        w_here = [st.sem(f"w_here{s}") for s in range(2)]
        summed = st.sem("summed")
        y_ready = st.sem("y_ready")
        bank_read = st.sem("bank_read")
        y_out = [st.sem(f"y_out{s}") for s in range(2)]
        turns = st.sem("turns")
        ND = D // P

        with nc.Block() as block:

            @block.sync
            def _(sp):
                w_v = io["w_down"].rearrange("(f p) (c n) -> c p f n", p=P, n=P)
                h_v = scr["h2T"].rearrange("(c p) n -> c p n", p=P)

                def load(c, s):
                    sp.dma_start(w[:, s, :, :], w_v[ds(c, 1), :, :, :].rearrange("c p f n -> p (c f) n")).then_inc(w_here[s], 16)
                    sp.dma_start(res[:, s, :], h_v[ds(c, 1), :, 0:TOK].rearrange("c p n -> p (c n)")).then_inc(w_here[s], 16)

                def store(c, s):
                    sp.dma_start(io["yT"].rearrange("(c p) n -> c p n", p=P)[ds(c, 1), :, 0:TOK].rearrange("c p n -> p (c n)"), yo[:, s, :]).then_inc(y_out[s], 16)

                load(0, 0)
                load(1, 1)
                with sp.Fori(0, ND // 2 - 1) as i:
                    for s in range(2):
                        wait_turn(sp, y_ready, 2 * i + s + 1, turns)
                        load(2 * i + s + 2, s)
                        store(2 * i + s, s)
                for s in range(2):
                    sp.wait_ge(y_ready, ND - 1 + s)
                    store(ND - 2 + s, s)
                for s in range(2):
                    sp.wait_ge(y_out[s], 16 * (ND // 2 + 1))

            @block.tensor
            def _(pe):
                with pe.Fori(0, ND // 2) as i:
                    for s in range(2):
                        pe.wait_ge(w_here[s], 32 * (i + 1))
                        pe.wait_ge(bank_read, 2 * i + s + 1)
                        for g, (a, b) in enumerate(SPLIT):
                            for f in range(FT):
                                m = pe.matmul(acc[s][:, g, 0:b - a], w[:, s, f, :], gT[:, f, a:b], start=(f == 0), stop=(f == FT - 1))
                        m.then_inc(summed, 1)

            @block.vector
            def _(dve):
                dve.sem_inc(bank_read, 2)
                for s in range(2):
                    dve.sem_inc(y_out[s], 16)
                with dve.Fori(0, ND // 2) as i:
                    for s in range(2):
                        dve.wait_ge(w_here[s], 32 * (i + 1))
                        dve.wait_ge(y_out[s], 16 * (i + 1))
                        dve.wait_ge(summed, 2 * i + s + 1)
                        two = lambda t: t[:, s, 0:2 * PART].rearrange("p (a b) -> p a b", a=2)
                        dve.tensor_tensor(two(yo), acc[s][:, 0:2, 0:PART], two(res), ALU.add)
                        dve.tensor_tensor(yo[:, s, 2 * PART:], acc[s][:, 2, 0:LAST], res[:, s, 2 * PART:], ALU.add)
                        dve.drain()
                        dve.sem_inc(y_ready, 1)
                        dve.sem_inc(bank_read, 1)


def program(nc, io, scr):
    with ExitStack() as ctx:
        ident = ctx.enter_context(nc.sbuf_tensor("ident", [P, P], F32))
        half = ctx.enter_context(nc.sbuf_tensor("half", [P, 32], F32))
        load_sem = nc.alloc_semaphore("ident_here")
        with nc.Block() as block:
            @block.sync
            def _(sp):
                sp.dma_start(ident[:, :], io["ident"][:, :]).then_inc(load_sem, 16)
                sp.wait_ge(load_sem, 16)

            @block.vector
            def _(dve):
                dve.memset(half[:, :], -0.5)
        with ExitStack() as front:
            xnT = front.enter_context(nc.sbuf_tensor("xnT", [P, KD, TOKP], F32))
            stage_project(nc, io, scr, xnT, ident, half)
            stage_channels_and_delta(nc, io, scr, xnT, ident, half)
        stage_nsa(nc, io, scr, ident, half)
        with ExitStack() as mix:
            w_out = mix.enter_context(nc.sbuf_tensor("w_out", [P, KD, D], F32))
            w_xq = mix.enter_context(nc.sbuf_tensor("w_xq", [P, KD, D], F32))
            stage_mem(nc, io, scr, ident, half, w_out, w_xq)
            stage_rows(nc, io, scr, ident, half, True, w_out, w_xq)
        with nc.sbuf_tensor("hnT", [P, KD, TOKP], F32) as hnT:
            with nc.sbuf_tensor("w_xo", [P, KD, D], F32) as w_xo:
                stage_cross_prompt(nc, io, scr, ident, w_xo)
                stage_cross_sample(nc, io, scr, ident)
                stage_rows(nc, io, scr, ident, half, False, w_xo, hnT=hnT)
            stage_mlp(nc, io, scr, hnT)


OUTS = {
    "yT": (D, TOKP), "rows": (TOKP, 512), "wrows": (TOKP, 256), "gstate_p": (4, P, P), "gstate_s": (NB, 4, P, P),
    "gconvT": (3 * GW, 27), "fconvT": (2 * FF, 18), "mem_kv": (MEM, 2048), "win_s": (NB, WIN, 256),
}
SCRATCH = {
    "qc": (TOKP, 512), "qr": (TOKP, 512), "z": (TOKP, 512), "misc": (TOKP, 32), "mix": (TOKP, 1024),
    "xq": (TOKP, 1024), "h1": (TOKP, 1024), "xo": (TOKP, 1024), "h2T": (D, TOKP),
}


def kernel(**inputs):
    import numpy as np
    import concourse.bacc as bacc
    from concourse.bass_utils import run_bass_kernel_spmd

    f32 = np.float32
    g = {k: np.asarray(v) for k, v in inputs.items()}
    a = {}
    a["x_all"] = np.concatenate([g["x_prompt"].reshape(SEQ, D), g["x_sample"].reshape(SAMP, D),
                                 np.zeros((TOKP - TOK, D), f32)])
    a["mem"] = g["mem_prompt"].reshape(MEM, D)
    a["cache_kv"] = g["cache_nsa_kv"].reshape(POOL, PAGE, 512)
    a["cache_win"] = g["cache_nsa_win"].reshape(NB, WIN, 256)
    a["state_gdn"] = g["state_gdn"].reshape(NB, 4, P, P)
    a["gconv_bufT"] = g["cache_gdn_conv"].reshape(NB * 3, 3 * GW).T
    a["fconv_bufT"] = g["cache_ffn_conv"].reshape(NB * 2, 2 * FF).T
    a["cache_mem"] = g["cache_mem_kv"].reshape(NB, MEM, 2048)
    a["pages"] = g["page_table"].reshape(1, NB * NPAGE)
    for n in ["attn_norm_w", "w_in", "nsa_q_norm_w", "nsa_k_norm_w", "cmp_w", "gdn_a_log", "gdn_dt_bias",
              "gdn_norm_w", "w_out", "mem_norm_w", "w_xk", "w_xv", "xk_norm_w", "xattn_norm_w", "w_xq", "xq_norm_w",
              "w_xo", "ffn_norm_w", "w_up", "w_down"]:
        a[n] = g[n][0]
    a["cmp_peT"] = g["cmp_pe"][0].transpose(2, 0, 1)
    a["gconv_wT"] = g["gdn_conv_w"][0].T
    a["fconv_wT"] = np.concatenate([g["ffn_conv_w"][0], g["ffn_conv_b"]]).T
    a.update(shape_constants())
    arrays = {k: np.ascontiguousarray(v) for k, v in a.items()}

    nc = bacc.Bacc("TRN2", target_bir_lowering=False, num_devices=1)
    io = {k: nc.dram_tensor(f"in_{k}", v.shape, mybir.dt.from_np(v.dtype), kind="ExternalInput").ap()
          for k, v in arrays.items()}
    for k, shape in OUTS.items():
        io[k] = nc.dram_tensor(f"out_{k}", shape, F32, kind="ExternalOutput").ap()
    scr = {k: nc.dram_tensor(f"scr_{k}", shape, F32, kind="Internal").ap() for k, shape in SCRATCH.items()}
    program(nc, io, scr)
    r = run_bass_kernel_spmd(nc, [{f"in_{k}": v for k, v in arrays.items()}], core_ids=[0]).results[0]
    o = {k: r[f"out_{k}"] for k in OUTS}
    y = o["yT"].T
    fconv = o["fconvT"].T
    gconv = o["gconvT"].T
    c = np.ascontiguousarray
    return (
        c(y[:SEQ]).reshape(1, SEQ, D), c(y[SEQ:TOK]).reshape(NB, NT, D),
        c(o["rows"][:SEQ]).reshape(1, 1, SEQ, 4, 2, HD), c(o["wrows"][SEQ - WIN:SEQ]).reshape(1, 1, WIN, 2, 2, HD),
        c(o["gstate_p"]).reshape(1, 1, 4, P, P), c(gconv[:3]).reshape(1, 1, 3, 3 * GW),
        c(fconv[:2]).reshape(1, 1, 2, 2 * FF), c(o["mem_kv"]).reshape(1, 1, MEM, 2, XH, XD),
        c(o["rows"][SEQ:TOK]).reshape(1, NB, NT, 4, 2, HD), c(o["win_s"]).reshape(1, NB, WIN, 2, 2, HD),
        c(o["gstate_s"]).reshape(1, NB, 4, P, P), c(gconv[3:]).reshape(1, NB, 3, 3 * GW),
        c(fconv[2:]).reshape(1, NB, 2, 2 * FF),
    )


def shape_constants():
    import numpy as np

    f32 = np.float32
    out = {"ident": np.eye(P, dtype=f32)}
    pos = np.concatenate([np.arange(SEQ), np.tile(PAST + np.arange(NT), NB), np.zeros(TOKP - TOK)]).astype(f32)
    half = HD // 2
    inv = np.power(10000.0, -np.arange(half) / half).astype(f32)
    ang = (pos[:, None] * inv[None, :]).astype(f32)
    cos, sin = np.cos(ang), np.sin(ang)
    out["rope"] = np.stack([np.concatenate([cos, cos], 1), np.concatenate([-sin, sin], 1)], 1).astype(f32)
    r, c = np.arange(P)[:, None], np.arange(P)[None, :]
    for name, block in (("p", 64), ("s", NT)):
        same = (r // block) == (c // block)
        levels = [(same & (r // s % 2 == 0) & (c // (2 * s) == r // (2 * s)) & (c // s % 2 == 1)).astype(f32)
                  for s in (1, 2, 4, 8, 16, 32)]
        out["gm_" + name] = np.stack([(same & (r <= c)).astype(f32), same.astype(f32)] + levels, 1)
    out["bsel"] = (np.arange(SAMP)[:, None] // NT == np.arange(NB)[None, :]).astype(f32)
    q, n = np.arange(SEQ)[:, None], np.arange(64)[None, :]
    out["cmp_ok"] = ((16 * n + 31 <= q) & (n < 63)).astype(f32)
    blk = np.arange(16)[None, :]
    forced = (blk == 0) | (blk == q // 64) | (blk == q // 64 - 1)
    out["blk_bonus"] = np.where(blk <= q // 64, np.where(forced, 1e4, 0.0), NEG).astype(f32)
    out["key_no"] = np.broadcast_to(np.arange(SEQ, dtype=f32), (P, SEQ))
    out["q_no"] = np.arange(SEQ, dtype=f32).reshape(8, P).T
    rr, cc, b = np.arange(P)[None, :, None], np.arange(640)[None, None, :], np.arange(8)[:, None, None]
    out["win_bias"] = np.where((cc <= rr + 512) & (cc > rr) & (cc >= 512 - 128 * b), 0.0, NEG).astype(f32)
    t = np.arange(P)[:, None] % NT
    out["samp_bonus"] = np.broadcast_to(np.where(np.isin(np.arange(65), (0, 63, 64)), 1e4, 0.0), (P, 65)).astype(f32)
    out["samp_new"] = np.where(np.arange(NT)[None, :] <= t, 0.0, NEG).astype(f32)
    cw = np.arange(WIN + NT)[None, :]
    out["samp_win"] = np.where((cw > t) & (cw <= t + WIN), 0.0, NEG).astype(f32)
    rb, rg, rt = np.arange(P) // 32, np.arange(P) // 8 % 4, np.arange(P) % 8
    out["gsum"] = ((rb[:, None] == rb[None, :]) & (rt[:, None] == rt[None, :])).astype(f32)
    out["cmp_last"] = np.broadcast_to((np.arange(256) < 255).astype(f32), (P, 256))
    return out
```
